# Optimizing a Trainium2 kernel written in Bass

```python
import jax, jax.numpy as jnp
from jax import lax
import numpy as np

D_MODEL = 1024
BATCH = 1
SEQ = 2048
DEPTH = 1
DEC_BATCH = 8
DEC_SEQ = 8
PAST_LEN = 4096
PAGE_SIZE = 128

D_CONV = D_MODEL // 2
CONV_WIDTH = 3
N_HEADS = 8
HEAD_DIM = 64
N_KV_HEADS = 2
GROUP = N_HEADS // N_KV_HEADS
D_ATT = N_HEADS * HEAD_DIM
D_KV = N_KV_HEADS * HEAD_DIM
N_IDX_HEADS = 8
IDX_DIM = 64
TOPK_MAX = 256
Q_BLOCK = 128
EPS = 1e-6
NEG = -1e30
IN_SIZES = (D_CONV, D_CONV, D_CONV, D_CONV, D_ATT, D_KV, D_KV, D_ATT,
            N_IDX_HEADS * IDX_DIM, IDX_DIM, N_IDX_HEADS, D_MODEL, D_MODEL)
D_IN = sum(IN_SIZES)

kernel_name = "hybrid_conv_dsa_gated_decode_step"

def rmsnorm(x, g):
    xf = x.astype(jnp.float32)
    y = xf * lax.rsqrt(jnp.mean(xf * xf, axis=-1, keepdims=True) + EPS)
    return (y * g.astype(jnp.float32)).astype(x.dtype)

def split_cols(h):
    idx, acc = [], 0
    for s in IN_SIZES[:-1]:
        acc += s
        idx.append(acc)
    return jnp.split(h, idx, axis=-1)

def alibi_slopes():
    h = jnp.arange(N_HEADS, dtype=jnp.float32) + 1.0
    return jnp.exp2(-8.0 * h / N_HEADS).reshape(N_KV_HEADS, GROUP)

def short_conv(u, prev, conv_w):
    T = u.shape[1]
    up = jnp.concatenate([prev.astype(u.dtype), u], axis=1)
    y = conv_w[0] * up[:, 0:T]
    for j in range(1, CONV_WIDTH):
        y = y + conv_w[j] * up[:, j:j + T]
    return y, up[:, T:]

def indexer_select(qi, wi, kidx, q_pos, k_sel):
    L = kidx.shape[1]
    s = jnp.einsum('bqhd,bsd->bqhs', qi, kidx)
    s = jnp.einsum('bqhs,bqh->bqs', jax.nn.relu(s), wi).astype(jnp.float32)
    k_pos = jnp.arange(L)
    s = jnp.where(k_pos[None, None, :] <= q_pos[None, :, None], s, -jnp.inf)
    _, sel = lax.top_k(s, k_sel)
    return sel

def sparse_attend(q, kg, vg, sel, q_pos):
    B, Tq = q.shape[0], q.shape[1]
    s = jnp.einsum('bqhgd,bqkhd->bqhgk', q, kg).astype(jnp.float32) * (HEAD_DIM ** -0.5)
    dist = (q_pos[None, :, None] - sel).astype(jnp.float32)
    s = s - alibi_slopes()[None, None, :, :, None] * dist[:, :, None, None, :]
    valid = (sel <= q_pos[None, :, None])[:, :, None, None, :]
    p = jax.nn.softmax(jnp.where(valid, s, NEG), axis=-1).astype(vg.dtype)
    o = jnp.einsum('bqhgk,bqkhd->bqhgd', p, vg)
    return o.reshape(B, Tq, D_ATT)

def gather_rows(a, ix):
    return jax.vmap(lambda aa, ii: aa[ii])(a, ix)

def prompt_attention(q, k, v, qi, wi, kidx):
    B, S = q.shape[0], q.shape[1]
    k_sel = min(TOPK_MAX, S // 4)
    qb = min(Q_BLOCK, S)
    nb = S // qb

    def block(i):
        start = i * qb
        q_b = lax.dynamic_slice_in_dim(q, start, qb, axis=1)
        qi_b = lax.dynamic_slice_in_dim(qi, start, qb, axis=1)
        wi_b = lax.dynamic_slice_in_dim(wi, start, qb, axis=1)
        q_pos = start + jnp.arange(qb)
        sel = indexer_select(qi_b, wi_b, kidx, q_pos, k_sel)
        return sparse_attend(q_b, gather_rows(k, sel), gather_rows(v, sel), sel, q_pos)

    out = lax.map(block, jnp.arange(nb))
    return out.transpose(1, 0, 2, 3).reshape(B, S, D_ATT)

def sample_attention(q, k_new, v_new, qi, wi, kidx_new, cache_k, cache_v, cache_kidx, page_table):
    DB, T = q.shape[0], q.shape[1]
    past = page_table.shape[1] * PAGE_SIZE
    L = past + T
    kidx_past = cache_kidx[page_table].reshape(DB, past, IDX_DIM)
    kidx_all = jnp.concatenate([kidx_past.astype(kidx_new.dtype), kidx_new], axis=1)
    q_pos = past + jnp.arange(T)
    sel = indexer_select(qi, wi, kidx_all, q_pos, min(TOPK_MAX, L // 4))
    in_past = (sel < past)[..., None, None]
    ps = jnp.minimum(sel, past - 1)
    phys = jax.vmap(lambda pt, ii: pt[ii])(page_table, ps // PAGE_SIZE)
    off = ps % PAGE_SIZE
    ns = jnp.clip(sel - past, 0, T - 1)
    kg = jnp.where(in_past, cache_k[phys, off].astype(k_new.dtype), gather_rows(k_new, ns))
    vg = jnp.where(in_past, cache_v[phys, off].astype(v_new.dtype), gather_rows(v_new, ns))
    return sparse_attend(q, kg, vg, sel, q_pos)

def layer(x, norm_gain, w_in, conv_w, w_up_conv, w_up_attn, w_out, conv_prev, attend):
    B, T = x.shape[0], x.shape[1]
    xn = rmsnorm(x, norm_gain)
    h = jnp.einsum('btd,dn->btn', xn, w_in)
    cb, cc, cu, cz, q, k, v, az, iq, ik, iw, gc, ga = split_cols(h)
    conv_y, conv_state = short_conv(cc * cu, conv_prev, conv_w)
    y_conv = cb * conv_y * jax.nn.silu(cz)
    q = q.reshape(B, T, N_KV_HEADS, GROUP, HEAD_DIM)
    k = k.reshape(B, T, N_KV_HEADS, HEAD_DIM)
    v = v.reshape(B, T, N_KV_HEADS, HEAD_DIM)
    iq = iq.reshape(B, T, N_IDX_HEADS, IDX_DIM) * (IDX_DIM ** -0.5)
    iw = iw * (N_IDX_HEADS ** -0.5)
    y_attn = attend(q, k, v, iq, iw, ik) * jax.nn.silu(az)
    m = (jax.nn.sigmoid(gc) * jnp.einsum('btc,cd->btd', y_conv, w_up_conv)
         + jax.nn.sigmoid(ga) * jnp.einsum('bta,ad->btd', y_attn, w_up_attn))
    x = x + jnp.einsum('btd,de->bte', m, w_out)
    return x, k, v, ik, conv_state

def setup_inputs(seed: int = 0) -> dict:
    key = jax.random.key(seed)
    ks = jax.random.split(key, 16)
    n_pages = PAST_LEN // PAGE_SIZE
    used = DEC_BATCH * n_pages
    n_phys = used + max(1, used // 4)
    f = jnp.float32
    x_prompt = jax.random.normal(ks[0], (BATCH, SEQ, D_MODEL), f)
    x_sample = jax.random.normal(ks[1], (DEC_BATCH, DEC_SEQ, D_MODEL), f)
    cache_k = jax.random.normal(ks[2], (DEPTH, n_phys, PAGE_SIZE, N_KV_HEADS, HEAD_DIM), f)
    cache_v = jax.random.normal(ks[3], (DEPTH, n_phys, PAGE_SIZE, N_KV_HEADS, HEAD_DIM), f)
    cache_kidx = jax.random.normal(ks[4], (DEPTH, n_phys, PAGE_SIZE, IDX_DIM), f)
    state_conv = jax.random.normal(ks[5], (DEPTH, DEC_BATCH, CONV_WIDTH - 1, D_CONV), f)
    page_table = jax.random.permutation(ks[6], n_phys)[:used].reshape(DEC_BATCH, n_pages).astype(jnp.int32)
    norm_gain = 1.0 + 0.1 * jax.random.normal(ks[7], (DEPTH, D_MODEL), f)
    w_in = jax.random.normal(ks[8], (DEPTH, D_MODEL, D_IN), f) * D_MODEL ** -0.5
    conv_w = jax.random.normal(ks[9], (DEPTH, CONV_WIDTH, D_CONV), f) * CONV_WIDTH ** -0.5
    w_up_conv = jax.random.normal(ks[10], (DEPTH, D_CONV, D_MODEL), f) * D_CONV ** -0.5
    w_up_attn = jax.random.normal(ks[11], (DEPTH, D_ATT, D_MODEL), f) * D_ATT ** -0.5
    w_out = jax.random.normal(ks[12], (DEPTH, D_MODEL, D_MODEL), f) * D_MODEL ** -0.5
    final_gain = 1.0 + 0.1 * jax.random.normal(ks[13], (D_MODEL,), f)
    return {"x_prompt": x_prompt, "x_sample": x_sample, "cache_k": cache_k, "cache_v": cache_v,
            "cache_kidx": cache_kidx, "state_conv": state_conv, "page_table": page_table,
            "norm_gain": norm_gain, "w_in": w_in, "conv_w": conv_w, "w_up_conv": w_up_conv,
            "w_up_attn": w_up_attn, "w_out": w_out, "final_gain": final_gain}

def reference(x_prompt, x_sample, cache_k, cache_v, cache_kidx, state_conv, page_table,
              norm_gain, w_in, conv_w, w_up_conv, w_up_attn, w_out, final_gain):
    xp, xs = x_prompt, x_sample
    kp_l, vp_l, ip_l, cp_l, ks_l, vs_l, is_l, cs_l = [], [], [], [], [], [], [], []
    for l in range(DEPTH):
        prev_p = jnp.zeros((xp.shape[0], CONV_WIDTH - 1, D_CONV), xp.dtype)
        xp, kp, vp, ip, cp = layer(xp, norm_gain[l], w_in[l], conv_w[l], w_up_conv[l], w_up_attn[l],
                                   w_out[l], prev_p, prompt_attention)
        ck, cv, ci = cache_k[l], cache_v[l], cache_kidx[l]
        attend_s = lambda q, k, v, qi, wi, ki, ck=ck, cv=cv, ci=ci: sample_attention(
            q, k, v, qi, wi, ki, ck, cv, ci, page_table)
        xs, ks_, vs_, is_, cs = layer(xs, norm_gain[l], w_in[l], conv_w[l], w_up_conv[l], w_up_attn[l],
                                      w_out[l], state_conv[l], attend_s)
        kp_l.append(kp); vp_l.append(vp); ip_l.append(ip); cp_l.append(cp)
        ks_l.append(ks_); vs_l.append(vs_); is_l.append(is_); cs_l.append(cs)
    y_prompt = rmsnorm(xp, final_gain)
    y_sample = rmsnorm(xs, final_gain)
    return (y_prompt, y_sample,
            jnp.stack(kp_l), jnp.stack(vp_l), jnp.stack(ip_l), jnp.stack(cp_l),
            jnp.stack(ks_l), jnp.stack(vs_l), jnp.stack(is_l), jnp.stack(cs_l))


_drawn_inputs = setup_inputs


def setup_inputs(seed=0):
    import zlib

    import numpy as np

    out = dict(_drawn_inputs(seed))
    spreads = {}
    factors = {}
    for name, (base, spread) in spreads.items():
        noise = np.random.default_rng([zlib.crc32(name.encode()), seed]).standard_normal(out[name].shape)
        drawn = base * np.exp(spread * noise) if base else spread * noise
        out[name] = __import__('jax').numpy.asarray(drawn.astype(out[name].dtype))
    for name, factor in factors.items():
        out[name] = (out[name] * factor).astype(out[name].dtype)
    return out
```

```python
from contextlib import ExitStack, contextmanager

import concourse.bass as bass
from concourse import mybir

F32 = mybir.dt.float32
I32 = mybir.dt.int32
ALU = mybir.AluOpType
ACT = mybir.ActivationFunctionType
AX_X = mybir.AxisListType.X

D = 1024
S = 2048
DB, DT = 8, 8
ST = DB * DT
DC = 512
NH, HD, NKV = 8, 64, 2
G = NH // NKV
NI, ID = 8, 64
PAGE, NPAGE = 128, 32
PAST = PAGE * NPAGE
TOPK = 256
EPS = 1e-6
P = 128
KC = D // P
NT = S // P
BAND = 512
NBAND = S // BAND
TPB = BAND // P
BIG = 1.0e33
MASKED = -1.0e30
TAKEN = -3.0e38
SLOPES = [2.0 ** (-8.0 * (h + 1) / NH) for h in range(NH)]
ISCALE = float(NI) ** -0.5
QSCALE = float(HD) ** -0.5

O_B, O_C, O_U, O_Z, O_Q, O_K, O_V, O_AZ, O_IQ, O_IK, O_IW, O_GC, O_GA = (
    0, 512, 1024, 1536, 2048, 2560, 2688, 2816, 3328, 3840, 3904, 3912, 4936)
KVW = 2 * NKV * HD
IKW = ID + NI


class Named:
    pass


class Chain:

    def __init__(self, eng, sem):
        self.eng, self.sem, self.n = eng, sem, 0

    def done(self, ins):
        ins.then_inc(self.sem, 1)
        self.n += 1
        self.eng.wait_ge(self.sem, self.n)


class Stage:

    def __init__(self, nc, ctx, name):
        self.nc, self.ctx, self.name, self.sems = nc, ctx, name, []

    def sb(self, name, shape, dt=F32):
        return self.ctx.enter_context(self.nc.sbuf_tensor(f"{self.name}_{name}", shape, dt))

    def psum(self, name, shape):
        return self.ctx.enter_context(self.nc.psum_tensor(f"{self.name}_{name}", shape, F32))

    def sem(self, name):
        self.sems.append(self.ctx.enter_context(self.nc.semaphore(f"{self.name}_{name}")))
        return self.sems[-1]

    @contextmanager
    def round(self):
        with self.nc.Block() as block:
            yield block
        for s in self.sems:
            self.nc.gpsimd.sem_clear(s)
        self.nc.all_engine_barrier()


def refined_rstd(nc, v, ms, tmp, rstd, std):
    v.done(nc.vector.reciprocal(rstd, std))
    v.done(nc.vector.tensor_tensor(tmp, rstd, rstd, ALU.mult))
    v.done(nc.vector.tensor_tensor(tmp, tmp, ms, ALU.mult))
    v.done(nc.vector.tensor_scalar(tmp, tmp, -0.5, 1.5, ALU.mult, ALU.add))
    v.done(nc.vector.tensor_tensor(rstd, rstd, tmp, ALU.mult))


def stage_constants(nc, c):
    with ExitStack() as ctx:
        m = Stage(nc, ctx, "const")
        iotas, cleared, made = m.sem("iotas"), m.sem("cleared"), m.sem("made")
        keys, tiles = m.sb("keys", [P, S], I32), m.sb("tiles", [P, NT], I32)
        with m.round() as block:

            @block.gpsimd
            def _(pool):
                nc.gpsimd.memset(c.ident[:], 0.0).then_inc(cleared, 1)
                nc.gpsimd.iota(keys[:], [[1, S]], base=0, channel_multiplier=-1).then_inc(iotas, 1)
                nc.gpsimd.iota(tiles[:], [[P, NT]], base=0, channel_multiplier=0).then_inc(iotas, 1)
                pool.wait_ge(cleared, 1)
                nc.gpsimd.affine_select(out=c.ident[:], in_=c.ident[:], compare_op=ALU.not_equal, fill=1.0,
                                        base=0, pattern=[[-1, P]], channel_multiplier=1).then_inc(made, 1)

            @block.vector
            def _(dve):
                dve.wait_ge(iotas, 2)
                nc.vector.tensor_copy(c.keypos[:], keys[:]).then_inc(made, 1)
                nc.vector.tensor_copy(c.tilepos[:], tiles[:]).then_inc(made, 1)


def stage_norm(nc, c, a):
    with ExitStack() as ctx:
        m = Stage(nc, ctx, "norm")
        gain = m.sb("gain", [P, D])
        wkv = m.sb("wkv", [P, KC, KVW])
        wik = m.sb("wik", [P, KC, IKW])
        x_in = m.sb("x_in", [P, 2, D])
        xn = m.sb("xn", [P, 2, D])
        junk = m.sb("junk", [P, D])
        xt = m.sb("xt", [P, 2, KC, P])
        kv = m.sb("kv", [P, 2, KVW])
        ik = m.sb("ik", [P, 2, 2, ID])
        st = m.sb("st", [P, 2, 8])
        ps_t = m.psum("ps_t", [P, KC, P])
        ps_kv = m.psum("ps_kv", [P, 512])
        ps_kt = m.psum("ps_kt", [P, 4, P])
        (weights, squared, meaned, rooted, normed, turned, staged, kept, projected, evacuated,
         k_turned, k_kept, own) = [m.sem(n) for n in (
            "weights", "squared", "meaned", "rooted", "normed", "turned", "staged", "kept",
            "projected", "evacuated", "k_turned", "k_kept", "own")]
        own_act = m.sem("own_act")
        x_ready = [m.sem(f"x_ready{s}") for s in range(2)]
        stored = [m.sem(f"stored{s}") for s in range(2)]
        x_tiles = a["x_prompt"].rearrange("b (t p) d -> (b t) p d", p=P)
        win = a["w_in"].rearrange("l (k p) n -> (l p) k n", p=P)
        k_out = a["new_k_prompt"].rearrange("l b (t p) h d -> (l b t) p (h d)", p=P)
        v_out = a["new_v_prompt"].rearrange("l b (t p) h d -> (l b t) p (h d)", p=P)
        i_out = a["new_kidx_prompt"].rearrange("l b (t p) d -> (l b t) p d", p=P)

        with m.round() as block:
            @block.sync
            def _(sp):
                sp.dma_start(gain[:], a["norm_gain"][0:1, :].to_broadcast([P, D])).then_inc(weights, 16)
                sp.dma_start(wkv[:], win[:, :, O_K:O_K + KVW]).then_inc(weights, 16)
                sp.dma_start(wik[:], win[:, :, O_IK:O_IK + IKW]).then_inc(weights, 16)
                sp.wait_ge(weights, 48)

        def tiles(n, rows, dram, dst):
            with m.round() as block:

                @block.sync
                def _(sp):
                    def load(t):
                        if t >= 2:
                            sp.wait_ge(normed, t - 1)
                        sp.dma_start(x_in[0:rows, t % 2, :], dram(t)[0]).then_inc(x_ready[t % 2], 16)

                    for t in range(min(n, 2)):
                        load(t)
                    for t in range(n):
                        s = t % 2
                        sp.wait_ge(evacuated, t + 1)
                        _, ko, vo, io = dram(t)
                        sp.dma_start(ko, kv[0:rows, s, 0:P]).then_inc(stored[s], 16)
                        sp.dma_start(vo, kv[0:rows, s, P:2 * P]).then_inc(stored[s], 16)
                        sp.dma_start(io, ik[0:rows, s, 0, :]).then_inc(stored[s], 16)
                        if t + 2 < n:
                            load(t + 2)
                    for s in range(min(n, 2)):
                        sp.wait_ge(stored[s], 48 * ((n + 1 - s) // 2))

                @block.scalar
                def _(act):
                    o = Chain(act, own_act)
                    def root(t):
                        s = t % 2
                        act.wait_ge(x_ready[s], 16 * (t // 2 + 1))
                        if t >= 2:
                            act.wait_ge(normed, t - 1)
                        o.done(nc.scalar.activation(junk[0:rows, :], x_in[0:rows, s, :], ACT.Square,
                                                    accum_out=st[0:rows, s, 0:1]))
                        nc.scalar.activation(st[0:rows, s, 5:6], st[0:rows, s, 0:1], ACT.Copy).then_inc(squared, 1)
                        act.wait_ge(meaned, t + 1)
                        nc.scalar.activation(st[0:rows, s, 2:3], st[0:rows, s, 1:2], ACT.Sqrt).then_inc(rooted, 1)

                    def keep(t):
                        xd, kd, ikd, _, _ = dst(t)
                        act.wait_ge(staged, t + 1)
                        nc.scalar.activation(xd, ps_t[:, :, 0:rows], ACT.Copy).then_inc(kept, 1)
                        act.wait_ge(k_turned, t + 1)
                        nc.scalar.activation(kd, ps_kt[:, 0, 0:rows], ACT.Copy)
                        nc.scalar.activation(ikd, ps_kt[:, 1, 0:rows], ACT.Copy).then_inc(k_kept, 1)

                    for t in range(n + 1):
                        if t < n:
                            root(t)
                        if t >= 1:
                            keep(t - 1)

                @block.vector
                def _(dve):
                    v = Chain(dve, own)

                    def norm(t):
                        s = t % 2
                        dve.wait_ge(squared, t + 1)
                        if t >= 2:
                            dve.wait_ge(turned, t - 1)
                        v.done(nc.vector.tensor_scalar(st[0:rows, s, 1:2], st[0:rows, s, 5:6], 1.0 / D, EPS,
                                                       ALU.mult, ALU.add))
                        nc.vector.tensor_copy(st[0:rows, s, 6:7], st[0:rows, s, 1:2]).then_inc(meaned, 1)
                        dve.wait_ge(rooted, t + 1)
                        refined_rstd(nc, v, st[0:rows, s, 1:2], st[0:rows, s, 4:5], st[0:rows, s, 3:4],
                                     st[0:rows, s, 2:3])
                        nc.vector.scalar_tensor_tensor(xn[0:rows, s, :], x_in[0:rows, s, :], st[0:rows, s, 3:4],
                                                       gain[0:rows, :], ALU.mult, ALU.mult).then_inc(normed, 1)

                    def evacuate(t):
                        s = t % 2
                        _, _, _, vd, iwd = dst(t)
                        dve.wait_ge(turned, t + 1)
                        if t >= 2:
                            dve.wait_ge(projected, t - 1)
                        nc.vector.tensor_copy(xt[:, s, :, 0:rows], ps_t[:, :, 0:rows]).then_inc(staged, 1)
                        dve.wait_ge(projected, t + 1)
                        if t >= 2:
                            dve.wait_ge(stored[s], 48 * (t // 2))
                            dve.wait_ge(k_turned, t - 1)
                        nc.vector.tensor_copy(kv[0:rows, s, :], ps_kv[0:rows, 0:KVW])
                        nc.vector.tensor_copy(vd, ps_kv[0:rows, P:2 * P])
                        nc.vector.tensor_scalar(iwd, ps_kv[0:rows, KVW + ID:KVW + IKW], ISCALE, None, ALU.mult)
                        nc.vector.tensor_copy(ik[0:rows, s, 0, :], ps_kv[0:rows, KVW:KVW + ID])
                        nc.vector.tensor_copy(ik[0:rows, s, 1, :], ps_kv[0:rows, KVW:KVW + ID]).then_inc(evacuated, 1)

                    for t in range(n + 1):
                        if t < n:
                            norm(t)
                        if t >= 1:
                            evacuate(t - 1)

                @block.tensor
                def _(pe):
                    for t in range(n):
                        s = t % 2
                        pe.wait_ge(normed, t + 1)
                        if t >= 1:
                            pe.wait_ge(kept, t)
                        for k in range(KC):
                            last = nc.tensor.transpose(ps_t[:, k, 0:rows], xn[0:rows, s, k * P:(k + 1) * P],
                                                       c.ident[0:rows, 0:rows])
                        last.then_inc(turned, 1)
                        pe.wait_ge(staged, t + 1)
                        if t >= 1:
                            pe.wait_ge(evacuated, t)
                        for k in range(KC):
                            nc.tensor.matmul(ps_kv[0:rows, 0:KVW], xt[:, s, k, 0:rows], wkv[:, k, :],
                                             start=(k == 0), stop=(k == KC - 1))
                        for k in range(KC):
                            last = nc.tensor.matmul(ps_kv[0:rows, KVW:KVW + IKW], xt[:, s, k, 0:rows],
                                                    wik[:, k, :], start=(k == 0), stop=(k == KC - 1))
                        last.then_inc(projected, 1)
                        pe.wait_ge(evacuated, t + 1)
                        if t >= 1:
                            pe.wait_ge(k_kept, t)
                        nc.tensor.transpose(ps_kt[:, 0, 0:rows], kv[0:rows, s, 0:P], c.ident[0:rows, 0:rows])
                        nc.tensor.transpose(ps_kt[:, 1, 0:rows], ik[0:rows, s, :, :].rearrange("p a d -> p (a d)"),
                                            c.ident[0:rows, 0:rows]).then_inc(k_turned, 1)

        with nc.Fori(0, NBAND) as i:
            def dram(t):
                u = i * TPB + t
                return x_tiles[u], k_out[u], v_out[u], i_out[u]

            def dst(t):
                u = i * TPB + t
                return (c.xnT[:, :, bass.ds(u * P, P)], c.kT[:, bass.ds(u * P, P)], c.ikT[:, bass.ds(u * P, P)],
                        c.v[:, bass.ds(u * P, P)], c.iw[:, bass.ds(u * NI, NI)])
            tiles(TPB, P, dram, dst)

        def sample_dram(t):
            return (a["x_sample"].rearrange("b t d -> (b t) d"), a["new_k_sample"].rearrange("l b t h d -> (l b t) (h d)"),
                    a["new_v_sample"].rearrange("l b t h d -> (l b t) (h d)"),
                    a["new_kidx_sample"].rearrange("l b t d -> (l b t) d"))
        tiles(1, ST, sample_dram, lambda t: (c.xsT[:], c.ksT[:], c.iksT[:], c.vs[:], c.iws[:]))


def stage_prompt_attention(nc, c, a):
    with ExitStack() as ctx:
        m = Stage(nc, ctx, "attn")
        wq = m.sb("wq", [P, 2, KC, NH * HD])
        qT = m.sb("qT", [P, 2, 4, BAND])
        q_idx = m.sb("q_idx", [P, 4, P])
        q_att = m.sb("q_att", [P, G, P])
        relu = m.sb("relu", [P, 4, 512])
        bias_h = relu
        acc = m.sb("acc", [P, S])
        bias = m.sb("bias", [P, S])
        prob = m.sb("prob", [P, 2, S])
        probT = m.sb("probT", [P, 2, 4, P])
        later = m.sb("later", [P, BAND])
        att = m.sb("att", [P, NH * HD])
        attT = m.sb("attT", [P, 4, P])
        iw = m.sb("iw", [P, NI])
        first = m.sb("first", [P, 1])
        best = m.sb("best", [P, 8])
        chunk_max = m.sb("chunk_max", [P, 4])
        negmax = m.sb("negmax", [P, NH])
        rowsum = m.sb("rowsum", [P, NH])
        ps_s = m.psum("ps_s", [P, 4, 512])
        ps_p = m.psum("ps_p", [P, 2, 4, P])
        ps_o = m.psum("ps_o", [P, NH * HD])
        ps_f = m.psum("ps_f", [P, 4, P])
        (loaded, projected, kept, q_staged, tile_ready, scored, rectified, summed, masked, scaled,
         multiplied, biased, maxed, exped, turned, turned_kept, weighted, normalised, att_turned,
         att_kept, stored, own) = [m.sem(n) for n in (
            "loaded", "projected", "kept", "q_staged", "tile_ready", "scored", "rectified", "summed",
            "masked", "scaled", "multiplied", "biased", "maxed", "exped", "turned", "turned_kept",
            "weighted", "normalised", "att_turned", "att_kept", "stored", "own")]
        win = a["w_in"].rearrange("l (k p) n -> (l p) k n", p=P)
        attn_out = a["attn_t"].rearrange("(n p) t -> p n t", p=P)

        with m.round() as block:
            @block.sync
            def _(sp):
                for j, col in enumerate((O_IQ, O_Q)):
                    sp.dma_start(wq[:, j], win[:, :, col:col + NH * HD]).then_inc(loaded, 16)
                sp.wait_ge(loaded, 32)

        def project(b):
            with m.round() as block:
                @block.tensor
                def _(pe):
                    for g in range(8):
                        if g >= 4:
                            pe.wait_ge(kept, g - 3)
                        for k in range(KC):
                            last = nc.tensor.matmul(ps_s[:, g % 4, :], wq[:, g // 4, k, (g % 4) * P:(g % 4 + 1) * P],
                                                    c.xnT[:, k, b * BAND:(b + 1) * BAND],
                                                    start=(k == 0), stop=(k == KC - 1))
                        last.then_inc(projected, 1)

                @block.scalar
                def _(act):
                    for g in range(8):
                        act.wait_ge(projected, g + 1)
                        nc.scalar.activation(qT[:, g // 4, g % 4, :], ps_s[:, g % 4, :], ACT.Copy,
                                             scale=1.0 if g < 4 else QSCALE).then_inc(kept, 1)

        def tile(b, i):
            nch = b + 1
            L = nch * BAND
            T = i + b * TPB
            with m.round() as block:

                @block.scalar
                def _(act):
                    rows = bass.ds(i * P, P)
                    nc.scalar.activation(q_idx[:], qT[:, 0, :, rows], ACT.Copy).then_inc(q_staged, 1)
                    for hh in range(2):
                        for kv in range(2):
                            nc.scalar.activation(q_att[kv * 64:kv * 64 + 64, hh::2, :],
                                                 qT[hh * 64:hh * 64 + 64, 1, 2 * kv:2 * kv + 2, rows],
                                                 ACT.Copy).then_inc(q_staged, 1)
                    for g in range(4 * nch):
                        act.wait_ge(scored, g + 1)
                        if g >= 2:
                            act.wait_ge(summed, 2 * (g - 1))
                        nc.scalar.activation(relu[:, 2 * (g % 2):2 * (g % 2) + 2, :],
                                             ps_s[:, 2 * (g % 2):2 * (g % 2) + 2, :], ACT.Relu).then_inc(rectified, 1)

                    def scale(h):
                        for ch in range(nch):
                            j = h * nch + ch
                            if j >= 4:
                                act.wait_ge(biased, j - 3)
                            nc.scalar.activation(bias_h[:, j % 4, :], bias[:, ch * 512:(ch + 1) * 512], ACT.Copy,
                                                 scale=SLOPES[h]).then_inc(scaled, 1)

                    act.wait_ge(masked, 1)
                    scale(0)
                    for h in range(NH):
                        if h + 1 < NH:
                            scale(h + 1)
                        act.wait_ge(maxed, h + 1)
                        nc.scalar.activation(prob[:, h % 2, 0:L], prob[:, h % 2, 0:L], ACT.Exp,
                                             bias=negmax[:, h:h + 1], accum_out=rowsum[:, h:h + 1]).then_inc(exped, 1)
                        for ch in range(nch):
                            j = h * nch + ch
                            act.wait_ge(turned, j + 1)
                            if j >= 2:
                                act.wait_ge(weighted, j - 1)
                            nc.scalar.activation(probT[:, j % 2], ps_p[:, j % 2], ACT.Copy).then_inc(turned_kept, 1)
                    act.wait_ge(att_turned, 1)
                    nc.scalar.activation(attT[:], ps_f[:], ACT.Copy).then_inc(att_kept, 1)

                @block.vector
                def _(dve):
                    v = Chain(dve, own)
                    diag = slice(b * BAND, (b + 1) * BAND)
                    v.done(nc.vector.tensor_copy(first[:], c.tilepos[:, bass.ds(T, 1)]))
                    v.done(nc.vector.tensor_copy(iw[:], c.iw[:, bass.ds(T * NI, NI)]))
                    v.done(nc.vector.tensor_scalar(later[:], c.keypos[:, diag], first[:], 0.0, ALU.subtract, ALU.is_gt))
                    v.done(nc.vector.tensor_scalar(later[:], later[:], MASKED, None, ALU.mult))
                    n = 0
                    for ch in range(nch):
                        out = acc[:, ch * 512:(ch + 1) * 512]
                        for g in range(4):
                            dve.wait_ge(rectified, ch * 4 + g + 1)
                            for hh in range(2):
                                h = 2 * g + hh
                                src = relu[:, 2 * ((ch * 4 + g) % 2) + hh, :]
                                if h == 0 and ch < b:
                                    ins = nc.vector.tensor_scalar(out, src, iw[:, 0:1], None, ALU.mult)
                                else:
                                    ins = nc.vector.scalar_tensor_tensor(out, src, iw[:, h:h + 1],
                                                                         later[:] if h == 0 else out, ALU.mult, ALU.add)
                                ins.then_inc(summed, 1)
                                n += 1
                                dve.wait_ge(summed, n)
                    for _ in range(TOPK // 8):
                        v.done(nc.vector.max(best[:], acc[:, 0:L]))
                        v.done(nc.vector.match_replace(acc[:, 0:L], best[:], acc[:, 0:L], TAKEN))
                    v.done(nc.vector.tensor_scalar(bias[:, 0:L], acc[:, 0:L], TAKEN, -BIG, ALU.not_equal, ALU.mult))
                    v.done(nc.vector.scalar_tensor_tensor(bias[:, 0:L], c.keypos[:, 0:L], first[:], bias[:, 0:L],
                                                          ALU.subtract, ALU.add))
                    nc.vector.scalar_tensor_tensor(bias[:, diag], later[:], BIG / -MASKED, bias[:, diag],
                                                   ALU.mult, ALU.add).then_inc(masked, 1)
                    for h in range(NH):
                        if h >= 2:
                            dve.wait_ge(turned, (h - 1) * nch)
                        for ch in range(nch):
                            j = h * nch + ch
                            dve.wait_ge(multiplied, j + 1)
                            dve.wait_ge(scaled, j + 1)
                            nc.vector.tensor_tensor_reduce(
                                out=prob[:, h % 2, ch * 512:(ch + 1) * 512], in0=ps_s[:, j % 4, :],
                                in1=bias_h[:, j % 4, :], scale=1.0, scalar=-3.0e38, op0=ALU.add, op1=ALU.max,
                                accum_out=chunk_max[:, ch:ch + 1]).then_inc(biased, 1)
                        dve.wait_ge(biased, (h + 1) * nch)
                        v.done(nc.vector.reduce_max(negmax[:, h:h + 1], chunk_max[:, 0:nch], AX_X))
                        nc.vector.tensor_scalar(negmax[:, h:h + 1], negmax[:, h:h + 1], -1.0, None,
                                                ALU.mult).then_inc(maxed, 1)
                    dve.wait_ge(exped, NH)
                    v.done(nc.vector.reciprocal(rowsum[:], rowsum[:]))
                    dve.wait_ge(weighted, NH * nch)
                    nc.vector.tensor_tensor(att[:].rearrange("p (h d) -> p h d", d=HD),
                                            ps_o[:].rearrange("p (h d) -> p h d", d=HD),
                                            rowsum[:].unsqueeze(2).to_broadcast([P, NH, HD]), ALU.mult).then_inc(normalised, 1)

                @block.tensor
                def _(pe):
                    pe.wait_ge(q_staged, 1)
                    for ch in range(nch):
                        for n in range(4):
                            g = ch * 4 + n
                            if g >= 2:
                                pe.wait_ge(rectified, g - 1)
                            for hh in range(2):
                                half = slice(hh * 64, hh * 64 + 64)
                                last = nc.tensor.matmul(ps_s[:, 2 * (g % 2) + hh, :], q_idx[half, n, :],
                                                        c.ikT[half, ch * 512:(ch + 1) * 512], start=True, stop=True)
                            last.then_inc(scored, 1)
                    pe.wait_ge(rectified, 4 * nch)
                    pe.wait_ge(q_staged, 5)

                    def scores(h):
                        half = slice(h // G * 64, h // G * 64 + 64)
                        for ch in range(nch):
                            j = h * nch + ch
                            if j >= 4:
                                pe.wait_ge(biased, j - 3)
                            nc.tensor.matmul(ps_s[:, j % 4, :], q_att[half, h % G, :],
                                             c.kT[half, ch * 512:(ch + 1) * 512],
                                             start=True, stop=True).then_inc(multiplied, 1)

                    def transpose(h, ch):
                        j = h * nch + ch
                        if j >= 2:
                            pe.wait_ge(turned_kept, j - 1)
                        for u in range(4):
                            last = nc.tensor.transpose(ps_p[:, j % 2, u, :], prob[:, h % 2, ch * 512 + u * P:ch * 512 + (u + 1) * P],
                                                       c.ident[:])
                        last.then_inc(turned, 1)

                    def weigh(h, ch):
                        j = h * nch + ch
                        kv = h // G
                        pe.wait_ge(turned_kept, j + 1)
                        for u in range(4):
                            t = ch * 4 + u
                            last = nc.tensor.matmul(ps_o[:, h * HD:(h + 1) * HD], probT[:, j % 2, u, :],
                                                    c.v[:, t * P + kv * HD:t * P + (kv + 1) * HD],
                                                    start=(t == 0), stop=(t == 4 * nch - 1))
                        last.then_inc(weighted, 1)

                    scores(0)
                    for h in range(NH):
                        if h + 1 < NH:
                            scores(h + 1)
                        pe.wait_ge(exped, h + 1)
                        transpose(h, 0)
                        for ch in range(nch):
                            if ch + 1 < nch:
                                transpose(h, ch + 1)
                            weigh(h, ch)
                    pe.wait_ge(normalised, 1)
                    for n in range(4):
                        last = nc.tensor.transpose(ps_f[:, n, :], att[:, n * P:(n + 1) * P], c.ident[:])
                    last.then_inc(att_turned, 1)

                @block.sync
                def _(sp):
                    sp.wait_ge(att_kept, 1)
                    sp.dma_start(attn_out[:, :, bass.ds(T * P, P)], attT[:]).then_inc(stored, 16)
                    sp.wait_ge(stored, 16)

        for b in range(NBAND):
            project(b)
            with nc.Fori(0, TPB) as i:
                tile(b, i)


KEYS = PAST + ST
QT = 4
TPR = PAGE // QT


def stage_sample_attention(nc, c, a):
    with ExitStack() as ctx:
        m = Stage(nc, ctx, "samp")
        k = Named()
        k.rows = m.sb("rows", [P, DB], I32)
        k.table = m.sb("table", [P, DB], I32)
        k.ints = m.sb("ints", [P, 16], I32)
        k.step8 = m.sb("step8", [P, NH], F32)
        k.low = m.sb("low", [P, 2], F32)
        k.same_t = m.sb("same_t", [P, DT])
        k.same_b = m.sb("same_b", [P, DB])
        k.later = m.sb("later", [ST, ST])
        k.newpos = m.sb("newpos", [ST, ST])
        k.slopes = m.sb("slopes", [ST, NH, DT])
        k.sel = m.sb("sel", [P, DB, ST])
        k.spread = m.sb("spread", [ST, DB, NH * DT])
        k.iq_bd = m.sb("iq_bd", [P, DB, P])
        k.q_bd = m.sb("q_bd", [P, DB, NH * DT])
        k.iw_rows = m.sb("iw_rows", [P, DB])
        k.bias = m.sb("bias", [ST, KEYS])
        k.attT = m.sb("attT", [HD, NH, ST])
        sample_scores(nc, c, a, k)
        sample_attend(nc, c, a, k)


def sample_scores(nc, c, a, o):
    (rows, table, ints, step8, low, same_t, same_b, later, newpos, slopes) = (
        o.rows, o.table, o.ints, o.step8, o.low, o.same_t, o.same_b, o.later, o.newpos, o.slopes)
    sel, spread, iq_bd, q_bd, iw_rows, bias = o.sel, o.spread, o.iq_bd, o.q_bd, o.iw_rows, o.bias
    with ExitStack() as ctx:
        m = Stage(nc, ctx, "sidx")
        kidx = m.sb("kidx", [P, DB, TPR * ID])
        with ExitStack() as inner:
            w = Stage(nc, inner, "sprj")
            wq = w.sb("wq", [P, 2, KC, NH * HD])
            qs = w.sb("qs", [P, 2, 4, ST])
            ps = w.psum("ps", [P, 8, ST])
            (tabled, loaded, stored, spread_in, ready, rowed, gathered, projected, kept, own) = [w.sem(n) for n in (
                "tabled", "loaded", "stored", "spread_in", "ready", "rowed", "gathered", "projected", "kept", "own")]
            win = a["w_in"].rearrange("l (k p) n -> (l p) k n", p=P)
            with w.round() as block:

                @block.sync
                def _(sp):
                    for q in range(QT):
                        sp.dma_start(table[q::QT, :], a["page_table"].rearrange("b j -> j b"),
                                     allow_slow_non_contiguous=True).then_inc(tabled, 16)
                    for b in range(DB):
                        sp.dma_start(a["iw_scratch"][b].rearrange("h t -> t h"), c.iws[b * DT:(b + 1) * DT, :],
                                     allow_slow_non_contiguous=True).then_inc(stored, 16)
                    for j, col in enumerate((O_IQ, O_Q)):
                        sp.dma_start(wq[:, j], win[:, :, col:col + NH * HD]).then_inc(loaded, 16)
                    sp.wait_ge(stored, 16 * DB)
                    for half in range(2):
                        sp.dma_start(iw_rows[half * 64:half * 64 + 64, :], a["iw_scratch"].rearrange("b h t -> (h t) b"),
                                     allow_slow_non_contiguous=True).then_inc(spread_in, 16)
                    sp.wait_ge(spread_in, 32)

                @block.gpsimd
                def _(pool):
                    nc.gpsimd.iota(ints[:, 0:1], [[0, 1]], base=0, channel_multiplier=1).then_inc(ready, 1)
                    nc.gpsimd.iota(ints[:, 8:16], [[1, 8]], base=0, channel_multiplier=0).then_inc(ready, 1)
                    nc.gpsimd.memset(iq_bd[:], 0.0).then_inc(ready, 1)
                    nc.gpsimd.memset(q_bd[:], 0.0).then_inc(ready, 1)
                    nc.gpsimd.memset(sel[:], 0.0).then_inc(ready, 1)
                    nc.gpsimd.memset(later[:], 0.0).then_inc(ready, 1)
                    pool.wait_ge(ready, 6)
                    nc.gpsimd.affine_select(out=later[:], in_=later[:], compare_op=ALU.is_ge, fill=MASKED, base=0,
                                            pattern=[[-1, ST]], channel_multiplier=1).then_inc(ready, 1)
                    pool.wait_ge(ready, 7)
                    v = later[:].rearrange("p (b t) -> p b t", t=DT)
                    nc.gpsimd.affine_select(out=v, in_=v, compare_op=ALU.is_ge, fill=MASKED, base=DT - 1,
                                            pattern=[[DT, DB], [0, DT]], channel_multiplier=-1).then_inc(ready, 1)
                    pool.wait_ge(rowed, 1)
                    src = a["cache_kidx"].rearrange("l n (q t) d -> (l n q) (t d)", q=QT)
                    for b in range(DB):
                        pool.indirect_dma_start(kidx[:, b, :], None, src,
                                                bass.IndirectOffsetOnAxis(ap=rows[:, b:b + 1], axis=0)).then_inc(gathered, 16)
                    pool.wait_ge(gathered, 16 * DB)
                    pool.dma_reset()

                @block.tensor
                def _(pe):
                    pe.wait_ge(loaded, 32)
                    for g in range(8):
                        for k in range(KC):
                            last = nc.tensor.matmul(ps[:, g, :], wq[:, g // 4, k, (g % 4) * P:(g % 4 + 1) * P],
                                                    c.xsT[:, k, :], start=(k == 0), stop=(k == KC - 1))
                    last.then_inc(projected, 1)

                @block.scalar
                def _(act):
                    act.wait_ge(projected, 1)
                    nc.scalar.activation(qs[:, 0], ps[:, 0:4, :], ACT.Copy)
                    nc.scalar.activation(qs[:, 1], ps[:, 4:8, :], ACT.Copy, scale=QSCALE).then_inc(kept, 1)

                @block.vector
                def _(dve):
                    v = Chain(dve, own)
                    nc.vector.memset(ints[:, 4:6], 0)
                    dve.wait_ge(ready, 5)
                    v.done(nc.vector.tensor_scalar(ints[:, 1:2], ints[:, 0:1], 3, None, ALU.bitwise_and))
                    dve.wait_ge(tabled, 16 * QT)
                    v.done(nc.vector.tensor_scalar(rows[:], table[:], float(QT), None, ALU.mult))
                    nc.vector.tensor_tensor(rows[:], rows[:], ints[:, 1:2].to_broadcast([P, DB]), ALU.add).then_inc(rowed, 1)
                    v.done(nc.vector.tensor_scalar(ints[:, 2:3], ints[:, 0:1], 7, None, ALU.bitwise_and))
                    v.done(nc.vector.tensor_scalar(ints[:, 3:4], ints[:, 0:1], 3, None, ALU.logical_shift_right))
                    v.done(nc.vector.tensor_copy(low[:], ints[:, 2:4]))
                    v.done(nc.vector.tensor_copy(step8[:], ints[:, 8:16]))
                    v.done(nc.vector.tensor_scalar(same_t[:], step8[:], low[:, 0:1], None, ALU.is_equal))
                    v.done(nc.vector.tensor_scalar(same_b[:], step8[:], low[:, 1:2], None, ALU.is_equal))
                    for b in range(DB):
                        v.done(nc.vector.tensor_copy(sel[:, b, b * DT:(b + 1) * DT], same_t[:]))
                    for h in range(NH):
                        v.done(nc.vector.tensor_scalar(slopes[:, h, :], same_t[0:ST, :], SLOPES[h], None, ALU.mult))
                    for b in range(DB):
                        v.done(nc.vector.tensor_scalar(spread[:, b, :], slopes[:].rearrange("p h t -> p (h t)"),
                                                       same_b[0:ST, b:b + 1], None, ALU.mult))
                    cols = newpos[:].rearrange("p (b t) -> p b t", t=DT)
                    v.done(nc.vector.tensor_copy(cols, step8[0:ST, :].unsqueeze(1).to_broadcast([ST, DB, DT])))
                    v.done(nc.vector.tensor_scalar(newpos[:], newpos[:], low[0:ST, 0:1], None, ALU.subtract))
                    dve.wait_ge(kept, 1)
                    for par in range(2):
                        for hh in range(2):
                            dst = iq_bd[par * 64:par * 64 + 64, :, par * 64:par * 64 + 64]
                            v.done(nc.vector.tensor_copy(
                                dst.rearrange("d b (n i t) -> d i n b t", i=2, t=DT)[:, hh],
                                qs[hh * 64:hh * 64 + 64, 0].rearrange("d n (b t) -> d n b t", t=DT)))
                    for kv in range(NKV):
                        for hh in range(2):
                            dst = q_bd[kv * 64:kv * 64 + 64, :, kv * 32:kv * 32 + 32]
                            v.done(nc.vector.tensor_copy(
                                dst.rearrange("d b (n i t) -> d i n b t", i=2, t=DT)[:, hh],
                                qs[hh * 64:hh * 64 + 64, 1, 2 * kv:2 * kv + 2].rearrange("d n (b t) -> d n b t", t=DT)))

        score = m.sb("score", [ST, KEYS])
        best = m.sb("best", [ST, 8])
        keysT = m.sb("keysT", [P, 2, 512])
        relu = m.sb("relu", [P, 2, 512])
        kpos = m.sb("kpos", [ST, PAST], I32)
        ps_t = m.psum("ps_t", [P, 2, 4, P])
        ps_i = m.psum("ps_i", [P, 2, 512])
        ps_s = m.psum("ps_s", [ST, 2, 2, 512])
        (turned, kept, scored, rectified, summed, read, positioned, own) = [m.sem(n) for n in (
            "turned", "kept", "scored", "rectified", "summed", "read", "positioned", "own")]
        items = [(ch, b) for ch in range(5) for b in range(DB)]
        with m.round() as block:

            @block.gpsimd
            def _(pool):
                nc.gpsimd.iota(kpos[:], [[1, PAST]], base=-PAST, channel_multiplier=0).then_inc(positioned, 1)

            @block.tensor
            def _(pe):
                def turn(g):
                    ch, b = items[g]
                    if g >= 2:
                        pe.wait_ge(kept, g - 1)
                    for u in range(4):
                        t = (ch * 4 + u) * 2
                        last = nc.tensor.transpose(ps_t[:, g % 2, u, :], kidx[:, b, t * ID:(t + 2) * ID], c.ident[:])
                    last.then_inc(turned, 1)

                def score_of(g):
                    ch, b = items[g]
                    if g >= 2:
                        pe.wait_ge(rectified, g - 1)
                    if ch < 4:
                        pe.wait_ge(kept, g + 1)
                        nc.tensor.matmul(ps_i[:, g % 2, :], iq_bd[:, b, :], keysT[:, g % 2, :],
                                         start=True, stop=True).then_inc(scored, 1)
                    else:
                        nc.tensor.matmul(ps_i[0:64, g % 2, 0:ST], iq_bd[0:64, b, 0:64], c.iksT[0:64, :],
                                         start=True, stop=True).then_inc(scored, 1)

                def sum_heads(g):
                    ch, b = items[g]
                    pe.wait_ge(rectified, g + 1)
                    if b == 0 and ch >= 2:
                        pe.wait_ge(read, ch - 1)
                    if ch < 4:
                        for par in range(2):
                            half = slice(par * 64, par * 64 + 64)
                            last = nc.tensor.matmul(ps_s[:, ch % 2, par, :], sel[half, b, :], relu[half, g % 2, :],
                                                    start=(b == 0), stop=(b == DB - 1))
                    else:
                        last = nc.tensor.matmul(ps_s[:, 0, 0, 0:ST], sel[0:64, b, :], relu[0:64, g % 2, 0:ST],
                                                start=(b == 0), stop=(b == DB - 1))
                    last.then_inc(summed, 1)

                turn(0)
                for g in range(len(items)):
                    if g + 1 < 4 * DB:
                        turn(g + 1)
                    score_of(g)
                    if g >= 1:
                        sum_heads(g - 1)
                sum_heads(len(items) - 1)

            @block.scalar
            def _(act):
                for g in range(4 * DB):
                    act.wait_ge(turned, g + 1)
                    if g >= 2:
                        act.wait_ge(scored, g - 1)
                    nc.scalar.activation(keysT[:, g % 2, :], ps_t[:, g % 2].rearrange("p u k -> p (u k)"),
                                         ACT.Copy).then_inc(kept, 1)

            @block.vector
            def _(dve):
                v = Chain(dve, own)

                def rectify(g):
                    ch, b = items[g]
                    n, width = (P, 512) if ch < 4 else (64, ST)
                    dve.wait_ge(scored, g + 1)
                    if g >= 2:
                        dve.wait_ge(summed, g - 1)
                    nc.vector.tensor_scalar(relu[0:n, g % 2, 0:width], ps_i[0:n, g % 2, 0:width], 0.0,
                                            iw_rows[0:n, b:b + 1], ALU.max, ALU.mult).then_inc(rectified, 1)

                def collect(ch):
                    dve.wait_ge(summed, (ch + 1) * DB)
                    if ch == 4:
                        v.done(nc.vector.tensor_tensor(score[:, PAST:KEYS], ps_s[:, 0, 0, 0:ST], later[:], ALU.add))
                        return
                    by_key = score[:, 0:PAST].rearrange("r (p v q) -> r q v p", v=TPR // 2, q=2)
                    for par in range(2):
                        last = nc.vector.tensor_copy(by_key[:, par, ch * 4:ch * 4 + 4, :],
                                                     ps_s[:, ch % 2, par, :].rearrange("r (v p) -> r v p", p=P))
                    last.then_inc(read, 1)

                for g in range(len(items)):
                    rectify(g)
                    if g >= DB and g % DB == 1:
                        collect(g // DB - 1)
                collect(4)
                dve.wait_ge(read, 4)
                for _ in range(TOPK // 8):
                    v.done(nc.vector.max(best[:], score[:]))
                    v.done(nc.vector.match_replace(score[:], best[:], score[:], TAKEN))
                v.done(nc.vector.tensor_scalar(bias[:], score[:], TAKEN, -BIG, ALU.not_equal, ALU.mult))
                dve.wait_ge(positioned, 1)
                v.done(nc.vector.tensor_copy(score[:, 0:PAST], kpos[:]))
                v.done(nc.vector.scalar_tensor_tensor(bias[:, 0:PAST], score[:, 0:PAST], low[0:ST, 0:1],
                                                      bias[:, 0:PAST], ALU.subtract, ALU.add))
                v.done(nc.vector.tensor_tensor(bias[:, PAST:KEYS], bias[:, PAST:KEYS], newpos[:], ALU.add))
                v.done(nc.vector.scalar_tensor_tensor(bias[:, PAST:KEYS], later[:], BIG / -MASKED,
                                                      bias[:, PAST:KEYS], ALU.mult, ALU.add))


def sample_attend(nc, c, a, o):
    rows, spread, q_bd, bias, attT = o.rows, o.spread, o.q_bd, o.bias, o.attT
    with ExitStack() as ctx:
        m = Stage(nc, ctx, "satt")
        R = NH * DT
        keys = m.sb("keys", [P, 2, TPR, P])
        values = m.sb("values", [P, 2, TPR, P])
        row_ids = m.sb("row_ids", [P, 2], I32)
        q_st = m.sb("q_st", [P, 2, R])
        spread_st = m.sb("spread_st", [ST, 2, R])
        keysT = m.sb("keysT", [P, 2, 512])
        prob = m.sb("prob", [R, 2, KEYS])
        probT = m.sb("probT", [P, 2, 8, R])
        att = m.sb("att", [R, 2, HD])
        chunk_max = m.sb("chunk_max", [R, 2, 16])
        negmax = m.sb("negmax", [R, 2])
        rowsum = m.sb("rowsum", [R, 2])
        ps_t = m.psum("ps_t", [P, 2, 4, P])
        ps_s = m.psum("ps_s", [R, 2, 512])
        ps_p = m.psum("ps_p", [P, 2, 8, R])
        ps_o = m.psum("ps_o", [R, P])
        ps_f = m.psum("ps_f", [HD, R])
        (indexed, staged, turned, kept, multiplied, moved, maxed, exped, p_turned, p_kept, weighted,
         normalised, att_turned, att_kept, stored, own) = [m.sem(n) for n in (
            "indexed", "staged", "turned", "kept", "multiplied", "moved", "maxed", "exped", "p_turned", "p_kept",
            "weighted", "normalised", "att_turned", "att_kept", "stored", "own")]
        k_in = [m.sem(f"k_in{u}") for u in range(2)]
        v_in = [m.sem(f"v_in{u}") for u in range(2)]
        NC = PAST // 512
        k_src = a["cache_k"].rearrange("l n (q t) h d -> (l n q) (t h d)", q=QT)
        v_src = a["cache_v"].rearrange("l n (q t) h d -> (l n q) (t h d)", q=QT)

        def pair(i):
            with m.round() as block:

                @block.gpsimd
                def _(pool):
                    pool.wait_ge(indexed, 1)
                    for dst, src, sems in ((keys, k_src, k_in), (values, v_src, v_in)):
                        for u in range(2):
                            pool.indirect_dma_start(dst[:, u].rearrange("p v d -> p (v d)"), None, src,
                                                    bass.IndirectOffsetOnAxis(ap=row_ids[:, u:u + 1], axis=0)
                                                    ).then_inc(sems[u], 16)
                    for sems in (k_in, v_in):
                        for u in range(2):
                            pool.wait_ge(sems[u], 16)
                    pool.dma_reset()

                @block.tensor
                def _(pe):
                    pe.wait_ge(staged, 2)

                    def turn(u, ch):
                        g = u * NC + ch
                        if ch == 0:
                            pe.wait_ge(k_in[u], 16)
                        if g >= 2:
                            pe.wait_ge(kept, g - 1)
                        for n in range(4):
                            last = nc.tensor.transpose(ps_t[:, g % 2, n, :], keys[:, u, ch * 4 + n, :], c.ident[:])
                        last.then_inc(turned, 1)

                    def scores(u, ch):
                        j = u * (NC + 1) + ch
                        if j >= 2:
                            pe.wait_ge(moved, j - 1)
                        if ch < NC:
                            pe.wait_ge(kept, u * NC + ch + 1)
                            width, kT = 512, keysT[:, (u * NC + ch) % 2, :]
                            kb = bias[:, 0:PAST].rearrange("r (p v) -> r v p", v=TPR)[:, ch * 4:ch * 4 + 4, :]
                        else:
                            width, kT, kb = ST, c.ksT[:], bias[:, PAST:KEYS]
                        nc.tensor.matmul(ps_s[:, j % 2, 0:width], q_st[:, u, :], kT, start=True, stop=False)
                        nc.tensor.matmul(ps_s[:, j % 2, 0:width], spread_st[:, u, :], kb,
                                         start=False, stop=True).then_inc(multiplied, 1)

                    def p_turn(u, q):
                        g = u * 5 + q
                        if g >= 2:
                            pe.wait_ge(p_kept, g - 1)
                        if q < 4:
                            for n in range(8):
                                v = q * 8 + n
                                last = nc.tensor.transpose(ps_p[:, g % 2, n, :], prob[:, u, v * P:(v + 1) * P],
                                                           c.ident[0:R, 0:R])
                        else:
                            last = nc.tensor.transpose(ps_p[0:ST, g % 2, 0, :], prob[:, u, PAST:KEYS], c.ident[0:R, 0:R])
                        last.then_inc(p_turned, 1)

                    def weigh(u, q):
                        g = u * 5 + q
                        pe.wait_ge(p_kept, g + 1)
                        if q == 0:
                            pe.wait_ge(v_in[u], 16)
                            if u:
                                pe.wait_ge(normalised, 1)
                        if q < 4:
                            for n in range(8):
                                v = q * 8 + n
                                last = nc.tensor.matmul(ps_o[:], probT[:, g % 2, n, :], values[:, u, v, :],
                                                        start=(v == 0), stop=False)
                        else:
                            last = nc.tensor.matmul(ps_o[:], probT[0:ST, g % 2, 0, :], c.vs[:], start=False, stop=True)
                        last.then_inc(weighted, 1)

                    for u in range(2):
                        turn(u, 0)
                        for ch in range(NC):
                            if ch + 1 < NC:
                                turn(u, ch + 1)
                            scores(u, ch)
                        scores(u, NC)
                    for u in range(2):
                        pe.wait_ge(exped, u + 1)
                        p_turn(u, 0)
                        for q in range(5):
                            if q < 4:
                                p_turn(u, q + 1)
                            weigh(u, q)
                        pe.wait_ge(normalised, u + 1)
                        if u:
                            pe.wait_ge(att_kept, 1)
                        nc.tensor.transpose(ps_f[:], att[:, u, :], c.ident[0:R, 0:R]).then_inc(att_turned, 1)

                @block.scalar
                def _(act):
                    nc.scalar.activation(q_st[:], q_bd[:, bass.ds(i * 2, 2), :], ACT.Copy).then_inc(staged, 1)
                    nc.scalar.activation(spread_st[:], spread[:, bass.ds(i * 2, 2), :], ACT.Copy).then_inc(staged, 1)

                    def exp(u):
                        act.wait_ge(maxed, u + 1)
                        nc.scalar.activation(prob[:, u, :], prob[:, u, :], ACT.Exp, bias=negmax[:, u:u + 1],
                                             accum_out=rowsum[:, u:u + 1]).then_inc(exped, 1)

                    for u in range(2):
                        for ch in range(NC):
                            g = u * NC + ch
                            act.wait_ge(turned, g + 1)
                            if g >= 2:
                                act.wait_ge(multiplied, (g - 2) // NC * (NC + 1) + (g - 2) % NC + 1)
                            nc.scalar.activation(keysT[:, g % 2, :], ps_t[:, g % 2].rearrange("p u k -> p (u k)"),
                                                 ACT.Copy).then_inc(kept, 1)
                    exp(0)
                    exp(1)
                    for u in range(2):
                        for q in range(5):
                            g = u * 5 + q
                            act.wait_ge(p_turned, g + 1)
                            if g >= 2:
                                act.wait_ge(weighted, g - 1)
                            if q < 4:
                                nc.scalar.activation(probT[:, g % 2], ps_p[:, g % 2], ACT.Copy).then_inc(p_kept, 1)
                            else:
                                nc.scalar.activation(probT[0:ST, g % 2, 0, :], ps_p[0:ST, g % 2, 0, :],
                                                     ACT.Copy).then_inc(p_kept, 1)
                        act.wait_ge(att_turned, u + 1)
                        dst = attT[:].rearrange("d h (b t) -> d h b t", t=DT)[:, :, bass.ds(i * 2 + u, 1), :]
                        nc.scalar.activation(dst, ps_f[:].rearrange("d (h t) -> d h t", t=DT).unsqueeze(2),
                                             ACT.Copy).then_inc(att_kept, 1)
                    act.wait_ge(att_kept, 2)

                @block.vector
                def _(dve):
                    v = Chain(dve, own)
                    nc.vector.tensor_copy(row_ids[:], rows[:, bass.ds(i * 2, 2)]).then_inc(indexed, 1)
                    for u in range(2):
                        for ch in range(NC + 1):
                            j = u * (NC + 1) + ch
                            width = 512 if ch < NC else ST
                            dve.wait_ge(multiplied, j + 1)
                            nc.vector.tensor_scalar(prob[:, u, ch * 512:ch * 512 + width], ps_s[:, j % 2, 0:width], 1.0,
                                                    None, ALU.mult, ALU.max,
                                                    accum_out=chunk_max[:, u, ch:ch + 1]).then_inc(moved, 1)
                        dve.wait_ge(moved, (u + 1) * (NC + 1))
                        v.done(nc.vector.reduce_max(negmax[:, u:u + 1], chunk_max[:, u, 0:NC + 1], AX_X))
                        nc.vector.tensor_scalar(negmax[:, u:u + 1], negmax[:, u:u + 1], -1.0, None,
                                                ALU.mult).then_inc(maxed, 1)
                    for u in range(2):
                        dve.wait_ge(exped, u + 1)
                        v.done(nc.vector.reciprocal(rowsum[:, u:u + 1], rowsum[:, u:u + 1]))
                        dve.wait_ge(weighted, 5 * (u + 1))
                        for kv in range(NKV):
                            r = slice(kv * 32, kv * 32 + 32)
                            last = nc.vector.tensor_scalar(att[r, u, :], ps_o[r, kv * HD:(kv + 1) * HD],
                                                           rowsum[r, u:u + 1], None, ALU.mult)
                        last.then_inc(normalised, 1)

        with nc.Fori(0, DB // 2) as i:
            pair(i)
        with m.round() as block:
            @block.sync
            def _(sp):
                sp.dma_start(a["attn_t"].rearrange("(h d) t -> d h t", d=HD)[:, :, S:S + ST], attT[:]).then_inc(stored, 16)
                sp.wait_ge(stored, 16)


def stage_gates(nc, c, a):
    with ExitStack() as ctx:
        m = Stage(nc, ctx, "gate")
        w = m.sb("w", [P, 2, 4, KC, P])
        wg = m.sb("wg", [P, 2, KC, 4 * P])
        convw = m.sb("convw", [P, 3, 4])
        p_all = m.sb("p_all", [P, 2 + S])
        p_new = m.sb("p_new", [P, DB, 2 + DT])
        u_sb = m.sb("u_sb", [P, 2, 512])
        z_sb = m.sb("z_sb", [P, 2, 512])
        y_sb = m.sb("y_sb", [P, 2, 512])
        out_sb = m.sb("out_sb", [P, 4, 512])
        ps = m.psum("ps", [P, 8, 512])
        (prev, projected, u_kept, z_kept, multiplied, gated, acted, saved, own) = [m.sem(n) for n in (
            "prev", "projected", "u_kept", "z_kept", "multiplied", "gated", "acted", "saved", "own")]
        loaded = [m.sem(f"loaded{s}") for s in range(2)]
        stored = [m.sem(f"stored{s}") for s in range(4)]
        win = a["w_in"].rearrange("l (k p) n -> (l p) k n", p=P)
        conv_out = a["conv_t"].rearrange("(g p) t -> g p t", p=P)
        state = a["state_conv"].rearrange("l b j (g p) -> g p (l b) j", p=P)
        new_p = a["new_conv_prompt"].rearrange("l b j (g p) -> g p (l b j)", p=P)
        new_s = a["new_conv_sample"].rearrange("l b j (g p) -> g p (l b) j", p=P)
        chunks = [(ch * 512, 512) for ch in range(NBAND)] + [(S, ST)]

        def tokens(k, ch):
            return c.xnT[:, k, ch * 512:(ch + 1) * 512] if ch < NBAND else c.xsT[:, k, :]

        with m.round() as block:
            @block.sync
            def _(sp):
                for j in range(3):
                    sp.dma_start(convw[:, j, :], a["conv_w"][0, j, :].rearrange("(g p) -> p g", p=P),
                                 allow_slow_non_contiguous=True).then_inc(prev, 16)
                sp.wait_ge(prev, 48)

            @block.vector
            def _(dve):
                nc.vector.memset(p_all[:, 0:2], 0.0)

        def conv(g):
            with m.round() as block:

                @block.sync
                def _(sp):
                    for j, col in enumerate((O_C, O_U, O_Z, O_B)):
                        sp.dma_start(w[:, 0, j], win[:, :, bass.ds(g * P + col, P)]).then_inc(loaded[0], 16)
                    for b in range(DB):
                        sp.dma_start(p_new[:, b, 0:2], state[g][:, b, :], allow_slow_non_contiguous=True).then_inc(prev, 16)
                    for ch, (t0, width) in enumerate(chunks):
                        sp.wait_ge(gated, ch + 1)
                        sp.dma_start(conv_out[g][:, t0:t0 + width], y_sb[:, ch % 2, 0:width]).then_inc(stored[ch % 2], 16)
                    sp.dma_start(new_p[g], p_all[:, S:S + 2], allow_slow_non_contiguous=True).then_inc(stored[2], 16)
                    for b in range(DB):
                        sp.dma_start(new_s[g][:, b, :], p_new[:, b, DT:DT + 2],
                                     allow_slow_non_contiguous=True).then_inc(stored[2], 16)
                    sp.wait_ge(stored[0], 48)
                    sp.wait_ge(stored[1], 32)
                    sp.wait_ge(stored[2], 16 + 16 * DB)

                @block.tensor
                def _(pe):
                    pe.wait_ge(loaded[0], 64)
                    for ch, (_, width) in enumerate(chunks):
                        if ch >= 2:
                            pe.wait_ge(gated, ch - 1)
                            pe.wait_ge(z_kept, ch - 1)
                        for j in range(4):
                            for k in range(KC):
                                last = nc.tensor.matmul(ps[:, 4 * (ch % 2) + j, 0:width], w[:, 0, j, k, :],
                                                        tokens(k, ch), start=(k == 0), stop=(k == KC - 1))
                            last.then_inc(projected, 1)

                @block.scalar
                def _(act):
                    for ch, (_, width) in enumerate(chunks):
                        s = ch % 2
                        act.wait_ge(projected, 4 * ch + 2)
                        if ch >= 2:
                            act.wait_ge(gated, ch - 1)
                        nc.scalar.activation(u_sb[:, s, 0:width], ps[:, 4 * s + 1, 0:width], ACT.Copy).then_inc(u_kept, 1)
                        act.wait_ge(projected, 4 * ch + 3)
                        nc.scalar.activation(z_sb[:, s, 0:width], ps[:, 4 * s + 2, 0:width], ACT.Silu).then_inc(z_kept, 1)

                @block.vector
                def _(dve):
                    v = Chain(dve, own)

                    def tap_w(j):
                        return convw[:, j, bass.ds(g, 1)]

                    for ch, (t0, width) in enumerate(chunks):
                        s = ch % 2
                        if ch < NBAND:
                            def taps(j):
                                return p_all[:, t0 + j:t0 + j + width]

                            def shaped(x):
                                return x
                        else:
                            dve.wait_ge(prev, 16 * DB)

                            def taps(j):
                                return p_new[:, :, j:j + DT]

                            def shaped(x):
                                return x.rearrange("p (b t) -> p b t", t=DT)
                        y = shaped(y_sb[:, s, 0:width])
                        dve.wait_ge(u_kept, ch + 1)
                        v.done(nc.vector.tensor_tensor(taps(2), shaped(ps[:, 4 * s, 0:width]),
                                                       shaped(u_sb[:, s, 0:width]), ALU.mult))
                        if ch >= 2:
                            dve.wait_ge(stored[s], 16 * (ch // 2))
                        v.done(nc.vector.tensor_scalar(y, taps(0), tap_w(0), None, ALU.mult))
                        v.done(nc.vector.scalar_tensor_tensor(y, taps(1), tap_w(1), y, ALU.mult, ALU.add))
                        v.done(nc.vector.scalar_tensor_tensor(y, taps(2), tap_w(2), y, ALU.mult, ALU.add))
                        dve.wait_ge(projected, 4 * ch + 4)
                        v.done(nc.vector.tensor_tensor(y, shaped(ps[:, 4 * s + 3, 0:width]), y, ALU.mult))
                        dve.wait_ge(z_kept, ch + 1)
                        nc.vector.tensor_tensor(y, shaped(z_sb[:, s, 0:width]), y, ALU.mult).then_inc(gated, 1)

        def plain(n_groups, func, col, out):
            with m.round() as block:
                items = [(gr, n, ch) for gr in range(n_groups) for n in range(4) for ch in range(len(chunks))]

                @block.sync
                def _(sp):
                    for gr in range(n_groups):
                        sp.dma_start(wg[:, gr], win[:, :, bass.ds(col(gr), 4 * P)]).then_inc(loaded[gr], 16)
                    for j, (gr, n, ch) in enumerate(items):
                        t0, width = chunks[ch]
                        sp.wait_ge(acted, j + 1)
                        sp.dma_start(out(gr, n)[:, t0:t0 + width], out_sb[:, j % 4, 0:width]).then_inc(stored[j % 4], 16)
                    for s in range(4):
                        sp.wait_ge(stored[s], 16 * (len(items) // 4))

                @block.tensor
                def _(pe):
                    for j, (gr, n, ch) in enumerate(items):
                        if n == 0 and ch == 0:
                            pe.wait_ge(loaded[gr], 16)
                        if j >= 8:
                            pe.wait_ge(acted, j - 7)
                        for k in range(KC):
                            last = nc.tensor.matmul(ps[:, j % 8, 0:chunks[ch][1]], wg[:, gr, k, n * P:(n + 1) * P],
                                                    tokens(k, ch), start=(k == 0), stop=(k == KC - 1))
                        last.then_inc(projected, 1)

                @block.scalar
                def _(act):
                    for j, (gr, n, ch) in enumerate(items):
                        width = chunks[ch][1]
                        act.wait_ge(projected, j + 1)
                        if j >= 4:
                            act.wait_ge(stored[j % 4], 16 * (j // 4))
                        nc.scalar.activation(out_sb[:, j % 4, 0:width], ps[:, j % 8, 0:width], func).then_inc(acted, 1)

        with nc.Fori(0, DC // P) as g:
            conv(g)
        silu_out = a["silu_t"].rearrange("(n p) t -> n p t", p=P)
        gates_out = a["gates_t"].rearrange("(n p) t -> n p t", p=P)
        plain(1, ACT.Silu, lambda gr: O_AZ, lambda gr, n: silu_out[n])
        with nc.Fori(0, 2) as i:
            plain(2, ACT.Sigmoid, lambda gr: (i * 2 + gr) * 512 + O_GC, lambda gr, n: gates_out[(i * 2 + gr) * 4 + n])


def stage_merge(nc, a):
    with ExitStack() as ctx:
        m = Stage(nc, ctx, "merge")
        up_c = m.sb("up_c", [P, 4, D])
        up_a = m.sb("up_a", [P, 4, D])
        w_out = m.sb("w_out", [P, KC, D])
        gain = m.sb("gain", [P, D])
        conv = m.sb("conv", [P, 4, BAND])
        silu = m.sb("silu", [P, 4, BAND])
        attn = m.sb("attn", [P, 4, BAND])
        gates = m.sb("gates", [P, 16, BAND])
        merged = m.sb("merged", [P, KC, BAND])
        part = m.sb("part", [P, BAND])
        x = m.sb("x", [P, TPB, D])
        y = m.sb("y", [P, 2, D])
        junk = m.sb("junk", [P, D])
        st = m.sb("st", [P, 2, 8])
        ps_u = m.psum("ps_u", [P, 4, 512])
        ps_y = m.psum("ps_y", [P, 2, D])
        (weights, conv_in, attn_in, x_in, gated, upped, merged_n, out_done, added, squared, meaned,
         rooted, finished, own, own_act) = [m.sem(n) for n in (
            "weights", "conv_in", "attn_in", "x_in", "gated", "upped", "merged_n", "out_done", "added",
            "squared", "meaned", "rooted", "finished", "own", "own_act")]
        gates_in = [m.sem(f"gates_in{s}") for s in range(4)]
        stored = [m.sem(f"stored{s}") for s in range(2)]

        with m.round() as block:
            @block.sync
            def _(sp):
                sp.dma_start(up_c[:], a["w_up_conv"].rearrange("l (k p) n -> (l p) k n", p=P)).then_inc(weights, 16)
                sp.dma_start(up_a[:], a["w_up_attn"].rearrange("l (k p) n -> (l p) k n", p=P)).then_inc(weights, 16)
                sp.dma_start(w_out[:], a["w_out"].rearrange("l (k p) n -> (l p) k n", p=P)).then_inc(weights, 16)
                sp.dma_start(gain[:], a["final_gain"].rearrange("(a d) -> a d", a=1).to_broadcast([P, D])).then_inc(weights, 16)
                sp.wait_ge(weights, 64)

        def band(cols, width, x_src, y_dst):
            rows = min(width, P)
            nt = width // rows
            with m.round() as block:

                @block.sync
                def _(sp):
                    def rows_of(t):
                        return t.rearrange("(n p) t -> p n t", p=P)
                    sp.dma_start(conv[:, :, 0:width], rows_of(a["conv_t"])[:, :, cols]).then_inc(conv_in, 16)
                    sp.dma_start(silu[:, :, 0:width], rows_of(a["silu_t"])[:, :, cols]).then_inc(attn_in, 16)
                    sp.dma_start(attn[:, :, 0:width], rows_of(a["attn_t"])[:, :, cols]).then_inc(attn_in, 16)
                    for q in range(4):
                        for half in range(2):
                            n = half * KC + 2 * q
                            sp.dma_start(gates[:, n:n + 2, 0:width],
                                         rows_of(a["gates_t"])[:, n:n + 2, cols]).then_inc(gates_in[q], 16)
                    sp.dma_start(x[0:rows, 0:nt, :], x_src).then_inc(x_in, 16)
                    for t in range(nt):
                        sp.wait_ge(finished, t + 1)
                        sp.dma_start(y_dst(t), y[0:rows, t % 2, :]).then_inc(stored[t % 2], 16)
                    for s in range(min(nt, 2)):
                        sp.wait_ge(stored[s], 16 * ((nt + 1 - s) // 2))

                @block.tensor
                def _(pe):
                    pe.wait_ge(conv_in, 16)
                    for n in range(KC):
                        if n >= 2:
                            pe.wait_ge(merged_n, n - 1)
                        for k in range(4):
                            nc.tensor.matmul(ps_u[:, 2 * (n % 2), 0:width], up_c[:, k, n * P:(n + 1) * P],
                                             conv[:, k, 0:width], start=(k == 0), stop=(k == 3))
                        if n == 0:
                            pe.wait_ge(gated, 1)
                        for k in range(4):
                            last = nc.tensor.matmul(ps_u[:, 2 * (n % 2) + 1, 0:width], up_a[:, k, n * P:(n + 1) * P],
                                                    attn[:, k, 0:width], start=(k == 0), stop=(k == 3))
                        last.then_inc(upped, 1)
                    pe.wait_ge(merged_n, KC)
                    for t in range(nt):
                        if t >= 2:
                            pe.wait_ge(added, t - 1)
                        for half in range(2):
                            for k in range(KC):
                                last = nc.tensor.matmul(ps_y[0:rows, t % 2, half * 512:(half + 1) * 512],
                                                        merged[:, k, t * rows:(t + 1) * rows],
                                                        w_out[:, k, half * 512:(half + 1) * 512],
                                                        start=(k == 0), stop=(k == KC - 1))
                        last.then_inc(out_done, 1)

                @block.vector
                def _(dve):
                    v = Chain(dve, own)
                    dve.wait_ge(attn_in, 32)
                    nc.vector.tensor_tensor(attn[:, :, 0:width], attn[:, :, 0:width], silu[:, :, 0:width],
                                            ALU.mult).then_inc(gated, 1)
                    for n in range(KC):
                        dve.wait_ge(upped, n + 1)
                        dve.wait_ge(gates_in[n // 2], 32)
                        v.done(nc.vector.tensor_tensor(merged[:, n, 0:width], ps_u[:, 2 * (n % 2), 0:width],
                                                       gates[:, n, 0:width], ALU.mult))
                        v.done(nc.vector.tensor_tensor(part[:, 0:width], ps_u[:, 2 * (n % 2) + 1, 0:width],
                                                       gates[:, KC + n, 0:width], ALU.mult))
                        nc.vector.tensor_tensor(merged[:, n, 0:width], merged[:, n, 0:width], part[:, 0:width],
                                                ALU.add).then_inc(merged_n, 1)
                        dve.wait_ge(merged_n, n + 1)
                    dve.wait_ge(x_in, 16)

                    def add(t):
                        s = t % 2
                        dve.wait_ge(out_done, t + 1)
                        if t >= 2:
                            dve.wait_ge(stored[s], 16 * (t // 2))
                        nc.vector.tensor_tensor(y[0:rows, s, :], ps_y[0:rows, s, :], x[0:rows, t, :], ALU.add).then_inc(added, 1)

                    def finish(t):
                        s = t % 2
                        dve.wait_ge(squared, t + 1)
                        v.done(nc.vector.tensor_scalar(st[0:rows, s, 1:2], st[0:rows, s, 5:6], 1.0 / D, EPS,
                                                       ALU.mult, ALU.add))
                        nc.vector.tensor_copy(st[0:rows, s, 6:7], st[0:rows, s, 1:2]).then_inc(meaned, 1)
                        dve.wait_ge(rooted, t + 1)
                        refined_rstd(nc, v, st[0:rows, s, 1:2], st[0:rows, s, 4:5], st[0:rows, s, 3:4],
                                     st[0:rows, s, 2:3])
                        nc.vector.scalar_tensor_tensor(y[0:rows, s, :], y[0:rows, s, :], st[0:rows, s, 3:4],
                                                       gain[0:rows, :], ALU.mult, ALU.mult).then_inc(finished, 1)

                    for t in range(nt):
                        add(t)
                        finish(t)

                @block.scalar
                def _(act):
                    o = Chain(act, own_act)
                    for t in range(nt):
                        s = t % 2
                        act.wait_ge(added, t + 1)
                        o.done(nc.scalar.activation(junk[0:rows, :], y[0:rows, s, :], ACT.Square,
                                                    accum_out=st[0:rows, s, 0:1]))
                        nc.scalar.activation(st[0:rows, s, 5:6], st[0:rows, s, 0:1], ACT.Copy).then_inc(squared, 1)
                        act.wait_ge(meaned, t + 1)
                        nc.scalar.activation(st[0:rows, s, 2:3], st[0:rows, s, 1:2], ACT.Sqrt).then_inc(rooted, 1)

        with nc.Fori(0, NBAND) as i:
            xb = a["x_prompt"].rearrange("b (i t p) d -> (b i) p t d", p=P, t=TPB)[i]
            yb = a["y_prompt"].rearrange("b (t p) d -> (b t) p d", p=P)
            band(bass.ds(i * BAND, BAND), BAND, xb, lambda t: yb[i * TPB + t])
        band(slice(S, S + ST), ST, a["x_sample"].rearrange("b t d -> (b t) d").unsqueeze(1),
             lambda t: a["y_sample"].rearrange("b t d -> (b t) d"))


def hybrid_kernel(nc, a):
    with ExitStack() as ctx:
        def sb(name, shape):
            return ctx.enter_context(nc.sbuf_tensor(name, shape, F32))

        c = Named()
        c.ident = sb("ident", [P, P])
        c.xnT = sb("xnT", [P, KC, S])
        c.xsT = sb("xsT", [P, KC, ST])
        c.ksT = sb("ksT", [P, ST])
        c.iksT = sb("iksT", [P, ST])
        c.vs = sb("vs", [ST, P])
        c.iws = sb("iws", [ST, NI])
        with ExitStack() as prompt:
            def of_prompt(name, shape):
                return prompt.enter_context(nc.sbuf_tensor(name, shape, F32))

            c.keypos = of_prompt("keypos", [P, S])
            c.tilepos = of_prompt("tilepos", [P, NT])
            c.kT = of_prompt("kT", [P, S])
            c.ikT = of_prompt("ikT", [P, S])
            c.v = of_prompt("v", [P, NT * P])
            c.iw = of_prompt("iw", [P, NT * NI])
            stage_constants(nc, c)
            stage_norm(nc, c, a)
            stage_prompt_attention(nc, c, a)
        stage_sample_attention(nc, c, a)
        stage_gates(nc, c, a)
    stage_merge(nc, a)


INPUTS = ["x_prompt", "x_sample", "cache_k", "cache_v", "cache_kidx", "state_conv", "page_table",
          "norm_gain", "w_in", "conv_w", "w_up_conv", "w_up_attn", "w_out", "final_gain"]
OUTPUTS = {
    "y_prompt": (1, S, D), "y_sample": (DB, DT, D),
    "new_k_prompt": (1, 1, S, NKV, HD), "new_v_prompt": (1, 1, S, NKV, HD),
    "new_kidx_prompt": (1, 1, S, ID), "new_conv_prompt": (1, 1, 2, DC),
    "new_k_sample": (1, DB, DT, NKV, HD), "new_v_sample": (1, DB, DT, NKV, HD),
    "new_kidx_sample": (1, DB, DT, ID), "new_conv_sample": (1, DB, 2, DC),
}


def kernel(**inputs):
    import numpy as np
    import concourse.bacc as bacc
    from concourse.bass_utils import run_bass_kernel_spmd

    nc = bacc.Bacc("TRN2", target_bir_lowering=False, num_devices=1)
    dram, arrays = {}, {}
    for name in INPUTS:
        x = np.ascontiguousarray(inputs[name])
        arrays[f"in_{name}"] = x
        dram[name] = nc.dram_tensor(f"in_{name}", x.shape, mybir.dt.from_np(x.dtype), kind="ExternalInput").ap()
    for name, shape in OUTPUTS.items():
        dram[name] = nc.dram_tensor(f"out_{name}", shape, F32, kind="ExternalOutput").ap()
    for name, rows in (("attn_t", DC), ("conv_t", DC), ("silu_t", DC), ("gates_t", 2 * D)):
        dram[name] = nc.dram_tensor(name, (rows, S + ST), F32).ap()
    dram["iw_scratch"] = nc.dram_tensor("iw_scratch", (DB, NI, DT), F32).ap()
    hybrid_kernel(nc, dram)
    r = run_bass_kernel_spmd(nc, [arrays], core_ids=[0])
    return tuple(r.results[0][f"out_{name}"] for name in OUTPUTS)
```

```python
from contextlib import ExitStack, contextmanager

import concourse.bass as bass
from concourse import mybir

F32 = mybir.dt.float32
I32 = mybir.dt.int32
ALU = mybir.AluOpType
ACT = mybir.ActivationFunctionType
AX_X = mybir.AxisListType.X

D = 1024
S = 2048
DB, DT = 8, 8
ST = DB * DT
DC = 512
NH, HD, NKV = 8, 64, 2
G = NH // NKV
NI, ID = 8, 64
PAGE, NPAGE = 128, 32
PAST = PAGE * NPAGE
TOPK = 256
EPS = 1e-6
P = 128
KC = D // P
NT = S // P
BAND = 512
NBAND = S // BAND
TPB = BAND // P
BIG = 1.0e33
MASKED = -1.0e30
TAKEN = -3.0e38
SLOPES = [2.0 ** (-8.0 * (h + 1) / NH) for h in range(NH)]
ISCALE = float(NI) ** -0.5
QSCALE = float(HD) ** -0.5

O_B, O_C, O_U, O_Z, O_Q, O_K, O_V, O_AZ, O_IQ, O_IK, O_IW, O_GC, O_GA = (
    0, 512, 1024, 1536, 2048, 2560, 2688, 2816, 3328, 3840, 3904, 3912, 4936)
KVW = 2 * NKV * HD
IKW = ID + NI


class Named:
    pass


class Chain:

    def __init__(self, eng, sem):
        self.eng, self.sem, self.n = eng, sem, 0

    def done(self, ins):
        ins.then_inc(self.sem, 1)
        self.n += 1
        self.eng.wait_ge(self.sem, self.n)


class Stage:

    def __init__(self, nc, ctx, name):
        self.nc, self.ctx, self.name, self.sems = nc, ctx, name, []

    def sb(self, name, shape, dt=F32):
        return self.ctx.enter_context(self.nc.sbuf_tensor(f"{self.name}_{name}", shape, dt))

    def psum(self, name, shape):
        return self.ctx.enter_context(self.nc.psum_tensor(f"{self.name}_{name}", shape, F32))

    def sem(self, name):
        self.sems.append(self.ctx.enter_context(self.nc.semaphore(f"{self.name}_{name}")))
        return self.sems[-1]

    @contextmanager
    def round(self):
        with self.nc.Block() as block:
            yield block
        for s in self.sems:
            self.nc.gpsimd.sem_clear(s)
        self.nc.all_engine_barrier()


def refined_rstd(nc, v, ms, tmp, rstd, std):
    v.done(nc.vector.reciprocal(rstd, std))
    v.done(nc.vector.tensor_tensor(tmp, rstd, rstd, ALU.mult))
    v.done(nc.vector.tensor_tensor(tmp, tmp, ms, ALU.mult))
    v.done(nc.vector.tensor_scalar(tmp, tmp, -0.5, 1.5, ALU.mult, ALU.add))
    v.done(nc.vector.tensor_tensor(rstd, rstd, tmp, ALU.mult))


def stage_constants(nc, c):
    with ExitStack() as ctx:
        m = Stage(nc, ctx, "const")
        iotas, cleared, made = m.sem("iotas"), m.sem("cleared"), m.sem("made")
        keys, tiles = m.sb("keys", [P, S], I32), m.sb("tiles", [P, NT], I32)
        with m.round() as block:

            @block.gpsimd
            def _(pool):
                nc.gpsimd.memset(c.ident[:], 0.0).then_inc(cleared, 1)
                nc.gpsimd.iota(keys[:], [[1, S]], base=0, channel_multiplier=-1).then_inc(iotas, 1)
                nc.gpsimd.iota(tiles[:], [[P, NT]], base=0, channel_multiplier=0).then_inc(iotas, 1)
                pool.wait_ge(cleared, 1)
                nc.gpsimd.affine_select(out=c.ident[:], in_=c.ident[:], compare_op=ALU.not_equal, fill=1.0,
                                        base=0, pattern=[[-1, P]], channel_multiplier=1).then_inc(made, 1)

            @block.vector
            def _(dve):
                dve.wait_ge(iotas, 2)
                nc.vector.tensor_copy(c.keypos[:], keys[:]).then_inc(made, 1)
                nc.vector.tensor_copy(c.tilepos[:], tiles[:]).then_inc(made, 1)


def stage_norm(nc, c, a):
    with ExitStack() as ctx:
        m = Stage(nc, ctx, "norm")
        gain = m.sb("gain", [P, D])
        wkv = m.sb("wkv", [P, KC, KVW])
        wik = m.sb("wik", [P, KC, IKW])
        x_in = m.sb("x_in", [P, 2, D])
        xn = m.sb("xn", [P, 2, D])
        junk = m.sb("junk", [P, D])
        xt = m.sb("xt", [P, 2, KC, P])
        kv = m.sb("kv", [P, 2, KVW])
        ik = m.sb("ik", [P, 2, 2, ID])
        st = m.sb("st", [P, 2, 8])
        ps_t = m.psum("ps_t", [P, KC, P])
        ps_kv = m.psum("ps_kv", [P, 512])
        ps_kt = m.psum("ps_kt", [P, 4, P])
        (weights, squared, meaned, rooted, normed, turned, staged, kept, projected, evacuated,
         k_turned, k_kept, own) = [m.sem(n) for n in (
            "weights", "squared", "meaned", "rooted", "normed", "turned", "staged", "kept",
            "projected", "evacuated", "k_turned", "k_kept", "own")]
        own_act = m.sem("own_act")
        x_ready = [m.sem(f"x_ready{s}") for s in range(2)]
        stored = [m.sem(f"stored{s}") for s in range(2)]
        x_tiles = a["x_prompt"].rearrange("b (t p) d -> (b t) p d", p=P)
        win = a["w_in"].rearrange("l (k p) n -> (l p) k n", p=P)
        k_out = a["new_k_prompt"].rearrange("l b (t p) h d -> (l b t) p (h d)", p=P)
        v_out = a["new_v_prompt"].rearrange("l b (t p) h d -> (l b t) p (h d)", p=P)
        i_out = a["new_kidx_prompt"].rearrange("l b (t p) d -> (l b t) p d", p=P)

        with m.round() as block:
            @block.sync
            def _(sp):
                sp.dma_start(gain[:], a["norm_gain"][0:1, :].to_broadcast([P, D])).then_inc(weights, 16)
                sp.dma_start(wkv[:], win[:, :, O_K:O_K + KVW]).then_inc(weights, 16)
                sp.dma_start(wik[:], win[:, :, O_IK:O_IK + IKW]).then_inc(weights, 16)
                sp.wait_ge(weights, 48)

        def tiles(n, rows, dram, dst):
            with m.round() as block:

                @block.sync
                def _(sp):
                    def load(t):
                        if t >= 2:
                            sp.wait_ge(normed, t - 1)
                        sp.dma_start(x_in[0:rows, t % 2, :], dram(t)[0]).then_inc(x_ready[t % 2], 16)

                    for t in range(min(n, 2)):
                        load(t)
                    for t in range(n):
                        s = t % 2
                        sp.wait_ge(evacuated, t + 1)
                        _, ko, vo, io = dram(t)
                        sp.dma_start(ko, kv[0:rows, s, 0:P]).then_inc(stored[s], 16)
                        sp.dma_start(vo, kv[0:rows, s, P:2 * P]).then_inc(stored[s], 16)
                        sp.dma_start(io, ik[0:rows, s, 0, :]).then_inc(stored[s], 16)
                        if t + 2 < n:
                            load(t + 2)
                    for s in range(min(n, 2)):
                        sp.wait_ge(stored[s], 48 * ((n + 1 - s) // 2))

                @block.scalar
                def _(act):
                    o = Chain(act, own_act)
                    def root(t):
                        s = t % 2
                        act.wait_ge(x_ready[s], 16 * (t // 2 + 1))
                        if t >= 2:
                            act.wait_ge(normed, t - 1)
                        o.done(nc.scalar.activation(junk[0:rows, :], x_in[0:rows, s, :], ACT.Square,
                                                    accum_out=st[0:rows, s, 0:1]))
                        nc.scalar.activation(st[0:rows, s, 5:6], st[0:rows, s, 0:1], ACT.Copy).then_inc(squared, 1)
                        act.wait_ge(meaned, t + 1)
                        nc.scalar.activation(st[0:rows, s, 2:3], st[0:rows, s, 1:2], ACT.Sqrt).then_inc(rooted, 1)

                    def keep(t):
                        xd, kd, ikd, _, _ = dst(t)
                        act.wait_ge(staged, t + 1)
                        nc.scalar.activation(xd, ps_t[:, :, 0:rows], ACT.Copy).then_inc(kept, 1)
                        act.wait_ge(k_turned, t + 1)
                        nc.scalar.activation(kd, ps_kt[:, 0, 0:rows], ACT.Copy)
                        nc.scalar.activation(ikd, ps_kt[:, 1, 0:rows], ACT.Copy).then_inc(k_kept, 1)

                    for t in range(n + 1):
                        if t < n:
                            root(t)
                        if t >= 1:
                            keep(t - 1)

                @block.vector
                def _(dve):
                    v = Chain(dve, own)

                    def norm(t):
                        s = t % 2
                        dve.wait_ge(squared, t + 1)
                        if t >= 2:
                            dve.wait_ge(turned, t - 1)
                        v.done(nc.vector.tensor_scalar(st[0:rows, s, 1:2], st[0:rows, s, 5:6], 1.0 / D, EPS,
                                                       ALU.mult, ALU.add))
                        nc.vector.tensor_copy(st[0:rows, s, 6:7], st[0:rows, s, 1:2]).then_inc(meaned, 1)
                        dve.wait_ge(rooted, t + 1)
                        refined_rstd(nc, v, st[0:rows, s, 1:2], st[0:rows, s, 4:5], st[0:rows, s, 3:4],
                                     st[0:rows, s, 2:3])
                        nc.vector.scalar_tensor_tensor(xn[0:rows, s, :], x_in[0:rows, s, :], st[0:rows, s, 3:4],
                                                       gain[0:rows, :], ALU.mult, ALU.mult).then_inc(normed, 1)

                    def evacuate(t):
                        s = t % 2
                        _, _, _, vd, iwd = dst(t)
                        dve.wait_ge(turned, t + 1)
                        if t >= 2:
                            dve.wait_ge(projected, t - 1)
                        nc.vector.tensor_copy(xt[:, s, :, 0:rows], ps_t[:, :, 0:rows]).then_inc(staged, 1)
                        dve.wait_ge(projected, t + 1)
                        if t >= 2:
                            dve.wait_ge(stored[s], 48 * (t // 2))
                            dve.wait_ge(k_turned, t - 1)
                        nc.vector.tensor_copy(kv[0:rows, s, :], ps_kv[0:rows, 0:KVW])
                        nc.vector.tensor_copy(vd, ps_kv[0:rows, P:2 * P])
                        nc.vector.tensor_scalar(iwd, ps_kv[0:rows, KVW + ID:KVW + IKW], ISCALE, None, ALU.mult)
                        nc.vector.tensor_copy(ik[0:rows, s, 0, :], ps_kv[0:rows, KVW:KVW + ID])
                        nc.vector.tensor_copy(ik[0:rows, s, 1, :], ps_kv[0:rows, KVW:KVW + ID]).then_inc(evacuated, 1)

                    for t in range(n + 1):
                        if t < n:
                            norm(t)
                        if t >= 1:
                            evacuate(t - 1)

                @block.tensor
                def _(pe):
                    for t in range(n):
                        s = t % 2
                        pe.wait_ge(normed, t + 1)
                        if t >= 1:
                            pe.wait_ge(kept, t)
                        for k in range(KC):
                            last = nc.tensor.transpose(ps_t[:, k, 0:rows], xn[0:rows, s, k * P:(k + 1) * P],
                                                       c.ident[0:rows, 0:rows])
                        last.then_inc(turned, 1)
                        pe.wait_ge(staged, t + 1)
                        if t >= 1:
                            pe.wait_ge(evacuated, t)
                        for k in range(KC):
                            nc.tensor.matmul(ps_kv[0:rows, 0:KVW], xt[:, s, k, 0:rows], wkv[:, k, :],
                                             start=(k == 0), stop=(k == KC - 1))
                        for k in range(KC):
                            last = nc.tensor.matmul(ps_kv[0:rows, KVW:KVW + IKW], xt[:, s, k, 0:rows],
                                                    wik[:, k, :], start=(k == 0), stop=(k == KC - 1))
                        last.then_inc(projected, 1)
                        pe.wait_ge(evacuated, t + 1)
                        if t >= 1:
                            pe.wait_ge(k_kept, t)
                        nc.tensor.transpose(ps_kt[:, 0, 0:rows], kv[0:rows, s, 0:P], c.ident[0:rows, 0:rows])
                        nc.tensor.transpose(ps_kt[:, 1, 0:rows], ik[0:rows, s, :, :].rearrange("p a d -> p (a d)"),
                                            c.ident[0:rows, 0:rows]).then_inc(k_turned, 1)

        with nc.Fori(0, NBAND) as i:
            def dram(t):
                u = i * TPB + t
                return x_tiles[u], k_out[u], v_out[u], i_out[u]

            def dst(t):
                u = i * TPB + t
                return (c.xnT[:, :, bass.ds(u * P, P)], c.kT[:, bass.ds(u * P, P)], c.ikT[:, bass.ds(u * P, P)],
                        c.v[:, bass.ds(u * P, P)], c.iw[:, bass.ds(u * NI, NI)])
            tiles(TPB, P, dram, dst)

        def sample_dram(t):
            return (a["x_sample"].rearrange("b t d -> (b t) d"), a["new_k_sample"].rearrange("l b t h d -> (l b t) (h d)"),
                    a["new_v_sample"].rearrange("l b t h d -> (l b t) (h d)"),
                    a["new_kidx_sample"].rearrange("l b t d -> (l b t) d"))
        tiles(1, ST, sample_dram, lambda t: (c.xsT[:], c.ksT[:], c.iksT[:], c.vs[:], c.iws[:]))


GROUPS = [O_B, O_C, O_U, O_Z, O_AZ, O_GC, O_GC + 512, O_GA, O_GA + 512]
R_B, R_C, R_U, R_Z, R_AZ, R_GC, R_GA = 0, 1, 2, 3, 4, 5, 7
LEAD = 2
BESIDE = [[0], [1, 2], [3, 4, 5], [6, 7, 8]]


def stage_prompt_attention(nc, c, a):
    with ExitStack() as ctx:
        m = Stage(nc, ctx, "attn")
        qT = m.sb("qT", [P, 2, 4, BAND])
        q_idx = m.sb("q_idx", [P, 4, P])
        q_att = m.sb("q_att", [P, G, P])
        work = m.sb("work", [P, 2 * S])
        acc = work[:, 0:S]
        relu = work[:, S:2 * S].rearrange("p (n k) -> p n k", k=512)
        bias_h = relu
        prob = m.sb("prob", [P, 2, S])
        bias = m.sb("bias", [P, S])
        w_q = [x.rearrange("p (k n) -> p k n", k=KC) for x in (work[:], prob[:].rearrange("p s k -> p (s k)"))]
        probT = m.sb("probT", [P, 2, 4, P])
        later = m.sb("later", [P, BAND])
        att = m.sb("att", [P, NH * HD])
        attT = m.sb("attT", [P, 4, P])
        w_rest = m.sb("w_rest", [P, 2, KC, P])
        rest = m.sb("rest", [P, 3, 512])
        iw = m.sb("iw", [P, NI])
        first = m.sb("first", [P, 1])
        best = m.sb("best", [P, 8])
        chunk_max = m.sb("chunk_max", [P, 4])
        negmax = m.sb("negmax", [P, NH])
        rowsum = m.sb("rowsum", [P, NH])
        ps_s = m.psum("ps_s", [P, 3, 512])
        ps_p = m.psum("ps_p", [P, 2, 4, P])
        ps_o = m.psum("ps_o", [P, NH * HD])
        ps_r = m.psum("ps_r", [P, 2, 512])
        (loaded, projected, kept, q_staged, next_staged, scored, rectified, summed, scaled,
         multiplied, biased, maxed, exped, turned, turned_kept, weighted, normalised, att_turned,
         att_kept, stored, rest_done, rest_kept, own) = [m.sem(n) for n in (
            "loaded", "projected", "kept", "q_staged", "next_staged", "scored", "rectified", "summed",
            "scaled", "multiplied", "biased", "maxed", "exped", "turned", "turned_kept",
            "weighted", "normalised", "att_turned", "att_kept", "stored", "rest_done", "rest_kept", "own")]
        w_in = [m.sem(f"w_in{s}") for s in range(2)]
        rest_stored = [m.sem(f"rest_stored{s}") for s in range(3)]
        win = a["w_in"].rearrange("l (k p) n -> (l p) k n", p=P)
        attn_out = a["attn_t"].rearrange("(n p) t -> p n t", p=P)
        rest_out = a["rest_t"].rearrange("(g n p) t -> g n p t", n=4, p=P)
        chunks = [(ch * 512, 512) for ch in range(NBAND)] + [(S, ST)]
        NCH = len(chunks)

        def project(b):
            with m.round() as block:
                @block.sync
                def _(sp):
                    for j, col in enumerate((O_IQ, O_Q)):
                        sp.dma_start(w_q[j], win[:, :, col:col + NH * HD]).then_inc(w_in[j], 16)
                    if b == 0:
                        sp.wait_ge(kept, 1)
                        for g in (R_C, R_U):
                            sp.dma_start(rest_out[g].rearrange("n p t -> p n t")[:, :, 0:LEAD],
                                         later[:, 0:4 * LEAD].rearrange("p (n t) -> p n t", t=LEAD)
                                         ).then_inc(stored, 16)
                        sp.wait_ge(stored, 32)
                    for j in range(2):
                        sp.wait_ge(w_in[j], 16)

                @block.tensor
                def _(pe):
                    for g in range(8):
                        if g % 4 == 0:
                            pe.wait_ge(w_in[g // 4], 16)
                        if g >= 2:
                            pe.wait_ge(projected, g - 1)
                        for k in range(KC):
                            last = nc.tensor.matmul(ps_r[:, g % 2, :], w_q[g // 4][:, k, (g % 4) * P:(g % 4 + 1) * P],
                                                    c.xnT[:, k, b * BAND:(b + 1) * BAND],
                                                    start=(k == 0), stop=(k == KC - 1))
                        last.then_inc(loaded, 1)

                @block.scalar
                def _(act):
                    for g in range(8):
                        act.wait_ge(loaded, g + 1)
                        nc.scalar.activation(qT[:, g // 4, g % 4, :], ps_r[:, g % 2, :], ACT.Copy,
                                             scale=1.0 if g < 4 else QSCALE).then_inc(projected, 1)

                @block.vector
                def _(dve):
                    if b == 0:
                        nc.vector.memset(later[:, 0:4 * LEAD], 0.0).then_inc(kept, 1)

        def tile(b, i, before):
            now = 0 if b is None else b + 1
            L = now * 512
            LB = before * 512
            T = NT if b is None else i + b * TPB
            groups = [] if b is None else BESIDE[b]
            items = [(j, ch) for j in range(len(groups)) for ch in range(NCH)]
            N = NH * before

            def beside(h):
                return range(len(items) * h // NH, len(items) * (h + 1) // NH)

            with m.round() as block:

                @block.sync
                def _(sp):
                    def load(j):
                        sp.dma_start(w_rest[:, j % 2], win[:, :, bass.ds(i * P + GROUPS[groups[j]], P)]
                                     ).then_inc(w_in[j % 2], 16)

                    for j in range(min(2, len(groups))):
                        load(j)
                    for g, (j, ch) in enumerate(items):
                        t0, width = chunks[ch]
                        sp.wait_ge(rest_kept, g + 1)
                        sp.dma_start(rest_out[groups[j]][i][:, LEAD + t0:LEAD + t0 + width],
                                     rest[:, g % 3, 0:width]).then_inc(rest_stored[g % 3], 16)
                        if ch == NCH - 1 and j + 2 < len(groups):
                            load(j + 2)
                    if before:
                        sp.wait_ge(att_kept, 1)
                        sp.dma_start(attn_out[:, :, bass.ds((T - 1) * P, P)], attT[:]).then_inc(stored, 16)
                        sp.wait_ge(stored, 16)
                    for s in range(min(3, len(items))):
                        sp.wait_ge(rest_stored[s], 16 * ((len(items) + 2 - s) // 3))

                @block.scalar
                def _(act):
                    def stage_query():
                        rows = bass.ds(i * P, P)
                        for hh in range(2):
                            for kv in range(2):
                                nc.scalar.activation(q_att[kv * 64:kv * 64 + 64, hh::2, :],
                                                     qT[hh * 64:hh * 64 + 64, 1, 2 * kv:2 * kv + 2, rows],
                                                     ACT.Copy).then_inc(next_staged, 1)

                    if now:
                        nc.scalar.activation(q_idx[:], qT[:, 0, :, bass.ds(i * P, P)], ACT.Copy).then_inc(q_staged, 1)
                    for g in range(NI * now):
                        act.wait_ge(scored, g + 1)
                        if g >= 4:
                            act.wait_ge(summed, g - 3)
                        nc.scalar.activation(relu[:, g % 4, :], ps_s[:, g % 3, :], ACT.Relu).then_inc(rectified, 1)

                    def scale(h):
                        for ch in range(before):
                            j = h * before + ch
                            if j >= 4:
                                act.wait_ge(biased, j - 3)
                            nc.scalar.activation(bias_h[:, j % 4, :], bias[:, ch * 512:(ch + 1) * 512], ACT.Copy,
                                                 scale=SLOPES[h]).then_inc(scaled, 1)

                    def keep_rest(g):
                        width = chunks[items[g][1]][1]
                        act.wait_ge(rest_done, g + 1)
                        if g >= 3:
                            act.wait_ge(rest_stored[g % 3], 16 * (g // 3))
                        nc.scalar.activation(rest[:, g % 3, 0:width], ps_r[:, g % 2, 0:width], ACT.Copy
                                             ).then_inc(rest_kept, 1)

                    if before:
                        if now:
                            act.wait_ge(summed, NI * now)
                        scale(0)
                    for h in range(NH):
                        if before and h + 1 < NH:
                            scale(h + 1)
                        for g in beside(h):
                            keep_rest(g)
                        if not before:
                            continue
                        act.wait_ge(maxed, h + 1)
                        nc.scalar.activation(prob[:, h % 2, 0:LB], prob[:, h % 2, 0:LB], ACT.Exp,
                                             bias=negmax[:, h:h + 1], accum_out=rowsum[:, h:h + 1]).then_inc(exped, 1)
                        for ch in range(before):
                            j = h * before + ch
                            act.wait_ge(turned, j + 1)
                            if j >= 2:
                                act.wait_ge(weighted, j - 1)
                            nc.scalar.activation(probT[:, j % 2], ps_p[:, j % 2], ACT.Copy).then_inc(turned_kept, 1)
                    if now:
                        if before:
                            act.wait_ge(multiplied, N)
                        stage_query()
                    if before:
                        act.wait_ge(att_turned, 1)
                        nc.scalar.activation(attT[:], ps_p[:, 0], ACT.Copy).then_inc(att_kept, 1)

                @block.vector
                def _(dve):
                    v = Chain(dve, own)
                    diag = slice(L - BAND, L)
                    if now:
                        v.done(nc.vector.tensor_copy(first[:], c.tilepos[:, bass.ds(T, 1)]))
                        v.done(nc.vector.tensor_copy(iw[:], c.iw[:, bass.ds(T * NI, NI)]))
                        v.done(nc.vector.tensor_scalar(later[:], c.keypos[:, diag], first[:], 0.0,
                                                       ALU.subtract, ALU.is_gt))
                        v.done(nc.vector.tensor_scalar(later[:], later[:], MASKED, None, ALU.mult))
                    for ch in range(now):
                        out = acc[:, ch * 512:(ch + 1) * 512]
                        for h in range(NI):
                            g = ch * NI + h
                            dve.wait_ge(rectified, g + 1)
                            if g:
                                dve.wait_ge(summed, g)
                            if h == 0 and ch < b:
                                ins = nc.vector.tensor_scalar(out, relu[:, g % 4, :], iw[:, 0:1], None, ALU.mult)
                            else:
                                ins = nc.vector.scalar_tensor_tensor(out, relu[:, g % 4, :], iw[:, h:h + 1],
                                                                     later[:] if h == 0 else out, ALU.mult, ALU.add)
                            ins.then_inc(summed, 1)
                    if now:
                        dve.wait_ge(summed, NI * now)

                    def bias_head(h):
                        if h >= 2:
                            dve.wait_ge(turned, (h - 1) * before)
                        for ch in range(before):
                            j = h * before + ch
                            dve.wait_ge(multiplied, j + 1)
                            dve.wait_ge(scaled, j + 1)
                            nc.vector.tensor_tensor_reduce(
                                out=prob[:, h % 2, ch * 512:(ch + 1) * 512], in0=ps_s[:, j % 3, :],
                                in1=bias_h[:, j % 4, :], scale=1.0, scalar=-3.0e38, op0=ALU.add, op1=ALU.max,
                                accum_out=chunk_max[:, ch:ch + 1]).then_inc(biased, 1)
                        dve.wait_ge(biased, (h + 1) * before)
                        v.done(nc.vector.reduce_max(negmax[:, h:h + 1], chunk_max[:, 0:before], AX_X))
                        nc.vector.tensor_scalar(negmax[:, h:h + 1], negmax[:, h:h + 1], -1.0, None,
                                                ALU.mult).then_inc(maxed, 1)

                    for h in range(NH):
                        if before:
                            bias_head(h)
                        if now:
                            for _ in range(TOPK // 8 // NH):
                                v.done(nc.vector.max(best[:], acc[:, 0:L]))
                                v.done(nc.vector.match_replace(acc[:, 0:L], best[:], acc[:, 0:L], TAKEN))
                    if now:
                        if before:
                            dve.wait_ge(scaled, N)
                        v.done(nc.vector.tensor_scalar(bias[:, 0:L], acc[:, 0:L], TAKEN, -BIG, ALU.not_equal, ALU.mult))
                        v.done(nc.vector.scalar_tensor_tensor(bias[:, 0:L], c.keypos[:, 0:L], first[:], bias[:, 0:L],
                                                              ALU.subtract, ALU.add))
                        v.done(nc.vector.scalar_tensor_tensor(bias[:, diag], later[:], BIG / -MASKED, bias[:, diag],
                                                              ALU.mult, ALU.add))
                    if before:
                        dve.wait_ge(exped, NH)
                        v.done(nc.vector.reciprocal(rowsum[:], rowsum[:]))
                        dve.wait_ge(weighted, N)
                        nc.vector.tensor_tensor(att[:].rearrange("p (h d) -> p h d", d=HD),
                                                ps_o[:].rearrange("p (h d) -> p h d", d=HD),
                                                rowsum[:].unsqueeze(2).to_broadcast([P, NH, HD]),
                                                ALU.mult).then_inc(normalised, 1)

                @block.tensor
                def _(pe):
                    if now:
                        pe.wait_ge(q_staged, 1)
                    for ch in range(now):
                        for h in range(NI):
                            g = ch * NI + h
                            half = slice(h % 2 * 64, h % 2 * 64 + 64)
                            if g >= 3:
                                pe.wait_ge(rectified, g - 2)
                            nc.tensor.matmul(ps_s[:, g % 3, :], q_idx[half, h // 2, :],
                                             c.ikT[half, ch * 512:(ch + 1) * 512],
                                             start=True, stop=True).then_inc(scored, 1)

                    def scores(h):
                        half = slice(h // G * 64, h // G * 64 + 64)
                        for ch in range(before):
                            j = h * before + ch
                            if j >= 3:
                                pe.wait_ge(biased, j - 2)
                            nc.tensor.matmul(ps_s[:, j % 3, :], q_att[half, h % G, :],
                                             c.kT[half, ch * 512:(ch + 1) * 512],
                                             start=True, stop=True).then_inc(multiplied, 1)

                    def project_rest(g):
                        j, ch = items[g]
                        if ch == 0:
                            pe.wait_ge(w_in[j % 2], 16 * (j // 2 + 1))
                        if g >= 2:
                            pe.wait_ge(rest_kept, g - 1)
                        for k in range(KC):
                            x = c.xnT[:, k, ch * 512:(ch + 1) * 512] if ch < NBAND else c.xsT[:, k, :]
                            last = nc.tensor.matmul(ps_r[:, g % 2, 0:chunks[ch][1]], w_rest[:, j % 2, k, :], x,
                                                    start=(k == 0), stop=(k == KC - 1))
                        last.then_inc(rest_done, 1)

                    def transpose(h, ch):
                        j = h * before + ch
                        if j >= 2:
                            pe.wait_ge(turned_kept, j - 1)
                        for u in range(4):
                            last = nc.tensor.transpose(ps_p[:, j % 2, u, :],
                                                       prob[:, h % 2, ch * 512 + u * P:ch * 512 + (u + 1) * P],
                                                       c.ident[:])
                        last.then_inc(turned, 1)

                    def weigh(h, ch):
                        j = h * before + ch
                        kv = h // G
                        pe.wait_ge(turned_kept, j + 1)
                        for u in range(4):
                            t = ch * 4 + u
                            last = nc.tensor.matmul(ps_o[:, h * HD:(h + 1) * HD], probT[:, j % 2, u, :],
                                                    c.v[:, t * P + kv * HD:t * P + (kv + 1) * HD],
                                                    start=(t == 0), stop=(t == 4 * before - 1))
                        last.then_inc(weighted, 1)

                    if before:
                        if now:
                            pe.wait_ge(rectified, NI * now)
                        scores(0)
                    for h in range(NH):
                        if before and h + 1 < NH:
                            scores(h + 1)
                        for g in beside(h):
                            project_rest(g)
                        if not before:
                            continue
                        pe.wait_ge(exped, h + 1)
                        transpose(h, 0)
                        for ch in range(before):
                            if ch + 1 < before:
                                transpose(h, ch + 1)
                            weigh(h, ch)
                    if before:
                        pe.wait_ge(normalised, 1)
                        pe.wait_ge(turned_kept, N)
                        for n in range(4):
                            last = nc.tensor.transpose(ps_p[:, 0, n, :], att[:, n * P:(n + 1) * P], c.ident[:])
                        last.then_inc(att_turned, 1)

        for b in range(NBAND):
            project(b)
            tile(b, 0, b)
            with nc.Fori(1, TPB) as i:
                tile(b, i, b + 1)
        tile(None, 0, NBAND)


KEYS = PAST + ST
QT = 4
TPR = PAGE // QT


def stage_sample_attention(nc, c, a):
    with ExitStack() as ctx:
        m = Stage(nc, ctx, "samp")
        k = Named()
        k.rows = m.sb("rows", [P, DB], I32)
        k.table = m.sb("table", [P, DB], I32)
        k.ints = m.sb("ints", [P, 16], I32)
        k.step8 = m.sb("step8", [P, NH], F32)
        k.low = m.sb("low", [P, 2], F32)
        k.same_t = m.sb("same_t", [P, DT])
        k.same_b = m.sb("same_b", [P, DB])
        k.later = m.sb("later", [ST, ST])
        k.newpos = m.sb("newpos", [ST, ST])
        k.slopes = m.sb("slopes", [ST, NH, DT])
        k.sel = m.sb("sel", [P, DB, ST])
        k.spread = m.sb("spread", [ST, DB, NH * DT])
        k.iq_bd = m.sb("iq_bd", [P, DB, P])
        k.q_bd = m.sb("q_bd", [P, DB, NH * DT])
        k.iw_rows = m.sb("iw_rows", [P, DB])
        k.bias = m.sb("bias", [ST, KEYS])
        k.attT = m.sb("attT", [HD, NH, ST])
        sample_scores(nc, c, a, k)
        sample_attend(nc, c, a, k)


def sample_scores(nc, c, a, o):
    (rows, table, ints, step8, low, same_t, same_b, later, newpos, slopes) = (
        o.rows, o.table, o.ints, o.step8, o.low, o.same_t, o.same_b, o.later, o.newpos, o.slopes)
    sel, spread, iq_bd, q_bd, iw_rows, bias = o.sel, o.spread, o.iq_bd, o.q_bd, o.iw_rows, o.bias
    with ExitStack() as ctx:
        m = Stage(nc, ctx, "sidx")
        kidx = m.sb("kidx", [P, DB, TPR * ID])
        with ExitStack() as inner:
            w = Stage(nc, inner, "sprj")
            wq = w.sb("wq", [P, 2, KC, NH * HD])
            qs = w.sb("qs", [P, 2, 4, ST])
            ps = w.psum("ps", [P, 8, ST])
            (tabled, loaded, stored, spread_in, ready, rowed, gathered, projected, kept, own) = [w.sem(n) for n in (
                "tabled", "loaded", "stored", "spread_in", "ready", "rowed", "gathered", "projected", "kept", "own")]
            win = a["w_in"].rearrange("l (k p) n -> (l p) k n", p=P)
            with w.round() as block:

                @block.sync
                def _(sp):
                    for q in range(QT):
                        sp.dma_start(table[q::QT, :], a["page_table"].rearrange("b j -> j b"),
                                     allow_slow_non_contiguous=True).then_inc(tabled, 16)
                    for b in range(DB):
                        sp.dma_start(a["iw_scratch"][b].rearrange("h t -> t h"), c.iws[b * DT:(b + 1) * DT, :],
                                     allow_slow_non_contiguous=True).then_inc(stored, 16)
                    for j, col in enumerate((O_IQ, O_Q)):
                        sp.dma_start(wq[:, j], win[:, :, col:col + NH * HD]).then_inc(loaded, 16)
                    sp.wait_ge(stored, 16 * DB)
                    for half in range(2):
                        sp.dma_start(iw_rows[half * 64:half * 64 + 64, :], a["iw_scratch"].rearrange("b h t -> (h t) b"),
                                     allow_slow_non_contiguous=True).then_inc(spread_in, 16)
                    sp.wait_ge(spread_in, 32)

                @block.gpsimd
                def _(pool):
                    nc.gpsimd.iota(ints[:, 0:1], [[0, 1]], base=0, channel_multiplier=1).then_inc(ready, 1)
                    nc.gpsimd.iota(ints[:, 8:16], [[1, 8]], base=0, channel_multiplier=0).then_inc(ready, 1)
                    nc.gpsimd.memset(iq_bd[:], 0.0).then_inc(ready, 1)
                    nc.gpsimd.memset(q_bd[:], 0.0).then_inc(ready, 1)
                    nc.gpsimd.memset(sel[:], 0.0).then_inc(ready, 1)
                    nc.gpsimd.memset(later[:], 0.0).then_inc(ready, 1)
                    pool.wait_ge(ready, 6)
                    nc.gpsimd.affine_select(out=later[:], in_=later[:], compare_op=ALU.is_ge, fill=MASKED, base=0,
                                            pattern=[[-1, ST]], channel_multiplier=1).then_inc(ready, 1)
                    pool.wait_ge(ready, 7)
                    v = later[:].rearrange("p (b t) -> p b t", t=DT)
                    nc.gpsimd.affine_select(out=v, in_=v, compare_op=ALU.is_ge, fill=MASKED, base=DT - 1,
                                            pattern=[[DT, DB], [0, DT]], channel_multiplier=-1).then_inc(ready, 1)
                    pool.wait_ge(rowed, 1)
                    src = a["cache_kidx"].rearrange("l n (q t) d -> (l n q) (t d)", q=QT)
                    for b in range(DB):
                        pool.indirect_dma_start(kidx[:, b, :], None, src,
                                                bass.IndirectOffsetOnAxis(ap=rows[:, b:b + 1], axis=0)).then_inc(gathered, 16)
                    pool.wait_ge(gathered, 16 * DB)
                    pool.dma_reset()

                @block.tensor
                def _(pe):
                    pe.wait_ge(loaded, 32)
                    for g in range(8):
                        for k in range(KC):
                            last = nc.tensor.matmul(ps[:, g, :], wq[:, g // 4, k, (g % 4) * P:(g % 4 + 1) * P],
                                                    c.xsT[:, k, :], start=(k == 0), stop=(k == KC - 1))
                    last.then_inc(projected, 1)

                @block.scalar
                def _(act):
                    act.wait_ge(projected, 1)
                    nc.scalar.activation(qs[:, 0], ps[:, 0:4, :], ACT.Copy)
                    nc.scalar.activation(qs[:, 1], ps[:, 4:8, :], ACT.Copy, scale=QSCALE).then_inc(kept, 1)

                @block.vector
                def _(dve):
                    v = Chain(dve, own)
                    nc.vector.memset(ints[:, 4:6], 0)
                    dve.wait_ge(ready, 5)
                    v.done(nc.vector.tensor_scalar(ints[:, 1:2], ints[:, 0:1], 3, None, ALU.bitwise_and))
                    dve.wait_ge(tabled, 16 * QT)
                    v.done(nc.vector.tensor_scalar(rows[:], table[:], float(QT), None, ALU.mult))
                    nc.vector.tensor_tensor(rows[:], rows[:], ints[:, 1:2].to_broadcast([P, DB]), ALU.add).then_inc(rowed, 1)
                    v.done(nc.vector.tensor_scalar(ints[:, 2:3], ints[:, 0:1], 7, None, ALU.bitwise_and))
                    v.done(nc.vector.tensor_scalar(ints[:, 3:4], ints[:, 0:1], 3, None, ALU.logical_shift_right))
                    v.done(nc.vector.tensor_copy(low[:], ints[:, 2:4]))
                    v.done(nc.vector.tensor_copy(step8[:], ints[:, 8:16]))
                    v.done(nc.vector.tensor_scalar(same_t[:], step8[:], low[:, 0:1], None, ALU.is_equal))
                    v.done(nc.vector.tensor_scalar(same_b[:], step8[:], low[:, 1:2], None, ALU.is_equal))
                    for b in range(DB):
                        v.done(nc.vector.tensor_copy(sel[:, b, b * DT:(b + 1) * DT], same_t[:]))
                    for h in range(NH):
                        v.done(nc.vector.tensor_scalar(slopes[:, h, :], same_t[0:ST, :], SLOPES[h], None, ALU.mult))
                    for b in range(DB):
                        v.done(nc.vector.tensor_scalar(spread[:, b, :], slopes[:].rearrange("p h t -> p (h t)"),
                                                       same_b[0:ST, b:b + 1], None, ALU.mult))
                    cols = newpos[:].rearrange("p (b t) -> p b t", t=DT)
                    v.done(nc.vector.tensor_copy(cols, step8[0:ST, :].unsqueeze(1).to_broadcast([ST, DB, DT])))
                    v.done(nc.vector.tensor_scalar(newpos[:], newpos[:], low[0:ST, 0:1], None, ALU.subtract))
                    dve.wait_ge(kept, 1)
                    for par in range(2):
                        for hh in range(2):
                            dst = iq_bd[par * 64:par * 64 + 64, :, par * 64:par * 64 + 64]
                            v.done(nc.vector.tensor_copy(
                                dst.rearrange("d b (n i t) -> d i n b t", i=2, t=DT)[:, hh],
                                qs[hh * 64:hh * 64 + 64, 0].rearrange("d n (b t) -> d n b t", t=DT)))
                    for kv in range(NKV):
                        for hh in range(2):
                            dst = q_bd[kv * 64:kv * 64 + 64, :, kv * 32:kv * 32 + 32]
                            v.done(nc.vector.tensor_copy(
                                dst.rearrange("d b (n i t) -> d i n b t", i=2, t=DT)[:, hh],
                                qs[hh * 64:hh * 64 + 64, 1, 2 * kv:2 * kv + 2].rearrange("d n (b t) -> d n b t", t=DT)))

        score = m.sb("score", [ST, KEYS])
        best = m.sb("best", [ST, 8])
        keysT = m.sb("keysT", [P, 2, 512])
        relu = m.sb("relu", [P, 2, 512])
        kpos = m.sb("kpos", [ST, PAST], I32)
        ps_t = m.psum("ps_t", [P, 2, 4, P])
        ps_i = m.psum("ps_i", [P, 2, 512])
        ps_s = m.psum("ps_s", [ST, 2, 2, 512])
        (turned, kept, scored, rectified, summed, read, positioned, own) = [m.sem(n) for n in (
            "turned", "kept", "scored", "rectified", "summed", "read", "positioned", "own")]
        items = [(ch, b) for ch in range(5) for b in range(DB)]
        with m.round() as block:

            @block.gpsimd
            def _(pool):
                nc.gpsimd.iota(kpos[:], [[1, PAST]], base=-PAST, channel_multiplier=0).then_inc(positioned, 1)

            @block.tensor
            def _(pe):
                def turn(g):
                    ch, b = items[g]
                    if g >= 2:
                        pe.wait_ge(kept, g - 1)
                    for u in range(4):
                        t = (ch * 4 + u) * 2
                        last = nc.tensor.transpose(ps_t[:, g % 2, u, :], kidx[:, b, t * ID:(t + 2) * ID], c.ident[:])
                    last.then_inc(turned, 1)

                def score_of(g):
                    ch, b = items[g]
                    if g >= 2:
                        pe.wait_ge(rectified, g - 1)
                    if ch < 4:
                        pe.wait_ge(kept, g + 1)
                        nc.tensor.matmul(ps_i[:, g % 2, :], iq_bd[:, b, :], keysT[:, g % 2, :],
                                         start=True, stop=True).then_inc(scored, 1)
                    else:
                        nc.tensor.matmul(ps_i[0:64, g % 2, 0:ST], iq_bd[0:64, b, 0:64], c.iksT[0:64, :],
                                         start=True, stop=True).then_inc(scored, 1)

                def sum_heads(g):
                    ch, b = items[g]
                    pe.wait_ge(rectified, g + 1)
                    if b == 0 and ch >= 2:
                        pe.wait_ge(read, ch - 1)
                    if ch < 4:
                        for par in range(2):
                            half = slice(par * 64, par * 64 + 64)
                            last = nc.tensor.matmul(ps_s[:, ch % 2, par, :], sel[half, b, :], relu[half, g % 2, :],
                                                    start=(b == 0), stop=(b == DB - 1))
                    else:
                        last = nc.tensor.matmul(ps_s[:, 0, 0, 0:ST], sel[0:64, b, :], relu[0:64, g % 2, 0:ST],
                                                start=(b == 0), stop=(b == DB - 1))
                    last.then_inc(summed, 1)

                turn(0)
                for g in range(len(items)):
                    if g + 1 < 4 * DB:
                        turn(g + 1)
                    score_of(g)
                    if g >= 1:
                        sum_heads(g - 1)
                sum_heads(len(items) - 1)

            @block.scalar
            def _(act):
                for g in range(4 * DB):
                    act.wait_ge(turned, g + 1)
                    if g >= 2:
                        act.wait_ge(scored, g - 1)
                    nc.scalar.activation(keysT[:, g % 2, :], ps_t[:, g % 2].rearrange("p u k -> p (u k)"),
                                         ACT.Copy).then_inc(kept, 1)

            @block.vector
            def _(dve):
                v = Chain(dve, own)

                def rectify(g):
                    ch, b = items[g]
                    n, width = (P, 512) if ch < 4 else (64, ST)
                    dve.wait_ge(scored, g + 1)
                    if g >= 2:
                        dve.wait_ge(summed, g - 1)
                    nc.vector.tensor_scalar(relu[0:n, g % 2, 0:width], ps_i[0:n, g % 2, 0:width], 0.0,
                                            iw_rows[0:n, b:b + 1], ALU.max, ALU.mult).then_inc(rectified, 1)

                def collect(ch):
                    dve.wait_ge(summed, (ch + 1) * DB)
                    if ch == 4:
                        v.done(nc.vector.tensor_tensor(score[:, PAST:KEYS], ps_s[:, 0, 0, 0:ST], later[:], ALU.add))
                        return
                    by_key = score[:, 0:PAST].rearrange("r (p v q) -> r q v p", v=TPR // 2, q=2)
                    for par in range(2):
                        last = nc.vector.tensor_copy(by_key[:, par, ch * 4:ch * 4 + 4, :],
                                                     ps_s[:, ch % 2, par, :].rearrange("r (v p) -> r v p", p=P))
                    last.then_inc(read, 1)

                for g in range(len(items)):
                    rectify(g)
                    if g >= DB and g % DB == 1:
                        collect(g // DB - 1)
                collect(4)
                dve.wait_ge(read, 4)
                for _ in range(TOPK // 8):
                    v.done(nc.vector.max(best[:], score[:]))
                    v.done(nc.vector.match_replace(score[:], best[:], score[:], TAKEN))
                v.done(nc.vector.tensor_scalar(bias[:], score[:], TAKEN, -BIG, ALU.not_equal, ALU.mult))
                dve.wait_ge(positioned, 1)
                v.done(nc.vector.tensor_copy(score[:, 0:PAST], kpos[:]))
                v.done(nc.vector.scalar_tensor_tensor(bias[:, 0:PAST], score[:, 0:PAST], low[0:ST, 0:1],
                                                      bias[:, 0:PAST], ALU.subtract, ALU.add))
                v.done(nc.vector.tensor_tensor(bias[:, PAST:KEYS], bias[:, PAST:KEYS], newpos[:], ALU.add))
                v.done(nc.vector.scalar_tensor_tensor(bias[:, PAST:KEYS], later[:], BIG / -MASKED,
                                                      bias[:, PAST:KEYS], ALU.mult, ALU.add))


def sample_attend(nc, c, a, o):
    rows, spread, q_bd, bias, attT = o.rows, o.spread, o.q_bd, o.bias, o.attT
    with ExitStack() as ctx:
        m = Stage(nc, ctx, "satt")
        R = NH * DT
        keys = m.sb("keys", [P, 2, TPR, P])
        values = m.sb("values", [P, 2, TPR, P])
        row_ids = m.sb("row_ids", [P, 2], I32)
        q_st = m.sb("q_st", [P, 2, R])
        spread_st = m.sb("spread_st", [ST, 2, R])
        keysT = m.sb("keysT", [P, 2, 512])
        prob = m.sb("prob", [R, 2, KEYS])
        probT = m.sb("probT", [P, 2, 8, R])
        att = m.sb("att", [R, 2, HD])
        chunk_max = m.sb("chunk_max", [R, 2, 16])
        negmax = m.sb("negmax", [R, 2])
        rowsum = m.sb("rowsum", [R, 2])
        ps_t = m.psum("ps_t", [P, 2, 4, P])
        ps_s = m.psum("ps_s", [R, 2, 512])
        ps_p = m.psum("ps_p", [P, 2, 8, R])
        ps_o = m.psum("ps_o", [R, P])
        ps_f = m.psum("ps_f", [HD, R])
        (indexed, staged, turned, kept, multiplied, moved, maxed, exped, p_turned, p_kept, weighted,
         normalised, att_turned, att_kept, stored, own) = [m.sem(n) for n in (
            "indexed", "staged", "turned", "kept", "multiplied", "moved", "maxed", "exped", "p_turned", "p_kept",
            "weighted", "normalised", "att_turned", "att_kept", "stored", "own")]
        k_in = [m.sem(f"k_in{u}") for u in range(2)]
        v_in = [m.sem(f"v_in{u}") for u in range(2)]
        NC = PAST // 512
        k_src = a["cache_k"].rearrange("l n (q t) h d -> (l n q) (t h d)", q=QT)
        v_src = a["cache_v"].rearrange("l n (q t) h d -> (l n q) (t h d)", q=QT)

        def pair(i):
            with m.round() as block:

                @block.gpsimd
                def _(pool):
                    pool.wait_ge(indexed, 1)
                    for dst, src, sems in ((keys, k_src, k_in), (values, v_src, v_in)):
                        for u in range(2):
                            pool.indirect_dma_start(dst[:, u].rearrange("p v d -> p (v d)"), None, src,
                                                    bass.IndirectOffsetOnAxis(ap=row_ids[:, u:u + 1], axis=0)
                                                    ).then_inc(sems[u], 16)
                    for sems in (k_in, v_in):
                        for u in range(2):
                            pool.wait_ge(sems[u], 16)
                    pool.dma_reset()

                @block.tensor
                def _(pe):
                    pe.wait_ge(staged, 2)

                    def turn(u, ch):
                        g = u * NC + ch
                        if ch == 0:
                            pe.wait_ge(k_in[u], 16)
                        if g >= 2:
                            pe.wait_ge(kept, g - 1)
                        for n in range(4):
                            last = nc.tensor.transpose(ps_t[:, g % 2, n, :], keys[:, u, ch * 4 + n, :], c.ident[:])
                        last.then_inc(turned, 1)

                    def scores(u, ch):
                        j = u * (NC + 1) + ch
                        if j >= 2:
                            pe.wait_ge(moved, j - 1)
                        if ch < NC:
                            pe.wait_ge(kept, u * NC + ch + 1)
                            width, kT = 512, keysT[:, (u * NC + ch) % 2, :]
                            kb = bias[:, 0:PAST].rearrange("r (p v) -> r v p", v=TPR)[:, ch * 4:ch * 4 + 4, :]
                        else:
                            width, kT, kb = ST, c.ksT[:], bias[:, PAST:KEYS]
                        nc.tensor.matmul(ps_s[:, j % 2, 0:width], q_st[:, u, :], kT, start=True, stop=False)
                        nc.tensor.matmul(ps_s[:, j % 2, 0:width], spread_st[:, u, :], kb,
                                         start=False, stop=True).then_inc(multiplied, 1)

                    def p_turn(u, q):
                        g = u * 5 + q
                        if g >= 2:
                            pe.wait_ge(p_kept, g - 1)
                        if q < 4:
                            for n in range(8):
                                v = q * 8 + n
                                last = nc.tensor.transpose(ps_p[:, g % 2, n, :], prob[:, u, v * P:(v + 1) * P],
                                                           c.ident[0:R, 0:R])
                        else:
                            last = nc.tensor.transpose(ps_p[0:ST, g % 2, 0, :], prob[:, u, PAST:KEYS], c.ident[0:R, 0:R])
                        last.then_inc(p_turned, 1)

                    def weigh(u, q):
                        g = u * 5 + q
                        pe.wait_ge(p_kept, g + 1)
                        if q == 0:
                            pe.wait_ge(v_in[u], 16)
                            if u:
                                pe.wait_ge(normalised, 1)
                        if q < 4:
                            for n in range(8):
                                v = q * 8 + n
                                last = nc.tensor.matmul(ps_o[:], probT[:, g % 2, n, :], values[:, u, v, :],
                                                        start=(v == 0), stop=False)
                        else:
                            last = nc.tensor.matmul(ps_o[:], probT[0:ST, g % 2, 0, :], c.vs[:], start=False, stop=True)
                        last.then_inc(weighted, 1)

                    for u in range(2):
                        turn(u, 0)
                        for ch in range(NC):
                            if ch + 1 < NC:
                                turn(u, ch + 1)
                            scores(u, ch)
                        scores(u, NC)
                    for u in range(2):
                        pe.wait_ge(exped, u + 1)
                        p_turn(u, 0)
                        for q in range(5):
                            if q < 4:
                                p_turn(u, q + 1)
                            weigh(u, q)
                        pe.wait_ge(normalised, u + 1)
                        if u:
                            pe.wait_ge(att_kept, 1)
                        nc.tensor.transpose(ps_f[:], att[:, u, :], c.ident[0:R, 0:R]).then_inc(att_turned, 1)

                @block.scalar
                def _(act):
                    nc.scalar.activation(q_st[:], q_bd[:, bass.ds(i * 2, 2), :], ACT.Copy).then_inc(staged, 1)
                    nc.scalar.activation(spread_st[:], spread[:, bass.ds(i * 2, 2), :], ACT.Copy).then_inc(staged, 1)

                    def exp(u):
                        act.wait_ge(maxed, u + 1)
                        nc.scalar.activation(prob[:, u, :], prob[:, u, :], ACT.Exp, bias=negmax[:, u:u + 1],
                                             accum_out=rowsum[:, u:u + 1]).then_inc(exped, 1)

                    for u in range(2):
                        for ch in range(NC):
                            g = u * NC + ch
                            act.wait_ge(turned, g + 1)
                            if g >= 2:
                                act.wait_ge(multiplied, (g - 2) // NC * (NC + 1) + (g - 2) % NC + 1)
                            nc.scalar.activation(keysT[:, g % 2, :], ps_t[:, g % 2].rearrange("p u k -> p (u k)"),
                                                 ACT.Copy).then_inc(kept, 1)
                    exp(0)
                    exp(1)
                    for u in range(2):
                        for q in range(5):
                            g = u * 5 + q
                            act.wait_ge(p_turned, g + 1)
                            if g >= 2:
                                act.wait_ge(weighted, g - 1)
                            if q < 4:
                                nc.scalar.activation(probT[:, g % 2], ps_p[:, g % 2], ACT.Copy).then_inc(p_kept, 1)
                            else:
                                nc.scalar.activation(probT[0:ST, g % 2, 0, :], ps_p[0:ST, g % 2, 0, :],
                                                     ACT.Copy).then_inc(p_kept, 1)
                        act.wait_ge(att_turned, u + 1)
                        dst = attT[:].rearrange("d h (b t) -> d h b t", t=DT)[:, :, bass.ds(i * 2 + u, 1), :]
                        nc.scalar.activation(dst, ps_f[:].rearrange("d (h t) -> d h t", t=DT).unsqueeze(2),
                                             ACT.Copy).then_inc(att_kept, 1)
                    act.wait_ge(att_kept, 2)

                @block.vector
                def _(dve):
                    v = Chain(dve, own)
                    nc.vector.tensor_copy(row_ids[:], rows[:, bass.ds(i * 2, 2)]).then_inc(indexed, 1)
                    for u in range(2):
                        for ch in range(NC + 1):
                            j = u * (NC + 1) + ch
                            width = 512 if ch < NC else ST
                            dve.wait_ge(multiplied, j + 1)
                            nc.vector.tensor_scalar(prob[:, u, ch * 512:ch * 512 + width], ps_s[:, j % 2, 0:width], 1.0,
                                                    None, ALU.mult, ALU.max,
                                                    accum_out=chunk_max[:, u, ch:ch + 1]).then_inc(moved, 1)
                        dve.wait_ge(moved, (u + 1) * (NC + 1))
                        v.done(nc.vector.reduce_max(negmax[:, u:u + 1], chunk_max[:, u, 0:NC + 1], AX_X))
                        nc.vector.tensor_scalar(negmax[:, u:u + 1], negmax[:, u:u + 1], -1.0, None,
                                                ALU.mult).then_inc(maxed, 1)
                    for u in range(2):
                        dve.wait_ge(exped, u + 1)
                        v.done(nc.vector.reciprocal(rowsum[:, u:u + 1], rowsum[:, u:u + 1]))
                        dve.wait_ge(weighted, 5 * (u + 1))
                        for kv in range(NKV):
                            r = slice(kv * 32, kv * 32 + 32)
                            last = nc.vector.tensor_scalar(att[r, u, :], ps_o[r, kv * HD:(kv + 1) * HD],
                                                           rowsum[r, u:u + 1], None, ALU.mult)
                        last.then_inc(normalised, 1)

        with nc.Fori(0, DB // 2) as i:
            pair(i)
        with m.round() as block:
            @block.sync
            def _(sp):
                sp.dma_start(a["attn_t"].rearrange("(h d) t -> d h t", d=HD)[:, :, S:S + ST], attT[:]).then_inc(stored, 16)
                sp.wait_ge(stored, 16)


def stage_merge(nc, a):
    with ExitStack() as ctx:
        m = Stage(nc, ctx, "merge")
        up_c = m.sb("up_c", [P, 4, D])
        up_a = m.sb("up_a", [P, 4, D])
        w_out = m.sb("w_out", [P, KC, D])
        gain = m.sb("gain", [P, D])
        convw = m.sb("convw", [P, 3, 4])
        pc = m.sb("pc", [P, 4, LEAD + BAND])
        pu = m.sb("pu", [P, 4, LEAD + BAND])
        p_new = m.sb("p_new", [P, 4, DB, 2 + DT])
        pb = m.sb("pb", [P, 4, BAND])
        conv = m.sb("conv", [P, 4, BAND])
        silu = m.sb("silu", [P, 4, BAND])
        attn = m.sb("attn", [P, 4, BAND])
        gates = m.sb("gates", [P, 16, BAND])
        merged = m.sb("merged", [P, KC, BAND])
        part = m.sb("part", [P, BAND])
        x = m.sb("x", [P, TPB, D])
        y = m.sb("y", [P, 2, D])
        st = m.sb("st", [P, 2, 8])
        ps_u = m.psum("ps_u", [P, 4, 512])
        ps_y = m.psum("ps_y", [P, 2, D])
        pu_flat = pu[:].rearrange("p n t -> p (n t)")
        (weights, conv_in, z_acted, az_acted, g_acted, convolved, outs, attn_in, x_in, gated, upped, merged_n, out_done, added, squared, meaned,
         rooted, finished, own, own_act) = [m.sem(n) for n in (
            "weights", "conv_in", "z_acted", "az_acted", "g_acted", "convolved", "outs", "attn_in", "x_in", "gated", "upped", "merged_n", "out_done", "added",
            "squared", "meaned", "rooted", "finished", "own", "own_act")]
        gates_in = [m.sem(f"gates_in{s}") for s in range(4)]
        stored = [m.sem(f"stored{s}") for s in range(2)]

        with m.round() as block:
            @block.sync
            def _(sp):
                sp.dma_start(up_c[:], a["w_up_conv"].rearrange("l (k p) n -> (l p) k n", p=P)).then_inc(weights, 16)
                sp.dma_start(up_a[:], a["w_up_attn"].rearrange("l (k p) n -> (l p) k n", p=P)).then_inc(weights, 16)
                sp.dma_start(w_out[:], a["w_out"].rearrange("l (k p) n -> (l p) k n", p=P)).then_inc(weights, 16)
                sp.dma_start(gain[:], a["final_gain"].rearrange("(a d) -> a d", a=1).to_broadcast([P, D])).then_inc(weights, 16)
                for j in range(3):
                    sp.dma_start(convw[:, j, :], a["conv_w"][0, j, :].rearrange("(g p) -> p g", p=P),
                                 allow_slow_non_contiguous=True).then_inc(weights, 16)
                for b in range(DB):
                    for j in range(2):
                        sp.dma_start(p_new[:, :, b, j], a["state_conv"][0, b, j, :].rearrange("(g p) -> p g", p=P),
                                     allow_slow_non_contiguous=True).then_inc(weights, 16)
                sp.wait_ge(weights, 16 * (7 + 2 * DB))

        def band(t0, width, x_src, y_dst, sample):
            cols, rest_cols = bass.ds(t0, width), bass.ds(t0 + LEAD, width)
            lead = 0 if sample else LEAD
            rows = min(width, P)
            nt = width // rows
            with m.round() as block:

                @block.sync
                def _(sp):
                    def rows_of(t):
                        return t.rearrange("(n p) t -> p n t", p=P)
                    rest = rows_of(a["rest_t"])
                    for dst, group in ((pc, R_C), (pu, R_U)):
                        sp.dma_start(dst[:, :, 0:lead + width],
                                     rest[:, 4 * group:4 * group + 4, bass.ds(t0 + LEAD - lead, lead + width)]
                                     ).then_inc(conv_in, 16)
                    for dst, group in ((conv, R_Z), (pb, R_B)):
                        sp.dma_start(dst[:, :, 0:width], rest[:, 4 * group:4 * group + 4, rest_cols]).then_inc(conv_in, 16)
                    sp.dma_start(silu[:, :, 0:width], rest[:, 4 * R_AZ:4 * R_AZ + 4, rest_cols]).then_inc(attn_in, 16)
                    sp.dma_start(attn[:, :, 0:width], rows_of(a["attn_t"])[:, :, cols]).then_inc(attn_in, 16)
                    for q in range(4):
                        for half, group in enumerate((R_GC, R_GA)):
                            n = half * KC + 2 * q
                            sp.dma_start(gates[:, n:n + 2, 0:width],
                                         rest[:, 4 * group + 2 * q:4 * group + 2 * q + 2, rest_cols]
                                         ).then_inc(gates_in[q], 16)
                    sp.dma_start(x[0:rows, 0:nt, :], x_src).then_inc(x_in, 16)
                    for t in range(nt):
                        sp.wait_ge(finished, t + 1)
                        sp.dma_start(y_dst(t), y[0:rows, t % 2, :]).then_inc(stored[t % 2], 16)
                    for s in range(min(nt, 2)):
                        sp.wait_ge(stored[s], 16 * ((nt + 1 - s) // 2))
                    sp.wait_ge(convolved, 1)
                    if sample:
                        for b in range(DB):
                            for j in range(2):
                                sp.dma_start(a["new_conv_sample"][0, b, j, :].rearrange("(g p) -> p g", p=P),
                                             p_new[:, :, b, DT + j], allow_slow_non_contiguous=True).then_inc(outs, 16)
                        sp.wait_ge(outs, 32 * DB)
                    else:
                        for j in range(2):
                            sp.dma_start(a["new_conv_prompt"][0, 0, j, :].rearrange("(g p) -> p g", p=P),
                                         pc[:, :, BAND + j], allow_slow_non_contiguous=True).then_inc(outs, 16)
                        sp.wait_ge(outs, 32)

                @block.tensor
                def _(pe):
                    pe.wait_ge(convolved, 1)
                    for n in range(KC):
                        if n >= 2:
                            pe.wait_ge(merged_n, n - 1)
                        for k in range(4):
                            nc.tensor.matmul(ps_u[:, 2 * (n % 2), 0:width], up_c[:, k, n * P:(n + 1) * P],
                                             conv[:, k, 0:width], start=(k == 0), stop=(k == 3))
                        if n == 0:
                            pe.wait_ge(gated, 1)
                        for k in range(4):
                            last = nc.tensor.matmul(ps_u[:, 2 * (n % 2) + 1, 0:width], up_a[:, k, n * P:(n + 1) * P],
                                                    attn[:, k, 0:width], start=(k == 0), stop=(k == 3))
                        last.then_inc(upped, 1)
                    pe.wait_ge(merged_n, KC)
                    for t in range(nt):
                        if t >= 2:
                            pe.wait_ge(added, t - 1)
                        for half in range(2):
                            for k in range(KC):
                                last = nc.tensor.matmul(ps_y[0:rows, t % 2, half * 512:(half + 1) * 512],
                                                        merged[:, k, t * rows:(t + 1) * rows],
                                                        w_out[:, k, half * 512:(half + 1) * 512],
                                                        start=(k == 0), stop=(k == KC - 1))
                        last.then_inc(out_done, 1)

                @block.vector
                def _(dve):
                    v = Chain(dve, own)
                    dve.wait_ge(conv_in, 64)

                    def by_sample(x):
                        return x.rearrange("p (b t) -> p b t", t=DT)

                    if sample:
                        for g in range(4):
                            v.done(nc.vector.tensor_tensor(p_new[:, g, :, 2:2 + DT], by_sample(pc[:, g, 0:width]),
                                                           by_sample(pu[:, g, 0:width]), ALU.mult))
                    else:
                        v.done(nc.vector.tensor_tensor(pc[:], pc[:], pu[:], ALU.mult))
                    y_conv = pu[:, :, 0:width]
                    for j in range(3):
                        for g in range(4):
                            if sample:
                                out, tap = by_sample(y_conv[:, g, :]), p_new[:, g, :, j:j + DT]
                            else:
                                out, tap = y_conv[:, g, :], pc[:, g, j:j + width]
                            if j == 0:
                                ins = nc.vector.tensor_scalar(out, tap, convw[:, j, g:g + 1], None, ALU.mult)
                            else:
                                ins = nc.vector.scalar_tensor_tensor(out, tap, convw[:, j, g:g + 1], out,
                                                                     ALU.mult, ALU.add)
                            v.done(ins)
                    v.done(nc.vector.tensor_tensor(y_conv, pb[:, :, 0:width], y_conv, ALU.mult))
                    dve.wait_ge(z_acted, 1)
                    nc.vector.tensor_tensor(conv[:, :, 0:width], conv[:, :, 0:width], y_conv,
                                            ALU.mult).then_inc(convolved, 1)
                    dve.wait_ge(attn_in, 32)
                    dve.wait_ge(az_acted, 1)
                    nc.vector.tensor_tensor(attn[:, :, 0:width], attn[:, :, 0:width], silu[:, :, 0:width],
                                            ALU.mult).then_inc(gated, 1)
                    for n in range(KC):
                        dve.wait_ge(upped, n + 1)
                        dve.wait_ge(g_acted, n // 2 + 1)
                        v.done(nc.vector.tensor_tensor(merged[:, n, 0:width], ps_u[:, 2 * (n % 2), 0:width],
                                                       gates[:, n, 0:width], ALU.mult))
                        v.done(nc.vector.tensor_tensor(part[:, 0:width], ps_u[:, 2 * (n % 2) + 1, 0:width],
                                                       gates[:, KC + n, 0:width], ALU.mult))
                        nc.vector.tensor_tensor(merged[:, n, 0:width], merged[:, n, 0:width], part[:, 0:width],
                                                ALU.add).then_inc(merged_n, 1)
                        dve.wait_ge(merged_n, n + 1)
                    dve.wait_ge(x_in, 16)

                    def add(t):
                        s = t % 2
                        dve.wait_ge(out_done, t + 1)
                        if t >= 2:
                            dve.wait_ge(stored[s], 16 * (t // 2))
                        nc.vector.tensor_tensor(y[0:rows, s, :], ps_y[0:rows, s, :], x[0:rows, t, :], ALU.add).then_inc(added, 1)

                    def finish(t):
                        s = t % 2
                        dve.wait_ge(squared, t + 1)
                        v.done(nc.vector.tensor_scalar(st[0:rows, s, 1:2], st[0:rows, s, 5:6], 1.0 / D, EPS,
                                                       ALU.mult, ALU.add))
                        nc.vector.tensor_copy(st[0:rows, s, 6:7], st[0:rows, s, 1:2]).then_inc(meaned, 1)
                        dve.wait_ge(rooted, t + 1)
                        refined_rstd(nc, v, st[0:rows, s, 1:2], st[0:rows, s, 4:5], st[0:rows, s, 3:4],
                                     st[0:rows, s, 2:3])
                        nc.vector.scalar_tensor_tensor(y[0:rows, s, :], y[0:rows, s, :], st[0:rows, s, 3:4],
                                                       gain[0:rows, :], ALU.mult, ALU.mult).then_inc(finished, 1)

                    for t in range(nt):
                        add(t)
                        finish(t)

                @block.scalar
                def _(act):
                    o = Chain(act, own_act)
                    act.wait_ge(conv_in, 64)
                    nc.scalar.activation(conv[:, :, 0:width], conv[:, :, 0:width], ACT.Silu).then_inc(z_acted, 1)
                    act.wait_ge(attn_in, 32)
                    nc.scalar.activation(silu[:, :, 0:width], silu[:, :, 0:width], ACT.Silu).then_inc(az_acted, 1)
                    for q in range(4):
                        act.wait_ge(gates_in[q], 32)
                        both = gates[:].rearrange("p (h n) t -> p h n t", h=2)
                        for half in range(2):
                            part_q = both[:, half, 2 * q:2 * q + 2, 0:width]
                            ins = nc.scalar.activation(part_q, part_q, ACT.Sigmoid)
                        ins.then_inc(g_acted, 1)
                    act.wait_ge(convolved, 1)
                    for t in range(nt):
                        s = t % 2
                        act.wait_ge(added, t + 1)
                        o.done(nc.scalar.activation(pu_flat[0:rows, 0:D], y[0:rows, s, :], ACT.Square,
                                                    accum_out=st[0:rows, s, 0:1]))
                        nc.scalar.activation(st[0:rows, s, 5:6], st[0:rows, s, 0:1], ACT.Copy).then_inc(squared, 1)
                        act.wait_ge(meaned, t + 1)
                        nc.scalar.activation(st[0:rows, s, 2:3], st[0:rows, s, 1:2], ACT.Sqrt).then_inc(rooted, 1)

        with nc.Fori(0, NBAND) as i:
            xb = a["x_prompt"].rearrange("b (i t p) d -> (b i) p t d", p=P, t=TPB)[i]
            yb = a["y_prompt"].rearrange("b (t p) d -> (b t) p d", p=P)
            band(i * BAND, BAND, xb, lambda t: yb[i * TPB + t], False)
        band(S, ST, a["x_sample"].rearrange("b t d -> (b t) d").unsqueeze(1),
             lambda t: a["y_sample"].rearrange("b t d -> (b t) d"), True)


def hybrid_kernel(nc, a):
    with ExitStack() as ctx:
        def sb(name, shape):
            return ctx.enter_context(nc.sbuf_tensor(name, shape, F32))

        c = Named()
        c.ident = sb("ident", [P, P])
        c.xnT = sb("xnT", [P, KC, S])
        c.xsT = sb("xsT", [P, KC, ST])
        c.ksT = sb("ksT", [P, ST])
        c.iksT = sb("iksT", [P, ST])
        c.vs = sb("vs", [ST, P])
        c.iws = sb("iws", [ST, NI])
        with ExitStack() as prompt:
            def of_prompt(name, shape):
                return prompt.enter_context(nc.sbuf_tensor(name, shape, F32))

            c.keypos = of_prompt("keypos", [P, S])
            c.tilepos = of_prompt("tilepos", [P, NT])
            c.kT = of_prompt("kT", [P, S])
            c.ikT = of_prompt("ikT", [P, S])
            c.v = of_prompt("v", [P, NT * P])
            c.iw = of_prompt("iw", [P, NT * NI])
            stage_constants(nc, c)
            stage_norm(nc, c, a)
            stage_prompt_attention(nc, c, a)
        stage_sample_attention(nc, c, a)
    stage_merge(nc, a)


INPUTS = ["x_prompt", "x_sample", "cache_k", "cache_v", "cache_kidx", "state_conv", "page_table",
          "norm_gain", "w_in", "conv_w", "w_up_conv", "w_up_attn", "w_out", "final_gain"]
OUTPUTS = {
    "y_prompt": (1, S, D), "y_sample": (DB, DT, D),
    "new_k_prompt": (1, 1, S, NKV, HD), "new_v_prompt": (1, 1, S, NKV, HD),
    "new_kidx_prompt": (1, 1, S, ID), "new_conv_prompt": (1, 1, 2, DC),
    "new_k_sample": (1, DB, DT, NKV, HD), "new_v_sample": (1, DB, DT, NKV, HD),
    "new_kidx_sample": (1, DB, DT, ID), "new_conv_sample": (1, DB, 2, DC),
}


def kernel(**inputs):
    import numpy as np
    import concourse.bacc as bacc
    from concourse.bass_utils import run_bass_kernel_spmd

    nc = bacc.Bacc("TRN2", target_bir_lowering=False, num_devices=1)
    dram, arrays = {}, {}
    for name in INPUTS:
        x = np.ascontiguousarray(inputs[name])
        arrays[f"in_{name}"] = x
        dram[name] = nc.dram_tensor(f"in_{name}", x.shape, mybir.dt.from_np(x.dtype), kind="ExternalInput").ap()
    for name, shape in OUTPUTS.items():
        dram[name] = nc.dram_tensor(f"out_{name}", shape, F32, kind="ExternalOutput").ap()
    dram["attn_t"] = nc.dram_tensor("attn_t", (NH * HD, S + ST), F32).ap()
    dram["rest_t"] = nc.dram_tensor("rest_t", (len(GROUPS) * 512, LEAD + S + ST), F32).ap()
    dram["iw_scratch"] = nc.dram_tensor("iw_scratch", (DB, NI, DT), F32).ap()
    hybrid_kernel(nc, dram)
    r = run_bass_kernel_spmd(nc, [arrays], core_ids=[0])
    return tuple(r.results[0][f"out_{name}"] for name in OUTPUTS)
```

```python
from contextlib import ExitStack, contextmanager

import concourse.bass as bass
from concourse import mybir

F32 = mybir.dt.float32
I32 = mybir.dt.int32
ALU = mybir.AluOpType
ACT = mybir.ActivationFunctionType
AX_X = mybir.AxisListType.X

D = 1024
S = 2048
DB, DT = 8, 8
ST = DB * DT
DC = 512
NH, HD, NKV = 8, 64, 2
G = NH // NKV
NI, ID = 8, 64
PAGE, NPAGE = 128, 32
PAST = PAGE * NPAGE
TOPK = 256
EPS = 1e-6
P = 128
KC = D // P
NT = S // P
BAND = 512
NBAND = S // BAND
TPB = BAND // P
BIG = 1.0e33
MASKED = -1.0e30
TAKEN = -3.0e38
SLOPES = [2.0 ** (-8.0 * (h + 1) / NH) for h in range(NH)]
ISCALE = float(NI) ** -0.5
QSCALE = float(HD) ** -0.5

O_B, O_C, O_U, O_Z, O_Q, O_K, O_V, O_AZ, O_IQ, O_IK, O_IW, O_GC, O_GA = (
    0, 512, 1024, 1536, 2048, 2560, 2688, 2816, 3328, 3840, 3904, 3912, 4936)
KVW = 2 * NKV * HD
IKW = ID + NI


class Named:
    pass


class Chain:

    def __init__(self, eng, sem):
        self.eng, self.sem, self.n = eng, sem, 0

    def done(self, ins):
        ins.then_inc(self.sem, 1)
        self.n += 1
        self.eng.wait_ge(self.sem, self.n)


class Stage:

    def __init__(self, nc, ctx, name):
        self.nc, self.ctx, self.name, self.sems = nc, ctx, name, []

    def sb(self, name, shape, dt=F32):
        return self.ctx.enter_context(self.nc.sbuf_tensor(f"{self.name}_{name}", shape, dt))

    def psum(self, name, shape):
        return self.ctx.enter_context(self.nc.psum_tensor(f"{self.name}_{name}", shape, F32))

    def sem(self, name):
        self.sems.append(self.ctx.enter_context(self.nc.semaphore(f"{self.name}_{name}")))
        return self.sems[-1]

    @contextmanager
    def round(self):
        with self.nc.Block() as block:
            yield block
        for s in self.sems:
            self.nc.gpsimd.sem_clear(s)
        self.nc.all_engine_barrier()


def refined_rstd(nc, v, ms, tmp, rstd, std):
    v.done(nc.vector.reciprocal(rstd, std))
    v.done(nc.vector.tensor_tensor(tmp, rstd, rstd, ALU.mult))
    v.done(nc.vector.tensor_tensor(tmp, tmp, ms, ALU.mult))
    v.done(nc.vector.tensor_scalar(tmp, tmp, -0.5, 1.5, ALU.mult, ALU.add))
    v.done(nc.vector.tensor_tensor(rstd, rstd, tmp, ALU.mult))


def stage_constants(nc, c):
    with ExitStack() as ctx:
        m = Stage(nc, ctx, "const")
        iotas, cleared, made = m.sem("iotas"), m.sem("cleared"), m.sem("made")
        keys = m.sb("keys", [P, S], I32)
        with m.round() as block:

            @block.gpsimd
            def _(pool):
                nc.gpsimd.memset(c.ident[:], 0.0).then_inc(cleared, 1)
                nc.gpsimd.iota(keys[:], [[1, S]], base=0, channel_multiplier=-1).then_inc(iotas, 1)
                pool.wait_ge(cleared, 1)
                nc.gpsimd.affine_select(out=c.ident[:], in_=c.ident[:], compare_op=ALU.not_equal, fill=1.0,
                                        base=0, pattern=[[-1, P]], channel_multiplier=1).then_inc(made, 1)

            @block.vector
            def _(dve):
                dve.wait_ge(iotas, 1)
                nc.vector.tensor_copy(c.keypos[:], keys[:]).then_inc(made, 1)


def stage_norm(nc, c, a):
    with ExitStack() as ctx:
        m = Stage(nc, ctx, "norm")
        XBUF = 4
        TPR_NORM = 8
        gain = m.sb("gain", [P, D])
        wkv = m.sb("wkv", [P, KC, KVW])
        wik = m.sb("wik", [P, KC, IKW])
        x_in = m.sb("x_in", [P, XBUF, D])
        xn = m.sb("xn", [P, 2, D])
        junk = m.sb("junk", [P, D])
        xt = m.sb("xt", [P, 2, KC, P])
        kv = m.sb("kv", [P, 2, KVW])
        ik = m.sb("ik", [P, 2, 2, ID])
        st = m.sb("st", [P, XBUF, 8])
        ps_t = m.psum("ps_t", [P, 2, KC, P])
        ps_kv = m.psum("ps_kv", [P, 2, 512])
        ps_kt = m.psum("ps_kt", [P, 2, 4, P])
        (weights, squared, meaned, rooted, normed, turned, staged, kept, projected, evacuated,
         k_turned, k_kept, own) = [m.sem(n) for n in (
            "weights", "squared", "meaned", "rooted", "normed", "turned", "staged", "kept",
            "projected", "evacuated", "k_turned", "k_kept", "own")]
        own_act = m.sem("own_act")
        x_ready = [m.sem(f"x_ready{s}") for s in range(XBUF)]
        stored = [m.sem(f"stored{s}") for s in range(2)]
        x_tiles = a["x_prompt"].rearrange("b (t p) d -> (b t) p d", p=P)
        win = a["w_in"].rearrange("l (k p) n -> (l p) k n", p=P)
        k_out = a["new_k_prompt"].rearrange("l b (t p) h d -> (l b t) p (h d)", p=P)
        v_out = a["new_v_prompt"].rearrange("l b (t p) h d -> (l b t) p (h d)", p=P)
        i_out = a["new_kidx_prompt"].rearrange("l b (t p) d -> (l b t) p d", p=P)

        with m.round() as block:
            @block.sync
            def _(sp):
                sp.dma_start(gain[:], a["norm_gain"][0:1, :].to_broadcast([P, D])).then_inc(weights, 16)
                sp.dma_start(wkv[:], win[:, :, O_K:O_K + KVW]).then_inc(weights, 16)
                sp.dma_start(wik[:], win[:, :, O_IK:O_IK + IKW]).then_inc(weights, 16)
                sp.wait_ge(weights, 48)

        def tiles(n, rows, dram, dst):
            def at(k):
                return 0 <= k < n

            with m.round() as block:

                @block.sync
                def _(sp):
                    def load(t):
                        if t >= XBUF:
                            sp.wait_ge(normed, t - XBUF + 1)
                        sp.dma_start(x_in[0:rows, t % XBUF, :], dram(t)[0]).then_inc(x_ready[t % XBUF], 16)

                    for t in range(min(n, XBUF)):
                        load(t)
                    for t in range(n):
                        s = t % 2
                        sp.wait_ge(evacuated, t + 1)
                        _, ko, vo, io = dram(t)
                        sp.dma_start(ko, kv[0:rows, s, 0:P]).then_inc(stored[s], 16)
                        sp.dma_start(vo, kv[0:rows, s, P:2 * P]).then_inc(stored[s], 16)
                        sp.dma_start(io, ik[0:rows, s, 0, :]).then_inc(stored[s], 16)
                        if t + XBUF < n:
                            load(t + XBUF)
                    for s in range(min(n, 2)):
                        sp.wait_ge(stored[s], 48 * ((n + 1 - s) // 2))

                @block.scalar
                def _(act):
                    o = Chain(act, own_act)

                    def square(t):
                        s = t % XBUF
                        act.wait_ge(x_ready[s], 16 * (t // XBUF + 1))
                        if t >= XBUF:
                            act.wait_ge(normed, t - XBUF + 1)
                        o.done(nc.scalar.activation(junk[0:rows, :], x_in[0:rows, s, :], ACT.Square,
                                                    accum_out=st[0:rows, s, 0:1]))
                        nc.scalar.activation(st[0:rows, s, 5:6], st[0:rows, s, 0:1], ACT.Copy).then_inc(squared, 1)

                    def root(t):
                        act.wait_ge(meaned, t + 1)
                        nc.scalar.activation(st[0:rows, t % XBUF, 2:3], st[0:rows, t % XBUF, 1:2], ACT.Sqrt
                                             ).then_inc(rooted, 1)

                    def keep(t):
                        act.wait_ge(staged, t + 1)
                        nc.scalar.activation(dst(t)[0], ps_t[:, t % 2, :, 0:rows], ACT.Copy).then_inc(kept, 1)

                    def keep_keys(t):
                        _, kd, ikd, _, _ = dst(t)
                        act.wait_ge(k_turned, t + 1)
                        nc.scalar.activation(kd, ps_kt[:, t % 2, 0, 0:rows], ACT.Copy)
                        nc.scalar.activation(ikd, ps_kt[:, t % 2, 1, 0:rows], ACT.Copy).then_inc(k_kept, 1)

                    for k in range(n + 4):
                        if at(k):
                            square(k)
                        if at(k - 1):
                            root(k - 1)
                        if at(k - 2):
                            keep(k - 2)
                        if at(k - 4):
                            keep_keys(k - 4)

                @block.vector
                def _(dve):
                    v = Chain(dve, own)

                    def mean(t):
                        s = t % XBUF
                        dve.wait_ge(squared, t + 1)
                        v.done(nc.vector.tensor_scalar(st[0:rows, s, 1:2], st[0:rows, s, 5:6], 1.0 / D, EPS,
                                                       ALU.mult, ALU.add))
                        nc.vector.tensor_copy(st[0:rows, s, 6:7], st[0:rows, s, 1:2]).then_inc(meaned, 1)

                    def norm(t):
                        s = t % XBUF
                        dve.wait_ge(rooted, t + 1)
                        refined_rstd(nc, v, st[0:rows, s, 1:2], st[0:rows, s, 4:5], st[0:rows, s, 3:4],
                                     st[0:rows, s, 2:3])
                        if t >= 2:
                            dve.wait_ge(turned, t - 1)
                        nc.vector.scalar_tensor_tensor(xn[0:rows, t % 2, :], x_in[0:rows, s, :], st[0:rows, s, 3:4],
                                                       gain[0:rows, :], ALU.mult, ALU.mult).then_inc(normed, 1)

                    def stage(t):
                        dve.wait_ge(turned, t + 1)
                        if t >= 2:
                            dve.wait_ge(projected, t - 1)
                        nc.vector.tensor_copy(xt[:, t % 2, :, 0:rows], ps_t[:, t % 2, :, 0:rows]).then_inc(staged, 1)

                    def evacuate(t):
                        s = t % 2
                        _, _, _, vd, iwd = dst(t)
                        dve.wait_ge(projected, t + 1)
                        if t >= 2:
                            dve.wait_ge(stored[s], 48 * (t // 2))
                            dve.wait_ge(k_turned, t - 1)
                        nc.vector.tensor_copy(kv[0:rows, s, :], ps_kv[0:rows, s, 0:KVW])
                        nc.vector.tensor_copy(vd, ps_kv[0:rows, s, P:2 * P])
                        nc.vector.tensor_scalar(iwd, ps_kv[0:rows, s, KVW + ID:KVW + IKW], ISCALE, None, ALU.mult)
                        nc.vector.tensor_copy(ik[0:rows, s, 0, :], ps_kv[0:rows, s, KVW:KVW + ID])
                        nc.vector.tensor_copy(ik[0:rows, s, 1, :], ps_kv[0:rows, s, KVW:KVW + ID]).then_inc(evacuated, 1)

                    for k in range(n + 3):
                        if at(k):
                            mean(k)
                        if at(k - 1):
                            norm(k - 1)
                        if at(k - 2):
                            stage(k - 2)
                        if at(k - 3):
                            evacuate(k - 3)

                @block.tensor
                def _(pe):
                    def turn(t):
                        pe.wait_ge(normed, t + 1)
                        if t >= 2:
                            pe.wait_ge(kept, t - 1)
                        for k in range(KC):
                            last = nc.tensor.transpose(ps_t[:, t % 2, k, 0:rows], xn[0:rows, t % 2, k * P:(k + 1) * P],
                                                       c.ident[0:rows, 0:rows])
                        last.then_inc(turned, 1)

                    def project(t):
                        s = t % 2
                        pe.wait_ge(staged, t + 1)
                        if t >= 2:
                            pe.wait_ge(evacuated, t - 1)
                        for k in range(KC):
                            nc.tensor.matmul(ps_kv[0:rows, s, 0:KVW], xt[:, s, k, 0:rows], wkv[:, k, :],
                                             start=(k == 0), stop=(k == KC - 1))
                        for k in range(KC):
                            last = nc.tensor.matmul(ps_kv[0:rows, s, KVW:KVW + IKW], xt[:, s, k, 0:rows],
                                                    wik[:, k, :], start=(k == 0), stop=(k == KC - 1))
                        last.then_inc(projected, 1)

                    def turn_keys(t):
                        s = t % 2
                        pe.wait_ge(evacuated, t + 1)
                        if t >= 2:
                            pe.wait_ge(k_kept, t - 1)
                        nc.tensor.transpose(ps_kt[:, s, 0, 0:rows], kv[0:rows, s, 0:P], c.ident[0:rows, 0:rows])
                        nc.tensor.transpose(ps_kt[:, s, 1, 0:rows], ik[0:rows, s, :, :].rearrange("p a d -> p (a d)"),
                                            c.ident[0:rows, 0:rows]).then_inc(k_turned, 1)

                    for k in range(2, n + 4):
                        if at(k - 2):
                            turn(k - 2)
                        if at(k - 3):
                            project(k - 3)
                        if at(k - 4):
                            turn_keys(k - 4)

        with nc.Fori(0, NT // TPR_NORM) as i:
            def dram(t):
                u = i * TPR_NORM + t
                return x_tiles[u], k_out[u], v_out[u], i_out[u]

            def dst(t):
                u = i * TPR_NORM + t
                return (c.xnT[:, :, bass.ds(u * P, P)], c.kT[:, bass.ds(u * P, P)], c.ikT[:, bass.ds(u * P, P)],
                        c.v[:, bass.ds(u * P, P)], c.iw[:, bass.ds(u * NI, NI)])
            tiles(TPR_NORM, P, dram, dst)

        def sample_dram(t):
            return (a["x_sample"].rearrange("b t d -> (b t) d"), a["new_k_sample"].rearrange("l b t h d -> (l b t) (h d)"),
                    a["new_v_sample"].rearrange("l b t h d -> (l b t) (h d)"),
                    a["new_kidx_sample"].rearrange("l b t d -> (l b t) d"))
        tiles(1, ST, sample_dram, lambda t: (c.xsT[:], c.ksT[:], c.iksT[:], c.vs[:], c.iws[:]))


GROUPS = [O_B, O_C, O_U, O_Z, O_AZ, O_GC, O_GC + 512, O_GA, O_GA + 512]
R_B, R_C, R_U, R_Z, R_AZ, R_GC, R_GA = 0, 1, 2, 3, 4, 5, 7
LEAD = 2
REST_LOADS = [0, 0, 0, 1, 1, 1, 1, 2, 1, 2, 2, 2, 3, 3, 3, 3, 1]
CHUNKS = [(ch * 512, 512) for ch in range(NBAND)] + [(S, ST)]


def stage_prompt_attention(nc, c, a):
    with ExitStack() as ctx:
        m = Stage(nc, ctx, "attn")
        qT = m.sb("qT", [P, 2, 2, 4, BAND])
        q_idx = m.sb("q_idx", [P, NI, P])
        q_att = m.sb("q_att", [P, NH, P])
        work = m.sb("work", [P, 2 * S])
        acc = work[:, 0:S]
        relu = work[:, S:2 * S].rearrange("p (n k) -> p n k", k=512)
        bias_h = relu
        prob = m.sb("prob", [P, 2, S])
        bias = m.sb("bias", [P, S])
        w_q = [x.rearrange("p (k n) -> p k n", k=KC) for x in (work[:], prob[:].rearrange("p s k -> p (s k)"))]
        probT = m.sb("probT", [P, 2, 4, P])
        later = m.sb("later", [P, P])
        att = m.sb("att", [P, NH * HD])
        attT = m.sb("attT", [P, 4, P])
        w_rest = m.sb("w_rest", [P, 2, KC, P])
        rest = m.sb("rest", [P, 3, 512])
        best = m.sb("best", [P, 8])
        zeros = m.sb("zeros", [P, 4 * LEAD])
        chunk_max = m.sb("chunk_max", [P, 4])
        negmax = m.sb("negmax", [P, NH])
        rowsum = m.sb("rowsum", [P, NH])
        ps_s = m.psum("ps_s", [P, 4, 512])
        ps_p = m.psum("ps_p", [P, 2, 4, P])
        ps_o = m.psum("ps_o", [P, NH * HD])
        ps_r = m.psum("ps_r", [P, 512])
        names = ("loaded", "projected", "sampled", "kept", "q_staged", "next_staged", "scored", "rectified", "summed",
                 "scaled", "multiplied", "biased", "maxed", "exped", "turned", "turned_kept", "weighted",
                 "normalised", "att_turned", "att_kept", "stored", "rest_done", "rest_kept", "own",
                 "w_in0", "w_in1", "rest_stored0", "rest_stored1", "rest_stored2")
        sets = [[m.sem(f"{n}_{u}") for n in names] for u in range(2)]
        win = a["w_in"].rearrange("l (k p) n -> (l p) k n", p=P)
        attn_out = a["attn_t"].rearrange("(n p) t -> p n t", p=P)
        rest_out = a["rest_t"].rearrange("(g n p) t -> g n p t", n=4, p=P)
        chunks, NCH = CHUNKS, len(CHUNKS)

        def project():
            (loaded, projected, sampled, kept), own = sets[1][:4], sets[1][names.index("own")]
            stored, w_in = sets[1][names.index("stored")], sets[1][names.index("w_in0"):][:2]
            with m.round() as block:
                @block.sync
                def _(sp):
                    for j, col in enumerate((O_IQ, O_Q)):
                        sp.dma_start(w_q[j], win[:, :, col:col + NH * HD]).then_inc(w_in[j], 16)
                    sp.wait_ge(kept, 1)
                    for g in (R_C, R_U):
                        sp.dma_start(rest_out[g].rearrange("n p t -> p n t")[:, :, 0:LEAD],
                                     zeros[:].rearrange("p (n t) -> p n t", t=LEAD)
                                     ).then_inc(stored, 16)
                    sp.wait_ge(stored, 32)
                    for j in range(2):
                        sp.wait_ge(w_in[j], 16)

                @block.tensor
                def _(pe):
                    for g in range(8):
                        if g % 4 == 0:
                            pe.wait_ge(w_in[g // 4], 16)
                        if g >= 4:
                            pe.wait_ge(projected, g - 3)
                        for k in range(KC):
                            last = nc.tensor.matmul(ps_s[:, g % 4, :], w_q[g // 4][:, k, (g % 4) * P:(g % 4 + 1) * P],
                                                    c.xnT[:, k, 0:BAND], start=(k == 0), stop=(k == KC - 1))
                        last.then_inc(loaded, 1)
                        for k in range(KC):
                            last = nc.tensor.matmul(ps_r[:, g * ST:(g + 1) * ST],
                                                    w_q[g // 4][:, k, (g % 4) * P:(g % 4 + 1) * P],
                                                    c.xsT[:, k, :], start=(k == 0), stop=(k == KC - 1))
                    last.then_inc(sampled, 1)

                @block.scalar
                def _(act):
                    for g in range(8):
                        act.wait_ge(loaded, g + 1)
                        nc.scalar.activation(qT[:, 0, g // 4, g % 4, :], ps_s[:, g % 4, :], ACT.Copy,
                                             scale=1.0 if g < 4 else QSCALE).then_inc(projected, 1)
                    act.wait_ge(sampled, 1)
                    for j in range(2):
                        nc.scalar.activation(c.qs[:, j], ps_r[:, 4 * ST * j:4 * ST * (j + 1)].rearrange(
                            "p (n t) -> p n t", t=ST), ACT.Copy, scale=QSCALE if j else 1.0)

                @block.vector
                def _(dve):
                    v = Chain(dve, own)
                    nc.vector.memset(zeros[:], 0.0).then_inc(kept, 1)
                    nc.vector.memset(q_idx[:], 0.0)
                    nc.vector.memset(q_att[:], 0.0)
                    v.done(nc.vector.tensor_scalar(later[:], c.keypos[:, 0:P], 0.0, MASKED, ALU.is_gt, ALU.mult))

        def key_chunks(tokens):
            return [(k, min(512, tokens - k)) for k in range(0, tokens, 512)]

        def tile(T):
            (_, _, _, _, q_staged, next_staged, scored, rectified, summed, scaled, multiplied, biased, maxed, exped,
             turned, turned_kept, weighted, normalised, att_turned, att_kept, stored, rest_done, rest_kept, own,
             w_in0, w_in1, *rest_stored) = sets[T % 2]
            w_in = (w_in0, w_in1)
            b, i = divmod(T, TPB)
            fresh = T < NT
            scored_tile = fresh and (T + 1) * P > TOPK
            L, LB = (T + 1) * P, T * P
            idx_keys = key_chunks(L) if scored_tile else []
            att_keys = key_chunks(LB) if T <= NT else []
            leaves = T >= 2
            now, before = len(idx_keys), len(att_keys)
            N = NH * before
            ahead = [O_IQ + i * P, O_Q + i * P] if b + 1 < NBAND else []
            done = sum(REST_LOADS[:T])
            quarters = [divmod(q, 4) for q in range(done, done + (REST_LOADS[T] if T <= NT else 0))]
            loads = ahead + [GROUPS[g] + n * P for g, n in quarters]
            items = ([(j, b + 1, None) for j in range(len(ahead))] +
                     [(len(ahead) + j, ch, j * NCH + ch) for j in range(len(quarters)) for ch in range(NCH)])
            stores = len(quarters) * NCH
            per_head = max(before, 1)

            def slot(n):
                steps, slots = len(items) * KC, NH * per_head
                return range(steps * n // slots, steps * (n + 1) // slots)

            with nc.Block() as block:

                @block.gpsimd
                def _(pool):
                    for sem in sets[1 - T % 2]:
                        pool.sem_clear(sem)

                @block.sync
                def _(sp):
                    def load(j):
                        sp.dma_start(w_rest[:, j % 2], win[:, :, loads[j]:loads[j] + P]
                                     ).then_inc(w_in[j % 2], 16)

                    for j in range(min(2, len(loads))):
                        load(j)
                    if leaves:
                        sp.wait_ge(att_kept, 1)
                        sp.dma_start(attn_out[:, :, (T - 2) * P:(T - 1) * P], attT[:]).then_inc(stored, 16)
                    for g, (j, ch, n) in enumerate(items):
                        t0, width = chunks[ch]
                        sp.wait_ge(rest_kept, g + 1)
                        if n is not None:
                            group, quarter = quarters[j - len(ahead)]
                            sp.dma_start(rest_out[group][quarter][:, LEAD + t0:LEAD + t0 + width],
                                         rest[:, n % 3, 0:width]).then_inc(rest_stored[n % 3], 16)
                        if (n is None or ch == NCH - 1) and j + 2 < len(loads):
                            load(j + 2)
                    if leaves:
                        sp.wait_ge(stored, 16)
                    for s in range(min(3, stores)):
                        sp.wait_ge(rest_stored[s], 16 * ((stores + 2 - s) // 3))

                @block.scalar
                def _(act):
                    for g in range(NI * now):
                        k0, width = idx_keys[g // NI]
                        act.wait_ge(scored, g + 1)
                        if g >= 4:
                            act.wait_ge(summed, g - 3)
                        nc.scalar.activation(relu[:, g % 4, 0:width], ps_s[:, g % 4, 0:width], ACT.Relu
                                             ).then_inc(rectified, 1)

                    if leaves:
                        act.wait_ge(att_turned, 1)
                        nc.scalar.activation(attT[:], ps_p[:, 0], ACT.Copy).then_inc(att_kept, 1)

                    def scale(h, ch):
                        j = h * before + ch
                        if j >= 4:
                            act.wait_ge(biased, j - 3)
                        k0, width = att_keys[ch]
                        nc.scalar.activation(bias_h[:, j % 4, 0:width], bias[:, k0:k0 + width], ACT.Copy,
                                             scale=SLOPES[h]).then_inc(scaled, 1)

                    def keep_rest(n):
                        for step in slot(n):
                            g, k = divmod(step, KC)
                            if k < KC - 1:
                                continue
                            j, ch, r = items[g]
                            width = chunks[ch][1]
                            act.wait_ge(rest_done, g + 1)
                            if r is None:
                                nc.scalar.activation(qT[:, (b + 1) % 2, j, i, :], ps_r[:], ACT.Copy, scale=QSCALE if j else 1.0).then_inc(rest_kept, 1)
                                continue
                            if r >= 3:
                                act.wait_ge(rest_stored[r % 3], 16 * (r // 3))
                            nc.scalar.activation(rest[:, r % 3, 0:width], ps_r[:, 0:width], ACT.Copy
                                                 ).then_inc(rest_kept, 1)

                    if before:
                        if now:
                            act.wait_ge(summed, NI * now)
                        for ch in range(before):
                            scale(0, ch)
                    for h in range(NH):
                        keep_rest(h * per_head)
                        if not before:
                            continue
                        act.wait_ge(maxed, h + 1)
                        nc.scalar.activation(prob[:, h % 2, 0:LB], prob[:, h % 2, 0:LB], ACT.Exp,
                                             bias=negmax[:, h:h + 1], accum_out=rowsum[:, h:h + 1]).then_inc(exped, 1)
                        for ch in range(before):
                            j = h * before + ch
                            act.wait_ge(turned, j + 1)
                            if j >= 2:
                                act.wait_ge(weighted, j - 1)
                            n = att_keys[ch][1] // P
                            nc.scalar.activation(probT[:, j % 2, 0:n, :], ps_p[:, j % 2, 0:n, :], ACT.Copy
                                                 ).then_inc(turned_kept, 1)
                            if h + 1 < NH:
                                scale(h + 1, ch)
                            if ch:
                                keep_rest(h * per_head + ch)
                    if fresh:
                        if before:
                            act.wait_ge(multiplied, N)
                        for hh in range(2):
                            for kv in range(NKV):
                                nc.scalar.activation(q_att[kv * 64:kv * 64 + 64, kv * G + hh:kv * G + G:2, :],
                                                     qT[hh * 64:hh * 64 + 64, b % 2, 1, 2 * kv:2 * kv + 2,
                                                        i * P:(i + 1) * P], ACT.Copy).then_inc(next_staged, 1)
                    if T + 1 < NT:
                        nb, ni = divmod(T + 1, TPB)
                        act.wait_ge(rest_kept, len(items))
                        for hh in range(2):
                            half = slice(hh * 64, hh * 64 + 64)
                            nc.scalar.activation(q_idx[half, hh::2, :], qT[half, nb % 2, 0, :, ni * P:(ni + 1) * P],
                                                 ACT.Copy).then_inc(q_staged, 1)

                @block.vector
                def _(dve):
                    v = Chain(dve, own)
                    if leaves:
                        v.done(nc.vector.reciprocal(rowsum[:], rowsum[:]))
                        nc.vector.tensor_tensor(att[:].rearrange("p (h d) -> p h d", d=HD),
                                                ps_o[:].rearrange("p (h d) -> p h d", d=HD),
                                                rowsum[:].unsqueeze(2).to_broadcast([P, NH, HD]),
                                                ALU.mult).then_inc(normalised, 1)
                    for ch, (k0, width) in enumerate(idx_keys):
                        out = acc[:, k0:k0 + width]
                        for h in range(NI):
                            g = ch * NI + h
                            iw = c.iw[:, T * NI + h:T * NI + h + 1]
                            dve.wait_ge(rectified, g + 1)
                            if g:
                                dve.wait_ge(summed, g)
                            if h == 0:
                                ins = nc.vector.tensor_scalar(out, relu[:, g % 4, 0:width], iw, None, ALU.mult)
                            else:
                                ins = nc.vector.scalar_tensor_tensor(out, relu[:, g % 4, 0:width], iw, out,
                                                                     ALU.mult, ALU.add)
                            ins.then_inc(summed, 1)
                    if now:
                        dve.wait_ge(summed, NI * now)
                        v.done(nc.vector.tensor_tensor(acc[:, LB:L], acc[:, LB:L], later[:], ALU.add))

                    def bias_head(h):
                        if h >= 2:
                            dve.wait_ge(turned, (h - 1) * before)
                        for ch, (k0, width) in enumerate(att_keys):
                            j = h * before + ch
                            dve.wait_ge(multiplied, j + 1)
                            dve.wait_ge(scaled, j + 1)
                            nc.vector.tensor_tensor_reduce(
                                out=prob[:, h % 2, k0:k0 + width], in0=ps_s[:, j % 4, 0:width],
                                in1=bias_h[:, j % 4, 0:width], scale=1.0, scalar=-3.0e38, op0=ALU.add, op1=ALU.max,
                                accum_out=chunk_max[:, ch:ch + 1]).then_inc(biased, 1)
                        dve.wait_ge(biased, (h + 1) * before)
                        v.done(nc.vector.reduce_max(negmax[:, h:h + 1], chunk_max[:, 0:before], AX_X))
                        nc.vector.tensor_scalar(negmax[:, h:h + 1], negmax[:, h:h + 1], -1.0, None,
                                                ALU.mult).then_inc(maxed, 1)

                    for h in range(NH):
                        if before:
                            bias_head(h)
                        if now:
                            for _ in range(TOPK // 8 // NH):
                                v.done(nc.vector.max(best[:], acc[:, 0:L]))
                                v.done(nc.vector.match_replace(acc[:, 0:L], best[:], acc[:, 0:L], TAKEN))
                    if fresh:
                        if before:
                            dve.wait_ge(scaled, N)
                        if now:
                            v.done(nc.vector.tensor_scalar(bias[:, 0:L], acc[:, 0:L], TAKEN, -BIG,
                                                           ALU.not_equal, ALU.mult))
                            v.done(nc.vector.scalar_tensor_tensor(bias[:, 0:L], c.keypos[:, 0:L], float(-LB), bias[:, 0:L],
                                                                  ALU.add, ALU.add))
                        else:
                            v.done(nc.vector.tensor_scalar(bias[:, 0:L], c.keypos[:, 0:L], float(-LB), None, ALU.add))
                        v.done(nc.vector.scalar_tensor_tensor(bias[:, LB:L], later[:], BIG / -MASKED, bias[:, LB:L],
                                                              ALU.mult, ALU.add))

                @block.tensor
                def _(pe):
                    for ch, (k0, width) in enumerate(idx_keys):
                        for h in range(NI):
                            g = ch * NI + h
                            if g >= 4:
                                pe.wait_ge(rectified, g - 3)
                            nc.tensor.matmul(ps_s[:, g % 4, 0:width], q_idx[:, h, :], c.ikT[:, k0:k0 + width],
                                             start=True, stop=True).then_inc(scored, 1)

                    if leaves:
                        pe.wait_ge(normalised, 1)
                        for n in range(4):
                            last = nc.tensor.transpose(ps_p[:, 0, n, :], att[:, n * P:(n + 1) * P], c.ident[:])
                        last.then_inc(att_turned, 1)

                    def scores(h, ch):
                        j = h * before + ch
                        k0, width = att_keys[ch]
                        if j >= 4:
                            pe.wait_ge(biased, j - 3)
                        nc.tensor.matmul(ps_s[:, j % 4, 0:width], q_att[:, h, :], c.kT[:, k0:k0 + width],
                                         start=True, stop=True).then_inc(multiplied, 1)

                    def project_rest(n):
                        for step in slot(n):
                            g, k = divmod(step, KC)
                            j, ch, _ = items[g]
                            if k == 0:
                                pe.wait_ge(w_in[j % 2], 16 * (j // 2 + 1))
                                if g >= 1:
                                    pe.wait_ge(rest_kept, g)
                            x = c.xnT[:, k, ch * 512:(ch + 1) * 512] if ch < NBAND else c.xsT[:, k, :]
                            ins = nc.tensor.matmul(ps_r[:, 0:chunks[ch][1]], w_rest[:, j % 2, k, :], x,
                                                   start=(k == 0), stop=(k == KC - 1))
                            if k == KC - 1:
                                ins.then_inc(rest_done, 1)

                    def transpose(h, ch):
                        j = h * before + ch
                        if j >= 2:
                            pe.wait_ge(turned_kept, j - 1)
                        for u in range(att_keys[ch][1] // P):
                            last = nc.tensor.transpose(ps_p[:, j % 2, u, :],
                                                       prob[:, h % 2, ch * 512 + u * P:ch * 512 + (u + 1) * P],
                                                       c.ident[:])
                        last.then_inc(turned, 1)

                    def weigh(h, ch):
                        j = h * before + ch
                        kv = h // G
                        pe.wait_ge(turned_kept, j + 1)
                        for u in range(att_keys[ch][1] // P):
                            t = ch * 4 + u
                            last = nc.tensor.matmul(ps_o[:, h * HD:(h + 1) * HD], probT[:, j % 2, u, :],
                                                    c.v[:, t * P + kv * HD:t * P + (kv + 1) * HD],
                                                    start=(t == 0), stop=(t == T - 1))
                        last.then_inc(weighted, 1)

                    if before:
                        if now:
                            pe.wait_ge(rectified, NI * now)
                        for ch in range(before):
                            scores(0, ch)
                    for h in range(NH):
                        project_rest(h * per_head)
                        if not before:
                            continue
                        pe.wait_ge(exped, h + 1)
                        if h == 0 and leaves:
                            pe.wait_ge(att_kept, 1)
                        transpose(h, 0)
                        for ch in range(before):
                            if ch + 1 < before:
                                transpose(h, ch + 1)
                            if h + 1 < NH:
                                scores(h + 1, ch)
                            if ch:
                                project_rest(h * per_head + ch)
                            weigh(h, ch)

        project()
        for T in range(NT + 2):
            tile(T)
        for sem in sets[(NT + 1) % 2]:
            nc.gpsimd.sem_clear(sem)
        nc.all_engine_barrier()


KEYS = PAST + ST
QT = 4
TPR = PAGE // QT


def stage_sample_attention(nc, c, a):
    with ExitStack() as ctx:
        m = Stage(nc, ctx, "samp")
        k = Named()
        k.rows = m.sb("rows", [P, DB], I32)
        k.table = m.sb("table", [P, DB], I32)
        k.ints = m.sb("ints", [P, 16], I32)
        k.step8 = m.sb("step8", [P, NH], F32)
        k.low = m.sb("low", [P, 2], F32)
        k.same_t = m.sb("same_t", [P, DT])
        k.same_b = m.sb("same_b", [P, DB])
        k.later = m.sb("later", [ST, ST])
        k.newpos = m.sb("newpos", [ST, ST])
        k.slopes = m.sb("slopes", [ST, NH, DT])
        k.sel = m.sb("sel", [P, DB, ST])
        k.spread = m.sb("spread", [ST, DB, NH * DT])
        k.iq_bd = m.sb("iq_bd", [P, DB, P])
        k.q_bd = m.sb("q_bd", [P, DB, NH * DT])
        k.iw_rows = m.sb("iw_rows", [P, DB])
        k.bias = m.sb("bias", [ST, KEYS])
        k.attT = m.sb("attT", [HD, NH, ST])
        sample_scores(nc, c, a, k)
        sample_attend(nc, c, a, k)


def sample_scores(nc, c, a, o):
    (rows, table, ints, step8, low, same_t, same_b, later, newpos, slopes) = (
        o.rows, o.table, o.ints, o.step8, o.low, o.same_t, o.same_b, o.later, o.newpos, o.slopes)
    sel, spread, iq_bd, q_bd, iw_rows, bias = o.sel, o.spread, o.iq_bd, o.q_bd, o.iw_rows, o.bias
    with ExitStack() as ctx:
        m = Stage(nc, ctx, "sidx")
        kidx = m.sb("kidx", [P, DB, TPR * ID])
        with ExitStack() as inner:
            w = Stage(nc, inner, "sprj")
            qs = c.qs
            (tabled, stored, spread_in, ready, rowed, gathered, own) = [w.sem(n) for n in (
                "tabled", "stored", "spread_in", "ready", "rowed", "gathered", "own")]
            with w.round() as block:

                @block.sync
                def _(sp):
                    for q in range(QT):
                        sp.dma_start(table[q::QT, :], a["page_table"].rearrange("b j -> j b"),
                                     allow_slow_non_contiguous=True).then_inc(tabled, 16)
                    for b in range(DB):
                        sp.dma_start(a["iw_scratch"][b].rearrange("h t -> t h"), c.iws[b * DT:(b + 1) * DT, :],
                                     allow_slow_non_contiguous=True).then_inc(stored, 16)
                    sp.wait_ge(stored, 16 * DB)
                    for half in range(2):
                        sp.dma_start(iw_rows[half * 64:half * 64 + 64, :], a["iw_scratch"].rearrange("b h t -> (h t) b"),
                                     allow_slow_non_contiguous=True).then_inc(spread_in, 16)
                    sp.wait_ge(spread_in, 32)

                @block.gpsimd
                def _(pool):
                    nc.gpsimd.iota(ints[:, 0:1], [[0, 1]], base=0, channel_multiplier=1).then_inc(ready, 1)
                    nc.gpsimd.iota(ints[:, 8:16], [[1, 8]], base=0, channel_multiplier=0).then_inc(ready, 1)
                    nc.gpsimd.memset(iq_bd[:], 0.0).then_inc(ready, 1)
                    nc.gpsimd.memset(q_bd[:], 0.0).then_inc(ready, 1)
                    nc.gpsimd.memset(sel[:], 0.0).then_inc(ready, 1)
                    nc.gpsimd.memset(later[:], 0.0).then_inc(ready, 1)
                    pool.wait_ge(ready, 6)
                    nc.gpsimd.affine_select(out=later[:], in_=later[:], compare_op=ALU.is_ge, fill=MASKED, base=0,
                                            pattern=[[-1, ST]], channel_multiplier=1).then_inc(ready, 1)
                    pool.wait_ge(ready, 7)
                    v = later[:].rearrange("p (b t) -> p b t", t=DT)
                    nc.gpsimd.affine_select(out=v, in_=v, compare_op=ALU.is_ge, fill=MASKED, base=DT - 1,
                                            pattern=[[DT, DB], [0, DT]], channel_multiplier=-1).then_inc(ready, 1)
                    pool.wait_ge(rowed, 1)
                    src = a["cache_kidx"].rearrange("l n (q t) d -> (l n q) (t d)", q=QT)
                    for b in range(DB):
                        pool.indirect_dma_start(kidx[:, b, :], None, src,
                                                bass.IndirectOffsetOnAxis(ap=rows[:, b:b + 1], axis=0)).then_inc(gathered, 16)
                    pool.wait_ge(gathered, 16 * DB)
                    pool.dma_reset()

                @block.vector
                def _(dve):
                    v = Chain(dve, own)
                    nc.vector.memset(ints[:, 4:6], 0)
                    dve.wait_ge(ready, 5)
                    v.done(nc.vector.tensor_scalar(ints[:, 1:2], ints[:, 0:1], 3, None, ALU.bitwise_and))
                    dve.wait_ge(tabled, 16 * QT)
                    v.done(nc.vector.tensor_scalar(rows[:], table[:], float(QT), None, ALU.mult))
                    nc.vector.tensor_tensor(rows[:], rows[:], ints[:, 1:2].to_broadcast([P, DB]), ALU.add).then_inc(rowed, 1)
                    v.done(nc.vector.tensor_scalar(ints[:, 2:3], ints[:, 0:1], 7, None, ALU.bitwise_and))
                    v.done(nc.vector.tensor_scalar(ints[:, 3:4], ints[:, 0:1], 3, None, ALU.logical_shift_right))
                    v.done(nc.vector.tensor_copy(low[:], ints[:, 2:4]))
                    v.done(nc.vector.tensor_copy(step8[:], ints[:, 8:16]))
                    v.done(nc.vector.tensor_scalar(same_t[:], step8[:], low[:, 0:1], None, ALU.is_equal))
                    v.done(nc.vector.tensor_scalar(same_b[:], step8[:], low[:, 1:2], None, ALU.is_equal))
                    for b in range(DB):
                        v.done(nc.vector.tensor_copy(sel[:, b, b * DT:(b + 1) * DT], same_t[:]))
                    for h in range(NH):
                        v.done(nc.vector.tensor_scalar(slopes[:, h, :], same_t[0:ST, :], SLOPES[h], None, ALU.mult))
                    for b in range(DB):
                        v.done(nc.vector.tensor_scalar(spread[:, b, :], slopes[:].rearrange("p h t -> p (h t)"),
                                                       same_b[0:ST, b:b + 1], None, ALU.mult))
                    cols = newpos[:].rearrange("p (b t) -> p b t", t=DT)
                    v.done(nc.vector.tensor_copy(cols, step8[0:ST, :].unsqueeze(1).to_broadcast([ST, DB, DT])))
                    v.done(nc.vector.tensor_scalar(newpos[:], newpos[:], low[0:ST, 0:1], None, ALU.subtract))
                    for par in range(2):
                        for hh in range(2):
                            dst = iq_bd[par * 64:par * 64 + 64, :, par * 64:par * 64 + 64]
                            v.done(nc.vector.tensor_copy(
                                dst.rearrange("d b (n i t) -> d i n b t", i=2, t=DT)[:, hh],
                                qs[hh * 64:hh * 64 + 64, 0].rearrange("d n (b t) -> d n b t", t=DT)))
                    for kv in range(NKV):
                        for hh in range(2):
                            dst = q_bd[kv * 64:kv * 64 + 64, :, kv * 32:kv * 32 + 32]
                            v.done(nc.vector.tensor_copy(
                                dst.rearrange("d b (n i t) -> d i n b t", i=2, t=DT)[:, hh],
                                qs[hh * 64:hh * 64 + 64, 1, 2 * kv:2 * kv + 2].rearrange("d n (b t) -> d n b t", t=DT)))

        score = m.sb("score", [ST, KEYS])
        best = m.sb("best", [ST, 8])
        keysT = m.sb("keysT", [P, 2, 512])
        relu = m.sb("relu", [P, 2, 512])
        kpos = m.sb("kpos", [ST, PAST], I32)
        ps_t = m.psum("ps_t", [P, 2, 4, P])
        ps_i = m.psum("ps_i", [P, 2, 512])
        ps_s = m.psum("ps_s", [ST, 2, 2, 512])
        (turned, kept, scored, rectified, summed, read, positioned, own, rest_done, rest_kept) = [m.sem(n) for n in (
            "turned", "kept", "scored", "rectified", "summed", "read", "positioned", "own", "rest_done", "rest_kept")]
        w_loaded = [m.sem(f"w_loaded{s}") for s in range(2)]
        rest_stored = [m.sem(f"rest_stored{s}") for s in range(4)]
        w_rest = kidx[:, 0, :].rearrange("p (s k n) -> p s k n", s=2, k=KC)
        rest = kidx[:, 1, :].rearrange("p (s n) -> p s n", s=4)
        win = a["w_in"].rearrange("l (k p) n -> (l p) k n", p=P)
        rest_out = a["rest_t"].rearrange("(g n p) t -> g n p t", n=4, p=P)
        items = [(ch, b) for ch in range(5) for b in range(DB)]
        with m.round() as block:

            @block.tensor
            def _(pe):
                def turn(g):
                    ch, b = items[g]
                    if g >= 2:
                        pe.wait_ge(kept, g - 1)
                    for u in range(4):
                        t = (ch * 4 + u) * 2
                        last = nc.tensor.transpose(ps_t[:, g % 2, u, :], kidx[:, b, t * ID:(t + 2) * ID], c.ident[:])
                    last.then_inc(turned, 1)

                def score_of(g):
                    ch, b = items[g]
                    if g >= 2:
                        pe.wait_ge(rectified, g - 1)
                    if ch < 4:
                        pe.wait_ge(kept, g + 1)
                        nc.tensor.matmul(ps_i[:, g % 2, :], iq_bd[:, b, :], keysT[:, g % 2, :],
                                         start=True, stop=True).then_inc(scored, 1)
                    else:
                        nc.tensor.matmul(ps_i[0:64, g % 2, 0:ST], iq_bd[0:64, b, 0:64], c.iksT[0:64, :],
                                         start=True, stop=True).then_inc(scored, 1)

                def sum_heads(g):
                    ch, b = items[g]
                    pe.wait_ge(rectified, g + 1)
                    if b == 0 and ch >= 2:
                        pe.wait_ge(read, ch - 1)
                    if ch < 4:
                        for par in range(2):
                            half = slice(par * 64, par * 64 + 64)
                            last = nc.tensor.matmul(ps_s[:, ch % 2, par, :], sel[half, b, :], relu[half, g % 2, :],
                                                    start=(b == 0), stop=(b == DB - 1))
                    else:
                        last = nc.tensor.matmul(ps_s[:, 0, 0, 0:ST], sel[0:64, b, :], relu[0:64, g % 2, 0:ST],
                                                start=(b == 0), stop=(b == DB - 1))
                    last.then_inc(summed, 1)

                turn(0)
                for g in range(len(items)):
                    if g + 1 < 4 * DB:
                        turn(g + 1)
                    score_of(g)
                    if g >= 1:
                        sum_heads(g - 1)
                sum_heads(len(items) - 1)

            @block.scalar
            def _(act):
                for g in range(4 * DB):
                    act.wait_ge(turned, g + 1)
                    if g >= 2:
                        act.wait_ge(scored, g - 1)
                    nc.scalar.activation(keysT[:, g % 2, :], ps_t[:, g % 2].rearrange("p u k -> p (u k)"),
                                         ACT.Copy).then_inc(kept, 1)

            @block.vector
            def _(dve):
                v = Chain(dve, own)

                def rectify(g):
                    ch, b = items[g]
                    n, width = (P, 512) if ch < 4 else (64, ST)
                    dve.wait_ge(scored, g + 1)
                    if g >= 2:
                        dve.wait_ge(summed, g - 1)
                    nc.vector.tensor_scalar(relu[0:n, g % 2, 0:width], ps_i[0:n, g % 2, 0:width], 0.0,
                                            iw_rows[0:n, b:b + 1], ALU.max, ALU.mult).then_inc(rectified, 1)

                def collect(ch):
                    dve.wait_ge(summed, (ch + 1) * DB)
                    if ch == 4:
                        v.done(nc.vector.tensor_tensor(score[:, PAST:KEYS], ps_s[:, 0, 0, 0:ST], later[:], ALU.add))
                        return
                    by_key = score[:, 0:PAST].rearrange("r (p v q) -> r q v p", v=TPR // 2, q=2)
                    for par in range(2):
                        last = nc.vector.tensor_copy(by_key[:, par, ch * 4:ch * 4 + 4, :],
                                                     ps_s[:, ch % 2, par, :].rearrange("r (v p) -> r v p", p=P))
                    last.then_inc(read, 1)

                for g in range(len(items)):
                    rectify(g)
                    if g >= DB and g % DB == 1:
                        collect(g // DB - 1)
                collect(4)
                dve.wait_ge(read, 4)

        loads = [divmod(q, 4) for q in range(sum(REST_LOADS), 4 * len(GROUPS))]
        steps = [(j, ch) for j in range(len(loads)) for ch in range(len(CHUNKS))]
        with m.round() as block:

            @block.gpsimd
            def _(pool):
                nc.gpsimd.iota(kpos[:], [[1, PAST]], base=-PAST, channel_multiplier=0).then_inc(positioned, 1)

            @block.sync
            def _(sp):
                def load(j):
                    g, n = loads[j]
                    sp.dma_start(w_rest[:, j % 2], win[:, :, GROUPS[g] + n * P:GROUPS[g] + (n + 1) * P]
                                 ).then_inc(w_loaded[j % 2], 16)

                load(0)
                load(1)
                for i, (j, ch) in enumerate(steps):
                    (g, n), (t0, width) = loads[j], CHUNKS[ch]
                    sp.wait_ge(rest_kept, i + 1)
                    sp.dma_start(rest_out[g][n][:, LEAD + t0:LEAD + t0 + width], rest[:, i % 4, 0:width]
                                 ).then_inc(rest_stored[i % 4], 16)
                    if ch == len(CHUNKS) - 1 and j + 2 < len(loads):
                        load(j + 2)
                for s in range(4):
                    sp.wait_ge(rest_stored[s], 16 * ((len(steps) + 3 - s) // 4))

            @block.tensor
            def _(pe):
                for i, (j, ch) in enumerate(steps):
                    if ch == 0:
                        pe.wait_ge(w_loaded[j % 2], 16 * (j // 2 + 1))
                    if i >= 2:
                        pe.wait_ge(rest_kept, i - 1)
                    for k in range(KC):
                        x = c.xnT[:, k, ch * 512:(ch + 1) * 512] if ch < NBAND else c.xsT[:, k, :]
                        last = nc.tensor.matmul(ps_i[:, i % 2, 0:CHUNKS[ch][1]], w_rest[:, j % 2, k, :], x,
                                                start=(k == 0), stop=(k == KC - 1))
                    last.then_inc(rest_done, 1)

            @block.scalar
            def _(act):
                for i, (j, ch) in enumerate(steps):
                    width = CHUNKS[ch][1]
                    act.wait_ge(rest_done, i + 1)
                    if i >= 4:
                        act.wait_ge(rest_stored[i % 4], 16 * (i // 4))
                    nc.scalar.activation(rest[:, i % 4, 0:width], ps_i[:, i % 2, 0:width], ACT.Copy
                                         ).then_inc(rest_kept, 1)

            @block.vector
            def _(dve):
                v = Chain(dve, own)
                for _ in range(TOPK // 8):
                    v.done(nc.vector.max(best[:], score[:]))
                    v.done(nc.vector.match_replace(score[:], best[:], score[:], TAKEN))
                v.done(nc.vector.tensor_scalar(bias[:], score[:], TAKEN, -BIG, ALU.not_equal, ALU.mult))
                dve.wait_ge(positioned, 1)
                v.done(nc.vector.tensor_copy(score[:, 0:PAST], kpos[:]))
                v.done(nc.vector.scalar_tensor_tensor(bias[:, 0:PAST], score[:, 0:PAST], low[0:ST, 0:1],
                                                      bias[:, 0:PAST], ALU.subtract, ALU.add))
                v.done(nc.vector.tensor_tensor(bias[:, PAST:KEYS], bias[:, PAST:KEYS], newpos[:], ALU.add))
                v.done(nc.vector.scalar_tensor_tensor(bias[:, PAST:KEYS], later[:], BIG / -MASKED,
                                                      bias[:, PAST:KEYS], ALU.mult, ALU.add))


def sample_attend(nc, c, a, o):
    rows, spread, q_bd, bias, attT = o.rows, o.spread, o.q_bd, o.bias, o.attT
    with ExitStack() as ctx:
        m = Stage(nc, ctx, "satt")
        R = NH * DT
        keys = m.sb("keys", [P, 2, TPR, P])
        values = m.sb("values", [P, 2, TPR, P])
        row_ids = m.sb("row_ids", [P, 2], I32)
        q_st = m.sb("q_st", [P, 2, R])
        spread_st = m.sb("spread_st", [ST, 2, R])
        keysT = m.sb("keysT", [P, 2, 512])
        prob = m.sb("prob", [R, 2, KEYS])
        probT = m.sb("probT", [P, 2, 8, R])
        att = m.sb("att", [R, 2, HD])
        chunk_max = m.sb("chunk_max", [R, 2, 16])
        negmax = m.sb("negmax", [R, 2])
        rowsum = m.sb("rowsum", [R, 2])
        ps_t = m.psum("ps_t", [P, 2, 4, P])
        ps_s = m.psum("ps_s", [R, 2, 512])
        ps_p = m.psum("ps_p", [P, 2, 8, R])
        ps_o = m.psum("ps_o", [R, P])
        ps_f = m.psum("ps_f", [HD, R])
        (indexed, staged, turned, kept, multiplied, moved, maxed, exped, p_turned, p_kept, weighted,
         normalised, att_turned, att_kept, stored, own) = [m.sem(n) for n in (
            "indexed", "staged", "turned", "kept", "multiplied", "moved", "maxed", "exped", "p_turned", "p_kept",
            "weighted", "normalised", "att_turned", "att_kept", "stored", "own")]
        k_in = [m.sem(f"k_in{u}") for u in range(2)]
        v_in = [m.sem(f"v_in{u}") for u in range(2)]
        NC = PAST // 512
        k_src = a["cache_k"].rearrange("l n (q t) h d -> (l n q) (t h d)", q=QT)
        v_src = a["cache_v"].rearrange("l n (q t) h d -> (l n q) (t h d)", q=QT)

        def pair(i):
            with m.round() as block:

                @block.gpsimd
                def _(pool):
                    pool.wait_ge(indexed, 1)
                    for dst, src, sems in ((keys, k_src, k_in), (values, v_src, v_in)):
                        for u in range(2):
                            pool.indirect_dma_start(dst[:, u].rearrange("p v d -> p (v d)"), None, src,
                                                    bass.IndirectOffsetOnAxis(ap=row_ids[:, u:u + 1], axis=0)
                                                    ).then_inc(sems[u], 16)
                    for sems in (k_in, v_in):
                        for u in range(2):
                            pool.wait_ge(sems[u], 16)
                    pool.dma_reset()

                @block.tensor
                def _(pe):
                    pe.wait_ge(staged, 2)

                    def turn(u, ch):
                        g = u * NC + ch
                        if ch == 0:
                            pe.wait_ge(k_in[u], 16)
                        if g >= 2:
                            pe.wait_ge(kept, g - 1)
                        for n in range(4):
                            last = nc.tensor.transpose(ps_t[:, g % 2, n, :], keys[:, u, ch * 4 + n, :], c.ident[:])
                        last.then_inc(turned, 1)

                    def scores(u, ch):
                        j = u * (NC + 1) + ch
                        if j >= 2:
                            pe.wait_ge(moved, j - 1)
                        if ch < NC:
                            pe.wait_ge(kept, u * NC + ch + 1)
                            width, kT = 512, keysT[:, (u * NC + ch) % 2, :]
                            kb = bias[:, 0:PAST].rearrange("r (p v) -> r v p", v=TPR)[:, ch * 4:ch * 4 + 4, :]
                        else:
                            width, kT, kb = ST, c.ksT[:], bias[:, PAST:KEYS]
                        nc.tensor.matmul(ps_s[:, j % 2, 0:width], q_st[:, u, :], kT, start=True, stop=False)
                        nc.tensor.matmul(ps_s[:, j % 2, 0:width], spread_st[:, u, :], kb,
                                         start=False, stop=True).then_inc(multiplied, 1)

                    def p_turn(u, q):
                        g = u * 5 + q
                        if g >= 2:
                            pe.wait_ge(p_kept, g - 1)
                        if q < 4:
                            for n in range(8):
                                v = q * 8 + n
                                last = nc.tensor.transpose(ps_p[:, g % 2, n, :], prob[:, u, v * P:(v + 1) * P],
                                                           c.ident[0:R, 0:R])
                        else:
                            last = nc.tensor.transpose(ps_p[0:ST, g % 2, 0, :], prob[:, u, PAST:KEYS], c.ident[0:R, 0:R])
                        last.then_inc(p_turned, 1)

                    def weigh(u, q):
                        g = u * 5 + q
                        pe.wait_ge(p_kept, g + 1)
                        if q == 0:
                            pe.wait_ge(v_in[u], 16)
                            if u:
                                pe.wait_ge(normalised, 1)
                        if q < 4:
                            for n in range(8):
                                v = q * 8 + n
                                last = nc.tensor.matmul(ps_o[:], probT[:, g % 2, n, :], values[:, u, v, :],
                                                        start=(v == 0), stop=False)
                        else:
                            last = nc.tensor.matmul(ps_o[:], probT[0:ST, g % 2, 0, :], c.vs[:], start=False, stop=True)
                        last.then_inc(weighted, 1)

                    for u in range(2):
                        turn(u, 0)
                        for ch in range(NC):
                            if ch + 1 < NC:
                                turn(u, ch + 1)
                            scores(u, ch)
                        scores(u, NC)
                    for u in range(2):
                        pe.wait_ge(exped, u + 1)
                        p_turn(u, 0)
                        for q in range(5):
                            if q < 4:
                                p_turn(u, q + 1)
                            weigh(u, q)
                        pe.wait_ge(normalised, u + 1)
                        if u:
                            pe.wait_ge(att_kept, 1)
                        nc.tensor.transpose(ps_f[:], att[:, u, :], c.ident[0:R, 0:R]).then_inc(att_turned, 1)

                @block.scalar
                def _(act):
                    nc.scalar.activation(q_st[:], q_bd[:, bass.ds(i * 2, 2), :], ACT.Copy).then_inc(staged, 1)
                    nc.scalar.activation(spread_st[:], spread[:, bass.ds(i * 2, 2), :], ACT.Copy).then_inc(staged, 1)

                    def exp(u):
                        act.wait_ge(maxed, u + 1)
                        nc.scalar.activation(prob[:, u, :], prob[:, u, :], ACT.Exp, bias=negmax[:, u:u + 1],
                                             accum_out=rowsum[:, u:u + 1]).then_inc(exped, 1)

                    for u in range(2):
                        for ch in range(NC):
                            g = u * NC + ch
                            act.wait_ge(turned, g + 1)
                            if g >= 2:
                                act.wait_ge(multiplied, (g - 2) // NC * (NC + 1) + (g - 2) % NC + 1)
                            nc.scalar.activation(keysT[:, g % 2, :], ps_t[:, g % 2].rearrange("p u k -> p (u k)"),
                                                 ACT.Copy).then_inc(kept, 1)
                    exp(0)
                    exp(1)
                    for u in range(2):
                        for q in range(5):
                            g = u * 5 + q
                            act.wait_ge(p_turned, g + 1)
                            if g >= 2:
                                act.wait_ge(weighted, g - 1)
                            if q < 4:
                                nc.scalar.activation(probT[:, g % 2], ps_p[:, g % 2], ACT.Copy).then_inc(p_kept, 1)
                            else:
                                nc.scalar.activation(probT[0:ST, g % 2, 0, :], ps_p[0:ST, g % 2, 0, :],
                                                     ACT.Copy).then_inc(p_kept, 1)
                        act.wait_ge(att_turned, u + 1)
                        dst = attT[:].rearrange("d h (b t) -> d h b t", t=DT)[:, :, bass.ds(i * 2 + u, 1), :]
                        nc.scalar.activation(dst, ps_f[:].rearrange("d (h t) -> d h t", t=DT).unsqueeze(2),
                                             ACT.Copy).then_inc(att_kept, 1)
                    act.wait_ge(att_kept, 2)

                @block.vector
                def _(dve):
                    v = Chain(dve, own)
                    nc.vector.tensor_copy(row_ids[:], rows[:, bass.ds(i * 2, 2)]).then_inc(indexed, 1)
                    for u in range(2):
                        for ch in range(NC + 1):
                            j = u * (NC + 1) + ch
                            width = 512 if ch < NC else ST
                            dve.wait_ge(multiplied, j + 1)
                            nc.vector.tensor_scalar(prob[:, u, ch * 512:ch * 512 + width], ps_s[:, j % 2, 0:width], 1.0,
                                                    None, ALU.mult, ALU.max,
                                                    accum_out=chunk_max[:, u, ch:ch + 1]).then_inc(moved, 1)
                        dve.wait_ge(moved, (u + 1) * (NC + 1))
                        v.done(nc.vector.reduce_max(negmax[:, u:u + 1], chunk_max[:, u, 0:NC + 1], AX_X))
                        nc.vector.tensor_scalar(negmax[:, u:u + 1], negmax[:, u:u + 1], -1.0, None,
                                                ALU.mult).then_inc(maxed, 1)
                    for u in range(2):
                        dve.wait_ge(exped, u + 1)
                        v.done(nc.vector.reciprocal(rowsum[:, u:u + 1], rowsum[:, u:u + 1]))
                        dve.wait_ge(weighted, 5 * (u + 1))
                        for kv in range(NKV):
                            r = slice(kv * 32, kv * 32 + 32)
                            last = nc.vector.tensor_scalar(att[r, u, :], ps_o[r, kv * HD:(kv + 1) * HD],
                                                           rowsum[r, u:u + 1], None, ALU.mult)
                        last.then_inc(normalised, 1)

        with nc.Fori(0, DB // 2) as i:
            pair(i)
        with m.round() as block:
            @block.sync
            def _(sp):
                sp.dma_start(a["attn_t"].rearrange("(h d) t -> d h t", d=HD)[:, :, S:S + ST], attT[:]).then_inc(stored, 16)
                sp.wait_ge(stored, 16)


def stage_merge(nc, a):
    with ExitStack() as ctx:
        m = Stage(nc, ctx, "merge")
        up_c = m.sb("up_c", [P, 4, D])
        up_a = m.sb("up_a", [P, 4, D])
        w_out = m.sb("w_out", [P, KC, D])
        gain = m.sb("gain", [P, D])
        convw = m.sb("convw", [P, 3, 4])
        pc = m.sb("pc", [P, 4, LEAD + BAND])
        pu = m.sb("pu", [P, 4, LEAD + BAND])
        p_new = m.sb("p_new", [P, 4, DB, 2 + DT])
        pb = m.sb("pb", [P, 4, BAND])
        conv = m.sb("conv", [P, 4, BAND])
        silu = m.sb("silu", [P, 4, BAND])
        attn = m.sb("attn", [P, 4, BAND])
        gates = m.sb("gates", [P, 16, BAND])
        merged = m.sb("merged", [P, KC, BAND])
        part = m.sb("part", [P, BAND])
        x = m.sb("x", [P, TPB, D])
        y = m.sb("y", [P, 2, D])
        junk = m.sb("junk", [P, D])
        st = m.sb("st", [P, 2, 8])
        ps_u = m.psum("ps_u", [P, 4, 512])
        ps_y = m.psum("ps_y", [P, 2, D])
        (weights, next_in, az_acted, z_acted, ga_acted, gc_acted, gated, convolved, outs, x_in, upped, taken,
         merged_n, out_done, added, squared, meaned, rooted, finished, own, own_act) = [m.sem(n) for n in (
            "weights", "next_in", "az_acted", "z_acted", "ga_acted", "gc_acted", "gated", "convolved", "outs", "x_in",
            "upped", "taken", "merged_n", "out_done", "added", "squared", "meaned", "rooted", "finished", "own", "own_act")]
        stored = [m.sem(f"stored{s}") for s in range(2)]
        both = gates[:].rearrange("p (h n) t -> p h n t", h=2)

        def rows_of(t):
            return t.rearrange("(n p) t -> p n t", p=P)

        class Loads:

            def __init__(self, sp, t0, width):
                self.sp, self.t0, self.width = sp, t0, width
                self.lead = 0 if width == ST else LEAD
                self.n = 0

            def rest(self, dst, group, lead=0, n=4):
                width = self.width
                self.sp.dma_start(dst[:, :, 0:lead + width], rows_of(a["rest_t"])[
                    :, 4 * group:4 * group + n, bass.ds(self.t0 + LEAD - lead, lead + width)]).then_inc(next_in, 16)
                self.n += 16

            def attention_gate(self):
                self.rest(silu, R_AZ)

            def attention(self):
                self.sp.dma_start(attn[:, :, 0:self.width], rows_of(a["attn_t"])[:, :, bass.ds(self.t0, self.width)]
                                  ).then_inc(next_in, 16)
                self.n += 16

            def conv_inputs(self):
                self.rest(pc, R_C, self.lead)
                self.rest(pu, R_U, self.lead)
                self.rest(pb, R_B)

            def conv_gate(self):
                self.rest(conv, R_Z)

            def merge_gates(self, half):
                self.rest(both[:, half], (R_GC, R_GA)[half], n=KC)

        with m.round() as block:
            @block.sync
            def _(sp):
                sp.dma_start(up_c[:], a["w_up_conv"].rearrange("l (k p) n -> (l p) k n", p=P)).then_inc(weights, 16)
                sp.dma_start(up_a[:], a["w_up_attn"].rearrange("l (k p) n -> (l p) k n", p=P)).then_inc(weights, 16)
                sp.dma_start(w_out[:], a["w_out"].rearrange("l (k p) n -> (l p) k n", p=P)).then_inc(weights, 16)
                sp.dma_start(gain[:], a["final_gain"].rearrange("(a d) -> a d", a=1).to_broadcast([P, D])).then_inc(weights, 16)
                for j in range(3):
                    sp.dma_start(convw[:, j, :], a["conv_w"][0, j, :].rearrange("(g p) -> p g", p=P),
                                 allow_slow_non_contiguous=True).then_inc(weights, 16)
                for b in range(DB):
                    for j in range(2):
                        sp.dma_start(p_new[:, :, b, j], a["state_conv"][0, b, j, :].rearrange("(g p) -> p g", p=P),
                                     allow_slow_non_contiguous=True).then_inc(weights, 16)
                first = Loads(sp, 0, BAND)
                first.attention_gate()
                first.attention()
                first.merge_gates(1)
                first.conv_inputs()
                first.conv_gate()
                first.merge_gates(0)
                sp.wait_ge(next_in, first.n)
                sp.wait_ge(weights, 16 * (7 + 2 * DB))

        def band(width, x_src, y_dst, following, sample=False, last=False):
            rows = min(width, P)
            nt = width // rows
            with m.round() as block:

                @block.sync
                def _(sp):
                    sp.dma_start(x[0:rows, 0:nt, :], x_src).then_inc(x_in, 16)
                    if sample or last:
                        sp.wait_ge(convolved, 1)
                    if sample:
                        for b in range(DB):
                            for j in range(2):
                                sp.dma_start(a["new_conv_sample"][0, b, j, :].rearrange("(g p) -> p g", p=P),
                                             p_new[:, :, b, DT + j], allow_slow_non_contiguous=True).then_inc(outs, 16)
                        sp.wait_ge(outs, 32 * DB)
                    if last:
                        for j in range(2):
                            sp.dma_start(a["new_conv_prompt"][0, 0, j, :].rearrange("(g p) -> p g", p=P),
                                         pc[:, :, BAND + j], allow_slow_non_contiguous=True).then_inc(outs, 16)
                        sp.wait_ge(outs, 32)
                    if following:
                        nxt = Loads(sp, *following)
                        sp.wait_ge(gated, 1)
                        nxt.attention_gate()
                        sp.wait_ge(upped, KC)
                        nxt.attention()
                        sp.wait_ge(taken, KC)
                        nxt.merge_gates(1)
                        sp.wait_ge(convolved, 1)
                        nxt.conv_inputs()
                        sp.wait_ge(upped, 2 * KC)
                        nxt.conv_gate()
                        sp.wait_ge(taken, 2 * KC)
                        nxt.merge_gates(0)
                    for t in range(nt):
                        sp.wait_ge(finished, t + 1)
                        sp.dma_start(y_dst(t), y[0:rows, t % 2, :]).then_inc(stored[t % 2], 16)
                    for s in range(min(nt, 2)):
                        sp.wait_ge(stored[s], 16 * ((nt + 1 - s) // 2))
                    if following:
                        sp.wait_ge(next_in, nxt.n)

                @block.tensor
                def _(pe):
                    for g in range(2 * KC):
                        if g == 0:
                            pe.wait_ge(gated, 1)
                        if g == KC:
                            pe.wait_ge(convolved, 1)
                        if g >= 4:
                            pe.wait_ge(taken, g - 3)
                        up, branch = (up_a, attn) if g < KC else (up_c, conv)
                        n = g % KC
                        for k in range(4):
                            last_k = nc.tensor.matmul(ps_u[:, g % 4, 0:width], up[:, k, n * P:(n + 1) * P],
                                                      branch[:, k, 0:width], start=(k == 0), stop=(k == 3))
                        last_k.then_inc(upped, 1)
                    for t in range(nt):
                        if t >= 2:
                            pe.wait_ge(added, t - 1)
                        for half in range(2):
                            for k in range(KC):
                                if t == 0 and half == 0:
                                    pe.wait_ge(merged_n, k + 1)
                                last_k = nc.tensor.matmul(ps_y[0:rows, t % 2, half * 512:(half + 1) * 512],
                                                          merged[:, k, t * rows:(t + 1) * rows],
                                                          w_out[:, k, half * 512:(half + 1) * 512],
                                                          start=(k == 0), stop=(k == KC - 1))
                        last_k.then_inc(out_done, 1)

                @block.vector
                def _(dve):
                    v = Chain(dve, own)

                    def by_sample(x):
                        return x.rearrange("p (b t) -> p b t", t=DT)

                    y_conv = pu[:, :, 0:width]

                    def tap(j):
                        for g in range(4):
                            if sample:
                                out, x_tap = by_sample(y_conv[:, g, :]), p_new[:, g, :, j:j + DT]
                            else:
                                out, x_tap = y_conv[:, g, :], pc[:, g, j:j + width]
                            if j == 0:
                                v.done(nc.vector.tensor_scalar(out, x_tap, convw[:, j, g:g + 1], None, ALU.mult))
                            else:
                                v.done(nc.vector.scalar_tensor_tensor(out, x_tap, convw[:, j, g:g + 1], out,
                                                                      ALU.mult, ALU.add))

                    dve.wait_ge(az_acted, 1)
                    nc.vector.tensor_tensor(attn[:, :, 0:width], attn[:, :, 0:width], silu[:, :, 0:width],
                                            ALU.mult).then_inc(gated, 1)
                    for n in range(KC):
                        if n == 0 and sample:
                            for g in range(4):
                                v.done(nc.vector.tensor_tensor(p_new[:, g, :, 2:2 + DT], by_sample(pc[:, g, 0:width]),
                                                               by_sample(pu[:, g, 0:width]), ALU.mult))
                        elif n == 0:
                            v.done(nc.vector.tensor_tensor(pc[:], pc[:], pu[:], ALU.mult))
                        elif n < 4:
                            tap(n - 1)
                        elif n == 4:
                            v.done(nc.vector.tensor_tensor(y_conv, pb[:, :, 0:width], y_conv, ALU.mult))
                        elif n == 5:
                            dve.wait_ge(z_acted, 1)
                            nc.vector.tensor_tensor(conv[:, :, 0:width], conv[:, :, 0:width], y_conv,
                                                    ALU.mult).then_inc(convolved, 1)
                        dve.wait_ge(upped, n + 1)
                        dve.wait_ge(ga_acted, n // 2 + 1)
                        nc.vector.tensor_tensor(merged[:, n, 0:width], ps_u[:, n % 4, 0:width],
                                                gates[:, KC + n, 0:width], ALU.mult).then_inc(taken, 1)
                    for n in range(KC):
                        dve.wait_ge(upped, KC + n + 1)
                        dve.wait_ge(gc_acted, n // 2 + 1)
                        if n:
                            dve.wait_ge(merged_n, n)
                        nc.vector.tensor_tensor(part[:, 0:width], ps_u[:, n % 4, 0:width],
                                                gates[:, n, 0:width], ALU.mult).then_inc(taken, 1)
                        dve.wait_ge(taken, KC + n + 1)
                        nc.vector.tensor_tensor(merged[:, n, 0:width], merged[:, n, 0:width], part[:, 0:width],
                                                ALU.add).then_inc(merged_n, 1)
                    dve.wait_ge(x_in, 16)

                    def add(t):
                        s = t % 2
                        dve.wait_ge(out_done, t + 1)
                        if t >= 2:
                            dve.wait_ge(stored[s], 16 * (t // 2))
                        nc.vector.tensor_tensor(y[0:rows, s, :], ps_y[0:rows, s, :], x[0:rows, t, :], ALU.add).then_inc(added, 1)

                    def finish(t):
                        s = t % 2
                        dve.wait_ge(squared, t + 1)
                        v.done(nc.vector.tensor_scalar(st[0:rows, s, 1:2], st[0:rows, s, 5:6], 1.0 / D, EPS,
                                                       ALU.mult, ALU.add))
                        nc.vector.tensor_copy(st[0:rows, s, 6:7], st[0:rows, s, 1:2]).then_inc(meaned, 1)
                        dve.wait_ge(rooted, t + 1)
                        refined_rstd(nc, v, st[0:rows, s, 1:2], st[0:rows, s, 4:5], st[0:rows, s, 3:4],
                                     st[0:rows, s, 2:3])
                        nc.vector.scalar_tensor_tensor(y[0:rows, s, :], y[0:rows, s, :], st[0:rows, s, 3:4],
                                                       gain[0:rows, :], ALU.mult, ALU.mult).then_inc(finished, 1)

                    for t in range(nt):
                        add(t)
                        finish(t)

                @block.scalar
                def _(act):
                    o = Chain(act, own_act)
                    nc.scalar.activation(silu[:, :, 0:width], silu[:, :, 0:width], ACT.Silu).then_inc(az_acted, 1)
                    nc.scalar.activation(conv[:, :, 0:width], conv[:, :, 0:width], ACT.Silu).then_inc(z_acted, 1)
                    for half, acted in ((1, ga_acted), (0, gc_acted)):
                        for q in range(4):
                            gate = both[:, half, 2 * q:2 * q + 2, 0:width]
                            nc.scalar.activation(gate, gate, ACT.Sigmoid).then_inc(acted, 1)
                    for t in range(nt):
                        s = t % 2
                        act.wait_ge(added, t + 1)
                        o.done(nc.scalar.activation(junk[0:rows, :], y[0:rows, s, :], ACT.Square,
                                                    accum_out=st[0:rows, s, 0:1]))
                        nc.scalar.activation(st[0:rows, s, 5:6], st[0:rows, s, 0:1], ACT.Copy).then_inc(squared, 1)
                        act.wait_ge(meaned, t + 1)
                        nc.scalar.activation(st[0:rows, s, 2:3], st[0:rows, s, 1:2], ACT.Sqrt).then_inc(rooted, 1)

        xb = a["x_prompt"].rearrange("b (i t p) d -> (b i) p t d", p=P, t=TPB)
        yb = a["y_prompt"].rearrange("b (t p) d -> (b t) p d", p=P)
        with nc.Fori(0, NBAND - 1) as i:
            band(BAND, xb[i], lambda t: yb[i * TPB + t], ((i + 1) * BAND, BAND))
        band(BAND, xb[NBAND - 1], lambda t: yb[(NBAND - 1) * TPB + t], (S, ST), last=True)
        band(ST, a["x_sample"].rearrange("b t d -> (b t) d").unsqueeze(1),
             lambda t: a["y_sample"].rearrange("b t d -> (b t) d"), None, sample=True)


def hybrid_kernel(nc, a):
    with ExitStack() as ctx:
        def sb(name, shape):
            return ctx.enter_context(nc.sbuf_tensor(name, shape, F32))

        c = Named()
        c.ident = sb("ident", [P, P])
        c.xnT = sb("xnT", [P, KC, S])
        c.xsT = sb("xsT", [P, KC, ST])
        c.qs = sb("qs", [P, 2, 4, ST])
        c.ksT = sb("ksT", [P, ST])
        c.iksT = sb("iksT", [P, ST])
        c.vs = sb("vs", [ST, P])
        c.iws = sb("iws", [ST, NI])
        with ExitStack() as prompt:
            def of_prompt(name, shape):
                return prompt.enter_context(nc.sbuf_tensor(name, shape, F32))

            c.keypos = of_prompt("keypos", [P, S])
            c.kT = of_prompt("kT", [P, S])
            c.ikT = of_prompt("ikT", [P, S])
            c.v = of_prompt("v", [P, NT * P])
            c.iw = of_prompt("iw", [P, NT * NI])
            stage_constants(nc, c)
            stage_norm(nc, c, a)
            stage_prompt_attention(nc, c, a)
        stage_sample_attention(nc, c, a)
    stage_merge(nc, a)


INPUTS = ["x_prompt", "x_sample", "cache_k", "cache_v", "cache_kidx", "state_conv", "page_table",
          "norm_gain", "w_in", "conv_w", "w_up_conv", "w_up_attn", "w_out", "final_gain"]
OUTPUTS = {
    "y_prompt": (1, S, D), "y_sample": (DB, DT, D),
    "new_k_prompt": (1, 1, S, NKV, HD), "new_v_prompt": (1, 1, S, NKV, HD),
    "new_kidx_prompt": (1, 1, S, ID), "new_conv_prompt": (1, 1, 2, DC),
    "new_k_sample": (1, DB, DT, NKV, HD), "new_v_sample": (1, DB, DT, NKV, HD),
    "new_kidx_sample": (1, DB, DT, ID), "new_conv_sample": (1, DB, 2, DC),
}


def kernel(**inputs):
    import numpy as np
    import concourse.bacc as bacc
    from concourse.bass_utils import run_bass_kernel_spmd

    nc = bacc.Bacc("TRN2", target_bir_lowering=False, num_devices=1)
    dram, arrays = {}, {}
    for name in INPUTS:
        x = np.ascontiguousarray(inputs[name])
        arrays[f"in_{name}"] = x
        dram[name] = nc.dram_tensor(f"in_{name}", x.shape, mybir.dt.from_np(x.dtype), kind="ExternalInput").ap()
    for name, shape in OUTPUTS.items():
        dram[name] = nc.dram_tensor(f"out_{name}", shape, F32, kind="ExternalOutput").ap()
    dram["attn_t"] = nc.dram_tensor("attn_t", (NH * HD, S + ST), F32).ap()
    dram["rest_t"] = nc.dram_tensor("rest_t", (len(GROUPS) * 512, LEAD + S + ST), F32).ap()
    dram["iw_scratch"] = nc.dram_tensor("iw_scratch", (DB, NI, DT), F32).ap()
    hybrid_kernel(nc, dram)
    r = run_bass_kernel_spmd(nc, [arrays], core_ids=[0])
    return tuple(r.results[0][f"out_{name}"] for name in OUTPUTS)
```
